# Optimizing a Trainium2 kernel written in Bass

```python
import jax, jax.numpy as jnp
from jax import lax
import numpy as np

D_MODEL = 2048
BATCH = 1
SEQ = 512
DEPTH = 2
DEC_BATCH = 8
DEC_SEQ = 4
PAST_LEN = 2048
PAGE_SIZE = 128

D_MIX = D_MODEL
HEAD_DIM = 64
D_ATT = D_MIX // 2
N_HEADS = D_ATT // HEAD_DIM
N_KV_HEADS = 4
GROUP = N_HEADS // N_KV_HEADS
D_KV = N_KV_HEADS * HEAD_DIM
WINDOW = 128
ROPE_THETA = 10000.0
D_POOL = D_MIX // 4
POOL_WINDOWS = (2, 4, 8, 16)
N_POOL_GROUPS = len(POOL_WINDOWS)
POOL_GROUP_DIM = D_POOL // N_POOL_GROUPS
POOL_HIST = max(POOL_WINDOWS) - 1
D_SGU = D_MIX - D_ATT - D_POOL
CHUNK = 128
N_SGU_HEADS = 4
SGU_HEAD_DIM = D_SGU // N_SGU_HEADS
SPLIT_SIZES = (D_ATT, D_KV, D_KV, D_ATT, D_POOL, D_POOL, D_SGU, D_SGU, D_SGU)
D_IN = sum(SPLIT_SIZES)
EPS = 1e-6

kernel_name = "hymba_swa_pool_sgu_step"

def _rmsnorm(x, g):
    xf = x.astype(jnp.float32)
    xf = xf * lax.rsqrt(jnp.mean(xf * xf, axis=-1, keepdims=True) + EPS)
    return (xf * g.astype(jnp.float32)).astype(x.dtype)

def _layernorm(x, g, b):
    xf = x.astype(jnp.float32)
    mu = jnp.mean(xf, axis=-1, keepdims=True)
    var = jnp.mean(jnp.square(xf - mu), axis=-1, keepdims=True)
    y = (xf - mu) * lax.rsqrt(var + EPS) * g.astype(jnp.float32) + b.astype(jnp.float32)
    return y.astype(x.dtype)

def _rope(x, pos):
    half = HEAD_DIM // 2
    inv = ROPE_THETA ** (-jnp.arange(0, HEAD_DIM, 2, dtype=jnp.float32) / HEAD_DIM)
    ang = pos.astype(jnp.float32)[:, None] * inv[None, :]
    cos = jnp.cos(ang)[:, None, :]
    sin = jnp.sin(ang)[:, None, :]
    xf = x.astype(jnp.float32)
    x1, x2 = xf[..., :half], xf[..., half:]
    return jnp.concatenate([x1 * cos - x2 * sin, x2 * cos + x1 * sin], axis=-1).astype(x.dtype)

def _project(x, pre_g, w_in, pos):
    h = _rmsnorm(x, pre_g)
    z = h @ w_in
    offs = np.cumsum(SPLIT_SIZES)[:-1].tolist()
    q, k, v, g_att, xb, g_pool, u, vs, g_sgu = jnp.split(z, offs, axis=-1)
    B, S = x.shape[:2]
    q = _rope(q.reshape(B, S, N_HEADS, HEAD_DIM), pos)
    k = _rope(k.reshape(B, S, N_KV_HEADS, HEAD_DIM), pos)
    v = v.reshape(B, S, N_KV_HEADS, HEAD_DIM)
    return q, k, v, g_att, xb, g_pool, u, vs, g_sgu

def _sink_attend(q, k, v, mask, sinks):
    s = jnp.einsum('...qkgd,...skd->...kgqs', q, k,
                   preferred_element_type=jnp.float32) * (HEAD_DIM ** -0.5)
    s = jnp.where(mask, s, -jnp.inf)
    sink = sinks.astype(jnp.float32).reshape(N_KV_HEADS, GROUP, 1, 1)
    m = jnp.maximum(jnp.max(s, axis=-1, keepdims=True), sink)
    p = jnp.exp(s - m)
    p = p / (jnp.sum(p, axis=-1, keepdims=True) + jnp.exp(sink - m))
    return jnp.einsum('...kgqs,...skd->...qkgd', p.astype(v.dtype), v)

def _window_attn_prompt(q, k, v, sinks):
    B, S = q.shape[:2]
    nb = S // WINDOW
    qb = q.reshape(B, nb, WINDOW, N_KV_HEADS, GROUP, HEAD_DIM)
    kb = k.reshape(B, nb, WINDOW, N_KV_HEADS, HEAD_DIM)
    vb = v.reshape(B, nb, WINDOW, N_KV_HEADS, HEAD_DIM)
    pad = ((0, 0), (1, 0), (0, 0), (0, 0), (0, 0))
    kk = jnp.concatenate([jnp.pad(kb[:, :-1], pad), kb], axis=2)
    vv = jnp.concatenate([jnp.pad(vb[:, :-1], pad), vb], axis=2)
    i = jnp.arange(WINDOW)[:, None]
    j = jnp.arange(2 * WINDOW)[None, :]
    diff = i + WINDOW - j
    band = (diff >= 0) & (diff < WINDOW)
    mask = band[None] & ((jnp.arange(nb)[:, None, None] > 0) | (j[None] >= WINDOW))
    out = _sink_attend(qb, kk, vv, mask[:, None, None], sinks)
    return out.reshape(B, S, D_ATT)

def _window_attn_sample(q, k_new, v_new, k_hist, v_hist, sinks):
    Bd, T = q.shape[:2]
    Lb = k_hist.shape[1]
    k_all = jnp.concatenate([k_hist, k_new], axis=1)
    v_all = jnp.concatenate([v_hist, v_new], axis=1)
    qpos = PAST_LEN + jnp.arange(T)
    kpos = PAST_LEN - Lb + jnp.arange(Lb + T)
    d = qpos[:, None] - kpos[None, :]
    mask = (d >= 0) & (d < WINDOW)
    out = _sink_attend(q.reshape(Bd, T, N_KV_HEADS, GROUP, HEAD_DIM), k_all, v_all, mask, sinks)
    return out.reshape(Bd, T, D_ATT), k_all[:, T:], v_all[:, T:]

def _pool_mix(xb_ext, start, pool_w, pool_scale):
    B = xb_ext.shape[0]
    n = xb_ext.shape[1] - POOL_HIST
    xf = xb_ext.astype(jnp.float32)
    cs = jnp.pad(jnp.cumsum(xf, axis=1), ((0, 0), (1, 0), (0, 0)))
    hi = cs[:, POOL_HIST + 1:]
    pos = start + jnp.arange(n)
    outs = []
    for g, w in enumerate(POOL_WINDOWS):
        sl = slice(g * POOL_GROUP_DIM, (g + 1) * POOL_GROUP_DIM)
        lo = cs[:, POOL_HIST + 1 - w:POOL_HIST + 1 - w + n, sl]
        cnt = jnp.minimum(w, pos + 1).astype(jnp.float32)[:, None]
        outs.append((hi[..., sl] - lo) / cnt - xf[:, POOL_HIST:, sl])
    pooled = jnp.stack(outs, axis=2).astype(pool_w.dtype)
    mixed = jnp.einsum('bngc,gcd->bngd', pooled, pool_w)
    return mixed.reshape(B, n, D_POOL) * pool_scale

def _sgu(u, v, ln_g, ln_b, w_s, b_s, L):
    B, S = u.shape[:2]
    vn = _layernorm(v, ln_g, ln_b)
    vc = vn.reshape(B, S // L, L, N_SGU_HEADS, SGU_HEAD_DIM)
    tri = jnp.tril(jnp.ones((L, L), dtype=bool))
    wm = jnp.where(tri, w_s[:, :L, :L], 0)
    mixed = jnp.einsum('hts,bnshd->bnthd', wm, vc) + b_s[:, :L].T[:, :, None]
    out = u.reshape(B, S // L, L, N_SGU_HEADS, SGU_HEAD_DIM) * mixed
    return out.reshape(B, S, D_SGU), vn

def _finish(x, o_att, g_att, o_pool, g_pool, o_sgu, g_sgu, w_out, post_g):
    y = jnp.concatenate([o_att * jax.nn.silu(g_att),
                         o_pool * jax.nn.silu(g_pool),
                         o_sgu * jax.nn.silu(g_sgu)], axis=-1) @ w_out
    return x + _rmsnorm(y, post_g)

def setup_inputs(seed: int = 0) -> dict:
    key = jax.random.key(seed)
    ks = jax.random.split(key, 16)
    nrm = jax.random.normal
    win = min(WINDOW, PAST_LEN)
    return {
        "x_prompt": nrm(ks[0], (BATCH, SEQ, D_MODEL), jnp.float32),
        "x_sample": nrm(ks[1], (DEC_BATCH, DEC_SEQ, D_MODEL), jnp.float32),
        "cache_k": nrm(ks[2], (DEPTH, DEC_BATCH, win, N_KV_HEADS, HEAD_DIM), jnp.float32),
        "cache_v": nrm(ks[3], (DEPTH, DEC_BATCH, win, N_KV_HEADS, HEAD_DIM), jnp.float32),
        "state_pool": nrm(ks[4], (DEPTH, DEC_BATCH, POOL_HIST, D_POOL), jnp.float32),
        "w_in": nrm(ks[5], (DEPTH, D_MODEL, D_IN), jnp.float32) * D_MODEL ** -0.5,
        "w_out": nrm(ks[6], (DEPTH, D_MIX, D_MODEL), jnp.float32) * D_MIX ** -0.5,
        "norm_pre": 1.0 + 0.1 * nrm(ks[7], (DEPTH, D_MODEL), jnp.float32),
        "norm_post": 1.0 + 0.1 * nrm(ks[8], (DEPTH, D_MODEL), jnp.float32),
        "attn_sinks": 0.5 * nrm(ks[9], (DEPTH, N_HEADS), jnp.float32),
        "pool_w": nrm(ks[10], (DEPTH, N_POOL_GROUPS, POOL_GROUP_DIM, POOL_GROUP_DIM), jnp.float32) * POOL_GROUP_DIM ** -0.5,
        "pool_scale": 1.0 + 0.1 * nrm(ks[11], (DEPTH, D_POOL), jnp.float32),
        "sgu_ln_g": 1.0 + 0.1 * nrm(ks[12], (DEPTH, D_SGU), jnp.float32),
        "sgu_ln_b": 0.02 * nrm(ks[13], (DEPTH, D_SGU), jnp.float32),
        "sgu_w": nrm(ks[14], (DEPTH, N_SGU_HEADS, CHUNK, CHUNK), jnp.float32) * CHUNK ** -0.5,
        "sgu_b": 1.0 + 0.1 * nrm(ks[15], (DEPTH, N_SGU_HEADS, CHUNK), jnp.float32),
    }

def reference(x_prompt, x_sample, cache_k, cache_v, state_pool, w_in, w_out, norm_pre,
              norm_post, attn_sinks, pool_w, pool_scale, sgu_ln_g, sgu_ln_b, sgu_w, sgu_b):
    pos_p = jnp.arange(SEQ)
    pos_s = PAST_LEN + jnp.arange(DEC_SEQ)
    xp, xs = x_prompt, x_sample
    nk_p, nv_p, npool_p = [], [], []
    nk_s, nv_s, npool_s, nchunk_s = [], [], [], []
    for l in range(DEPTH):
        q, k, v, g_att, xb, g_pool, u, vs, g_sgu = _project(xp, norm_pre[l], w_in[l], pos_p)
        o_att = _window_attn_prompt(q, k, v, attn_sinks[l])
        xb_ext = jnp.pad(xb, ((0, 0), (POOL_HIST, 0), (0, 0)))
        o_pool = _pool_mix(xb_ext, 0, pool_w[l], pool_scale[l])
        o_sgu, _ = _sgu(u, vs, sgu_ln_g[l], sgu_ln_b[l], sgu_w[l], sgu_b[l], CHUNK)
        xp_next = _finish(xp, o_att, g_att, o_pool, g_pool, o_sgu, g_sgu, w_out[l], norm_post[l])
        nk_p.append(k[:, -WINDOW:])
        nv_p.append(v[:, -WINDOW:])
        npool_p.append(xb[:, -POOL_HIST:])
        xp = xp_next

        q, k, v, g_att, xb, g_pool, u, vs, g_sgu = _project(xs, norm_pre[l], w_in[l], pos_s)
        o_att, k_buf, v_buf = _window_attn_sample(q, k, v, cache_k[l], cache_v[l], attn_sinks[l])
        xb_ext = jnp.concatenate([state_pool[l].astype(xb.dtype), xb], axis=1)
        o_pool = _pool_mix(xb_ext, PAST_LEN, pool_w[l], pool_scale[l])
        o_sgu, vn = _sgu(u, vs, sgu_ln_g[l], sgu_ln_b[l], sgu_w[l], sgu_b[l], DEC_SEQ)
        xs = _finish(xs, o_att, g_att, o_pool, g_pool, o_sgu, g_sgu, w_out[l], norm_post[l])
        nk_s.append(k_buf)
        nv_s.append(v_buf)
        npool_s.append(xb_ext[:, -POOL_HIST:])
        nchunk_s.append(vn)

    return (xp, xs,
            jnp.stack(nk_p), jnp.stack(nv_p), jnp.stack(npool_p),
            jnp.stack(nk_s), jnp.stack(nv_s), jnp.stack(npool_s), jnp.stack(nchunk_s))


_drawn_inputs = setup_inputs


def setup_inputs(seed=0):
    import zlib

    import numpy as np

    out = dict(_drawn_inputs(seed))
    spreads = {}
    factors = {'attn_sinks': 6.083, 'sgu_ln_b': 2.77}
    for name, (base, spread) in spreads.items():
        noise = np.random.default_rng([zlib.crc32(name.encode()), seed]).standard_normal(out[name].shape)
        drawn = base * np.exp(spread * noise) if base else spread * noise
        out[name] = __import__('jax').numpy.asarray(drawn.astype(out[name].dtype))
    for name, factor in factors.items():
        out[name] = (out[name] * factor).astype(out[name].dtype)
    return out
```

```python
from contextlib import ExitStack, contextmanager

import numpy as np

import concourse.bass as bass
from concourse import mybir

F32 = mybir.dt.float32
F32R = mybir.dt.float32r
ALU = mybir.AluOpType
ACT = mybir.ActivationFunctionType
AX_X = mybir.AxisListType.X

P = 128
D = 2048
KT = D // P
DEPTH = 2
SEQ = 512
NBLK = SEQ // P
DB, DT = 8, 4
NS = DB * DT
NTOK = SEQ + NS
HALF = NTOK // 2
HD = 64
NH, NKV, GROUP = 16, 4, 4
SCALE = HD ** -0.5
POOLW = (2, 4, 8, 16)
HIST = 15
SEXT = HIST + DT
EXT = HIST + SEQ + DB * SEXT
PAST = 2048
EPS = 1e-6
NEG = -1.0e30

DIN = 5120
N_IN, N_OUT = DIN // P, D // P
NB = N_IN + N_OUT
KV0, Q0, XB0, VS0, U0, GB0, GC0, GA0, OUT0 = 0, 4, 12, 16, 20, 24, 28, 32, 40
COL = {KV0: 1024, Q0: 0, XB0: 2560, VS0: 4096, U0: 3584, GB0: 3072, GC0: 4608, GA0: 1536}
HK = KT // 2
OUT_ORDER = list(range(8, 16)) + list(range(0, 8))

SKEYS = ["xsum", "kvtail", "kc1", "state", "ssc"]
TKEYS = ["v", "kc0", "wm"]
for _u in range(16):
    SKEYS.append(("sc", _u))
    if _u:
        TKEYS.append(("pv", _u - 1))
    TKEYS += {1: ["spt"], 2: ["spv"], 3: [("pm", 0)], 4: [("pm", 1)], 5: [("pm", 2)], 6: [("pm", 3)], 7: ["xbo"],
              8: ["vt0", "vt2"], 12: [("sg", 0)], 13: [("sg", 1)], 14: [("sg", 2)], 15: [("sg", 3)]}.get(_u, [])
    if _u == 8:
        SKEYS.append("vt1")
    TKEYS.append(("tp", _u))
TKEYS += [("pv", 15), "ysum"]
S_TURN = {k: i for i, k in enumerate(SKEYS)}
T_TURN = {k: i for i, k in enumerate(TKEYS)}

DVE_OWN, ACT_OWN, POOL_OWN = 132, 0, 21
PARAMS = 3
CONSTS = 7
MEMSETS = 5


def program(nc, x_p, x_s, cache_k, cache_v, state_pool, w_in, w_out, norm_pre, norm_post, sinks, pool_w, pool_scale,
            ln_g, ln_b, sgu_w, sgu_b, c_cos, c_sin, c_band, c_smask, c_ident, c_sel, c_fix,
            y_p, y_s, nk_p, nv_p, npool_p, nk_s, nv_s, npool_s, nchunk_s, x_park):
    with ExitStack() as ctx:
        ctx.enter_context(nc.allow_non_contiguous_dma(reason="small parameters, a few hundred words a layer"))

        def sb(name, shape, dt=F32):
            return ctx.enter_context(nc.sbuf_tensor(name, shape, dt))

        def sem(name):
            return ctx.enter_context(nc.semaphore(name))

        h_hi = sb("h_hi", [P, KT, NTOK], F32R)
        h_lo = sb("h_lo", [P, KT, NTOK], F32R)
        mix = sb("mix", [P, KT, NTOK])
        w_raw = sb("w_raw", [P, 2, HK, P])
        w_hi = sb("w_hi", [P, 2, HK, P], F32R)
        w_lo = sb("w_lo", [P, 2, HK, P], F32R)
        arena = sb("arena", [P, KT * NTOK])
        k_hi = sb("k_hi", [P, SEQ], F32R)
        k_lo = sb("k_lo", [P, SEQ], F32R)
        q_st = sb("q_st", [P, GROUP, P], F32R)
        pt_hi = sb("pt_hi", [P, 2, GROUP * P], F32R)
        pt_lo = sb("pt_lo", [P, 2, GROUP * P], F32R)
        v_hi = sb("v_hi", [P, 2, 2, HD], F32R)
        v_lo = sb("v_lo", [P, 2, 2, HD], F32R)
        cos = sb("cos", [P, NTOK])
        sin = sb("sin", [P, NTOK])
        band = sb("band", [P, 2 * P])
        smask = sb("smask", [P, 2, P + NS])
        ident = sb("ident", [P, P])
        ones = sb("ones", [P, P])
        rms = sb("rms", [P, NTOK])
        acc = sb("acc", [P, NTOK])
        pars = sb("pars", [P, 3, SEQ])
        wmt = sb("wmt", [P, 4, P])
        w4 = sb("w4", [NS, 4, NS])
        poolw = sb("poolw", [P, 4, P])
        qbd = sb("qbd", [P, 2, DB, 32])
        stt = sb("stt", [P, 4, DB * HIST])
        g_pre = sb("g_pre", [P, DEPTH, KT])
        g_post = sb("g_post", [P, DEPTH, KT])
        pscale = sb("pscale", [P, 4])
        sink = sb("sink", [P, NH])
        sel = sb("sel", [P, 8])
        fix = sb("fix", [P, 4, 16])
        v_new = sb("v_new", [NS, 4 * HD])
        xbo = sb("xbo", [HIST + NS, SEQ])
        xb_keep = sb("xb_keep", [P, 4, HIST + NS])
        eps = sb("eps", [P, 1])
        zeros = sb("zeros", [P, HIST])
        junk = sb("junk", [P, 6])
        sm = sb("sm", [P, 2, 6, GROUP])
        sms = sb("sms", [P, 8, 4])
        ssel = sb("ssel", [P, 2, 8])
        ssink = sb("ssink", [P, 2])
        es = sb("es", [P, GROUP])
        ess = sb("ess", [P, 4])
        stats = sb("stats", [P, 5, 6])
        mv = sb("mv", [P, 5, 2])
        rstd = sb("rstd", [P, 5])

        at = [0]

        def part(n):
            at[0] += n
            assert at[0] <= KT * NTOK
            return arena[:, at[0] - n:at[0]]

        zr = part(2 * NTOK).rearrange("p (a n) -> p a n", a=2)
        krot = part(2 * NTOK).rearrange("p (a n) -> p a n", a=2)
        v_tok = part(NBLK * 4 * HD).rearrange("p (b f) -> p b f", b=NBLK)
        prob = part(GROUP * 2 * P).rearrange("p (h k) -> p h k", h=GROUP)
        late = part(2 * DB * (P + NS))
        kct = late.rearrange("p (a b k) -> p a b k", a=2, b=DB)
        ps = late[:, 0:4 * (P + NS)].rearrange("p (a k) -> p a k", a=4)
        pst = late[:, 4 * (P + NS):4 * (P + NS) + 1024].rearrange("p (a k) -> p a k", a=2)
        vn = late.rearrange("p (b f) -> p b f", b=5)
        ext_a = part(EXT)
        ext_b = part(EXT)
        th = part(NTOK)
        ext_c = pars[:, :, :].rearrange("p a n -> p (a n)")[:, 0:EXT]
        sq = pars[:, :, :].rearrange("p a n -> p (a n)")[:, 0:2 * NTOK].rearrange("p (a n) -> p a n", a=2)
        tmp = ext_a[:, 0:NTOK]
        x_old = arena[:, :].rearrange("p (t n) -> p t n", t=KT)
        stage = arena[:, 0:NBLK * D].rearrange("p (b f) -> p b f", b=NBLK)
        g_raw = arena[0:DEPTH * KT, NBLK * D:NBLK * D + 2 * P].rearrange("p (a n) -> p a n", a=2)
        stage_s = w_raw[0:NS, :, :, :].rearrange("p a b c -> p (a b c)")
        cache = mix[:, 12:16, :].rearrange("p a n -> p (a n)")[:, 0:DB * 4 * HD].rearrange("p (b f) -> p b f", b=DB)
        outs = mix[:, 8:10, :].rearrange("p a n -> p (a n)")
        k_tail, k_new = outs[:, 0:256], outs[0:NS, 256:512]
        sgw_raw = prob[:, 0:2, :].rearrange("p h k -> p (h k)").rearrange("p (h s) -> p h s", h=4)
        st_raw = prob[0:DB * HIST, 2:4, :].rearrange("p h k -> p (h k)")

        Z = [ctx.enter_context(nc.psum_tensor(f"z{j}", [P, 2, 512], F32)) for j in range(2)]
        S = ctx.enter_context(nc.psum_tensor("side_s", [P, 2, 512], F32))
        T = ctx.enter_context(nc.psum_tensor("side_t", [P, 2, 512], F32))

        const_in, x_in, g_in, w4_in, par_in, lnp_in, raw_in, kc_in, vc_in, park_in = (sem(n) for n in (
            "const_in", "x_in", "g_in", "w4_in", "par_in", "lnp_in", "raw_in", "kc_in", "vc_in", "park_in"))
        w_landed = [sem("w_landed0"), sem("w_landed1")]
        park_out, kv_out, xb_out, vn_out, fin_out, copy_out = (sem(n) for n in (
            "park_out", "kv_out", "xb_out", "vn_out", "fin_out", "copy_out"))
        ready0, g_full, g_ready, xt_full, xt_act = (sem(n) for n in ("ready0", "g_full", "g_ready", "xt_full", "xt_act"))
        x_ready = sem("x_ready")
        w_hi_ready = sem("w_hi_ready")
        w_split = sem("w_split")
        w_half_used = sem("w_half_used")
        z_ready = sem("z_ready")
        z_free = sem("z_free")
        h_hi_ready, h_ready = sem("h_hi_ready"), sem("h_ready")
        sq_ready, acc_done = sem("sq_ready"), sem("acc_done")
        root_ready, rms_ready = sem("root_ready"), sem("rms_ready")
        s_full, s_free, t_full, t_free = sem("s_full"), sem("s_free"), sem("t_full"), sem("t_free")
        kv_rot, q_rot, kct_new = sem("kv_rot"), sem("q_rot"), sem("kct_new")
        wm_masked, qbd_ready = sem("wm_masked"), sem("qbd_ready")
        khi_ready, klo_ready, qhi_ready, qlo_ready, vhi_ready, vlo_ready, pthi_ready = (sem(n) for n in (
            "khi_ready", "klo_ready", "qhi_ready", "qlo_ready", "vhi_ready", "vlo_ready", "pthi_ready"))
        max_ready, exp_ready, den_ready, norm_ready, smax_ready, sexp_ready, sprob_ready = (sem(n) for n in (
            "max_ready", "exp_ready", "den_ready", "norm_ready", "smax_ready", "sexp_ready", "sprob_ready"))
        ext_ready, pooled_ready = sem("ext_ready"), sem("pooled_ready")
        var_ready, std_ready, ln_mid, vn_ready, sg_out = (sem(n) for n in ("var_ready", "std_ready", "ln_mid", "vn_ready", "sg_out"))
        gate_th, gate_t, gate_done = sem("gate_th"), sem("gate_t"), sem("gate_done")
        fin_full, fin_act = sem("fin_full"), sem("fin_act")
        own_v, own_a, own_p = sem("own_v"), sem("own_a"), sem("own_p")

        block = ctx.enter_context(nc.Block())

        def apart(eng):
            eng.nop(nofuse=True)

        class Own:

            def __init__(self, eng, s, per_layer):
                self.eng, self.s, self.per, self.n, self.extra, self.layer = eng, s, per_layer, 0, 0, None

            def mark(self, ins):
                ins.then_inc(self.s, 1)
                self.n += 1

            def settle(self):
                self.eng.wait_ge(self.s, self.layer * self.per + self.extra + self.n)

            @contextmanager
            def repeat(self, times, per_pass):
                first = self.n
                with self.eng.Fori(0, times) as i:
                    self.extra = i * per_pass
                    yield i
                assert self.n - first == per_pass, (self.n - first, per_pass)
                self.extra, self.n = 0, first + times * per_pass

        def two(ap):
            return ap.rearrange("p (c n) -> p c n", c=2)

        def zcols(z):
            return z[:, :, 0:HALF]

        class Sides:

            def __init__(self, eng, layer):
                self.eng, self.layer = eng, layer

            def _(self, key):
                if key in S_TURN:
                    return s_full, s_free, self.layer * len(SKEYS) + S_TURN[key]
                return t_full, t_free, self.layer * len(TKEYS) + T_TURN[key]

            def wait_free(self, key):
                _, free, turn = self._(key)
                self.eng.wait_ge(free, turn + 1)

            def wait_full(self, key):
                full, _, turn = self._(key)
                self.eng.wait_ge(full, turn + 1)

            def wait_read(self, key):
                _, free, turn = self._(key)
                self.eng.wait_ge(free, turn + 2)

            def filled(self, key, ins):
                ins.then_inc(self._(key)[0], 1)

            def freed(self, key, ins):
                ins.then_inc(self._(key)[1], 1)

        @block.sync
        def _(sp):
            sp.dma_start(stage, x_p.rearrange("a (b p) f -> p (a b) f", p=P)).then_inc(x_in, 16)
            sp.dma_start(stage_s, x_s.rearrange("b t f -> (b t) f")).then_inc(x_in, 16)
            sp.wait_ge(x_ready, KT)
            with sp.Fori(0, DEPTH) as l:
                def load_in(n, col):
                    for h in range(2):
                        sp.wait_ge(w_split, l * (2 * NB) + n * 2 + h + 1)
                        apart(sp)
                        sp.dma_start(w_raw[:, h, :, :],
                                     w_in[l, h * HK * P:(h + 1) * HK * P, bass.ds(col, P)].rearrange("(k p) c -> p k c", p=P)
                                     ).then_inc(w_landed[h], 16)

                def load_out(n, col):
                    for h in range(2):
                        r0 = OUT_ORDER[h * HK] * P
                        sp.wait_ge(w_split, l * (2 * NB) + n * 2 + h + 1)
                        apart(sp)
                        sp.dma_start(w_raw[:, h, :, :],
                                     w_out[l, r0:r0 + HK * P, bass.ds(col, P)].rearrange("(k p) c -> p k c", p=P)
                                     ).then_inc(w_landed[h], 16)

                starts = [KV0, Q0, XB0, VS0, U0, GB0, GC0, GA0, OUT0]
                for a, b in zip(starts[:-1], starts[1:]):
                    with sp.Fori(0, b - a) as i:
                        load_in(a + i, COL[a] + i * P)
                with sp.Fori(0, N_OUT) as i:
                    load_out(OUT0 + i, i * P)

        @block.tensor
        def _(pe):
            pe.wait_ge(const_in, 16 * CONSTS)
            pe.wait_ge(x_in, 32)
            pe.wait_ge(ready0, MEMSETS)
            pairs = [Z[0], Z[1], S, T]
            pe.wait_ge(g_in, 32)
            for i in range(2):
                mm = pe.transpose(T[:, 0, i * DEPTH * KT:(i + 1) * DEPTH * KT], g_raw[:, i, :], ident[0:DEPTH * KT, 0:DEPTH * KT])
            mm.then_inc(g_full, 1)
            for t in range(KT):
                o = pairs[t % 4]
                if t == 3:
                    pe.wait_ge(g_ready, 2)
                if t >= 4:
                    pe.wait_ge(x_ready, t - 3)
                for b in range(NBLK):
                    pe.transpose(o[:, 0, b * P:(b + 1) * P], stage[:, b, t * P:(t + 1) * P], ident[:, :])
                pe.transpose(o[:, 1, 0:NS], stage_s[:, t * P:(t + 1) * P], ident[0:NS, 0:NS]).then_inc(xt_full, 1)
            pe.wait_ge(x_ready, KT)

            with pe.Fori(0, DEPTH) as l:
                side = Sides(pe, l)

                def run(n, j, phase=0, first=False, mids=None, base=0):
                    mids = mids or {}
                    order = OUT_ORDER if phase else range(KT)
                    pe.wait_ge(z_free, l * NB + n + 1)
                    for i, k in enumerate(order):
                        h, kk = divmod(i, HK)
                        if kk == 0:
                            pe.wait_ge(w_split, l * (2 * NB) + n * 2 + h + 3)
                        if first:
                            pe.wait_ge(h_ready, (l * 2 + phase) * KT + i + 1)
                        for w, x in ((w_hi, h_hi), (w_hi, h_lo), (w_lo, h_hi)):
                            for c in range(2):
                                mm = pe.matmul(Z[j][:, c, 0:HALF], w[:, h, kk, :], x[:, k, c * HALF:(c + 1) * HALF],
                                               start=(i == 0 and w is w_hi and x is h_hi), stop=(i == KT - 1 and w is w_lo))
                        if i == HK - 1:
                            mm.then_inc(w_half_used, 1)
                        if i == KT - 1:
                            mm.then_inc(z_ready, 1)
                        if i in mids:
                            mids[i]()

                def turn_many(key, moves):
                    side.wait_free(key)
                    apart(pe)
                    for o, i in moves:
                        mm = pe.transpose(o, i, ident[0:i.shape[0], 0:i.shape[0]])
                    side.filled(key, mm)

                def rms_sum(key, o, count):
                    pe.wait_ge(acc_done, l * 30 + count)
                    side.wait_free(key)
                    for c in range(2):
                        mm = pe.matmul(o[:, c, 0:HALF], ones[:, :], acc[:, c * HALF:(c + 1) * HALF], start=True, stop=True)
                    side.filled(key, mm)

                def scores(u):
                    g, b = divmod(u, NBLK)
                    side.wait_free(("sc", u))
                    pe.wait_ge(qlo_ready, l * 16 + u + 1)
                    if b == 0:
                        pe.wait_ge(klo_ready, l * 4 + g + 1)
                    k0 = max(b - 1, 0) * P
                    w = (b + 1) * P - k0
                    for hh in range(GROUP):
                        o = S[:, hh // 2, (hh % 2) * 2 * P:(hh % 2) * 2 * P + w]
                        for kk in (k_hi, k_lo):
                            mm = pe.matmul(o, q_st[:, hh, :], kk[:, k0:k0 + w], start=(kk is k_hi), stop=(kk is k_lo))
                    side.filled(("sc", u), mm)

                def turn_probs(u):
                    b = u % NBLK
                    pe.wait_ge(norm_ready, l * 16 + u + 1)
                    nk = 1 if b == 0 else 2
                    turn_many(("tp", u), [(T[:, kb, hh * P:(hh + 1) * P], prob[:, hh, kb * P:(kb + 1) * P])
                                          for kb in range(nk) for hh in range(GROUP)])

                def values(u):
                    b = u % NBLK
                    side.wait_read(("tp", u))
                    pe.wait_ge(vlo_ready, l * 16 + u + 1)
                    side.wait_free(("pv", u))
                    nk = 1 if b == 0 else 2
                    terms = [(v, p, kb) for kb in range(nk) for v, p in ((v_hi, pt_hi), (v_hi, pt_lo), (v_lo, pt_hi))]
                    for i, (v, p, kb) in enumerate(terms):
                        mm = pe.matmul(T[:, 0, :], v[:, kb, :, :], p[:, kb, :], start=(i == 0), stop=(i == len(terms) - 1))
                    side.filled(("pv", u), mm)

                def pool_mm(g):
                    pe.wait_ge(pooled_ready, l * 4 + g + 1)
                    side.wait_free(("pm", g))
                    for c in range(2):
                        mm = pe.matmul(T[:, c, 0:HALF], poolw[:, g, :], mix[:, 8 + g, c * HALF:(c + 1) * HALF], start=True, stop=True)
                    side.filled(("pm", g), mm)

                def turn_xb():
                    pe.wait_ge(ext_ready, l * 4 + 4)
                    turn_many("xbo", [(T[0:HIST + NS, 0, g * P:(g + 1) * P], xb_keep[:, g, :]) for g in range(4)])

                def turn_vs(key):
                    pe.wait_ge(z_free, l * NB + VS0 + 3 + 3)
                    if key == "vt2":
                        turn_many(key, [(T[0:NS, 0, t * P:(t + 1) * P], mix[:, 12 + t, SEQ:NTOK]) for t in range(4)])
                    else:
                        o, b0 = (T, 0) if key == "vt0" else (S, 2)
                        turn_many(key, [(o[:, b, t * P:(t + 1) * P], mix[:, 12 + t, (b0 + b) * P:(b0 + b + 1) * P])
                                        for b in range(2) for t in range(4)])

                def spatial(hh):
                    pe.wait_ge(vn_ready, l + 1)
                    pe.wait_ge(wm_masked, l + 1)
                    pe.wait_ge(w4_in, DB * 16 * (l + 1))
                    side.wait_free(("sg", hh))
                    for b in range(NBLK):
                        pe.matmul(T[:, 0, b * P:(b + 1) * P], vn[:, b, hh * P:(hh + 1) * P], wmt[:, hh, :], start=True, stop=True)
                    mm = pe.matmul(T[:, 1, 0:NS], vn[0:NS, 4, hh * P:(hh + 1) * P], w4[:, hh, :], start=True, stop=True)
                    side.filled(("sg", hh), mm)

                def sample_scores():
                    pe.wait_ge(qbd_ready, l * 16 + 16)
                    pe.wait_ge(kct_new, l * 2 + 2)
                    side.wait_read("kc0")
                    side.wait_read("kc1")
                    side.wait_free("ssc")
                    for b in range(DB):
                        r = (b % 4) * 32
                        for p in range(2):
                            mm = pe.matmul(S[r:r + 32, b // 4, p * (P + NS):(p + 1) * (P + NS)], qbd[:, p, b, :], kct[:, p, b, :],
                                           start=True, stop=True)
                    side.filled("ssc", mm)

                def sample_turn():
                    pe.wait_ge(sprob_ready, l + 1)
                    turn_many("spt", [(T[:, 0, q * P:(q + 1) * P], ps[:, q, 0:P]) for q in range(4)]
                              + [(T[0:NS, 1, q * P:(q + 1) * P], ps[:, q, P:P + NS]) for q in range(4)])

                def sample_values():
                    side.wait_read("spt")
                    pe.wait_ge(vc_in, 16 * (l + 1))
                    side.wait_free("spv")
                    new = pst[0:NS, 1, :].rearrange("p (c a r) -> p c a r", c=2, a=2)
                    for p in range(2):
                        pe.matmul(T[:, 0, p * 256:(p + 1) * 256].rearrange("p (c r) -> p c r", c=2), v_new[:, p * P:(p + 1) * P],
                                  new[:, :, p, :], start=True, stop=False)
                        for b in range(DB):
                            c0 = (b // 4) * 256 + p * P + (b % 4) * 32
                            mm = pe.matmul(T[:, 0, p * 256 + b * 32:p * 256 + (b + 1) * 32], cache[:, b, p * P:(p + 1) * P],
                                           pst[:, 0, c0:c0 + 32], start=False, stop=(b == DB - 1))
                    side.filled("spv", mm)

                for n in range(KV0, Q0):
                    run(n, n % 2, first=(n == 0))
                    if n == 0:
                        rms_sum("xsum", S, 15)
                pe.wait_ge(z_free, l * NB + Q0 - 1 + 3)
                turn_many("v", [(T[:, t, b * P:(b + 1) * P], zr[:, t, b * P:(b + 1) * P]) for t in range(2) for b in range(NBLK)])
                pe.wait_ge(kv_rot, l * 2 + 2)
                turn_many("kvtail", [(S[:, 0, t * P:(t + 1) * P], krot[:, t, SEQ - P:SEQ]) for t in range(2)]
                          + [(S[0:NS, 1, t * P:(t + 1) * P], zr[:, t, SEQ:NTOK]) for t in range(2)]
                          + [(S[0:NS, 1, 256 + t * P:256 + (t + 1) * P], krot[:, t, SEQ:NTOK]) for t in range(2)])
                pe.wait_ge(kc_in, 16 * (l + 1))
                for key, o, b0 in (("kc0", T, 0), ("kc1", S, 4)):
                    turn_many(key, [(o[:, p, b * P:(b + 1) * P], cache[:, b0 + b, p * P:(p + 1) * P]) for p in range(2) for b in range(4)])
                pe.wait_ge(raw_in, 32 * (l + 1))
                turn_many("wm", [(T[:, 0, h * P:(h + 1) * P], sgw_raw[:, h, :]) for h in range(4)])
                turn_many("state", [(S[:, 0, g * DB * HIST:(g + 1) * DB * HIST], st_raw[:, g * P:(g + 1) * P]) for g in range(4)])
                with pe.Fori(0, (XB0 - Q0) // 2) as i:
                    for j in range(2):
                        run(Q0 + i * 2 + j, j)
                sample_scores()
                for u in range(16):
                    extra = {1: sample_turn, 2: sample_values, 3: lambda: pool_mm(0), 4: lambda: pool_mm(1),
                             5: lambda: pool_mm(2), 6: lambda: pool_mm(3), 7: turn_xb,
                             8: lambda: turn_vs("vt0"), 12: lambda: spatial(0), 13: lambda: spatial(1),
                             14: lambda: spatial(2), 15: lambda: spatial(3)}
                    mids = {4: (lambda u=u: values(u - 1)) if u else (lambda: None)}
                    if u in extra:
                        mids[8] = extra[u]
                    if u == 8:
                        mids[11] = lambda: turn_vs("vt1")
                        mids[13] = lambda: turn_vs("vt2")
                    scores(u)
                    run(XB0 + u, u % 2, mids=mids)
                    turn_probs(u)
                values(15)
                with pe.Fori(0, (OUT0 - GC0) // 2) as i:
                    for j in range(2):
                        run(GC0 + i * 2 + j, j)
                for n in (OUT0, OUT0 + 1):
                    run(n, n % 2, phase=1, first=(n == OUT0))
                with pe.Fori(0, (N_OUT - 4) // 2) as i:
                    for j in range(2):
                        run(OUT0 + 2 + i * 2 + j, j, phase=1)
                for n in (NB - 2, NB - 1):
                    run(n, n % 2, phase=1)
                rms_sum("ysum", T, 30)

            for b in range(NBLK + 1):
                for q in range(4):
                    r = b * 4 + q
                    o = pairs[r % 4]
                    if r >= 4:
                        pe.wait_ge(fin_act, r - 3)
                    else:
                        pe.wait_ge(x_ready, (DEPTH + 1) * KT)
                    for t in range(4 * q, 4 * q + 4):
                        if b < NBLK:
                            mm = pe.transpose(o[:, 0, (t % 4) * P:(t % 4 + 1) * P], mix[:, t, b * P:(b + 1) * P], ident[:, :])
                        else:
                            mm = pe.transpose(o[0:NS, 0, (t % 4) * P:(t % 4 + 1) * P], mix[:, t, SEQ:NTOK], ident[:, :])
                    mm.then_inc(fin_full, 1)


        @block.scalar
        def _(act):
            for t in range(KT):
                act.wait_ge(xt_full, t + 1)
                act.activation(mix[:, t, 0:SEQ], [Z[0], Z[1], S, T][t % 4][:, 0, :], ACT.Copy).then_inc(xt_act, 1)
            act.wait_ge(ready0, MEMSETS)
            with act.Fori(0, DEPTH) as l:
                own = Own(act, own_a, ACT_OWN)
                own.layer = l
                side = Sides(act, l)

                def split(n, h):
                    act.wait_ge(w_landed[h], (l * NB + n + 1) * 16)
                    act.wait_ge(z_ready if h else w_half_used, l * NB + n + 1)
                    act.activation(w_hi[:, h, :, :], w_raw[:, h, :, :], ACT.Copy).then_inc(w_hi_ready, 1)

                def z_read(n):
                    act.wait_ge(z_free, l * NB + n + 3)

                def root(key, o):
                    side.wait_full(key)
                    act.activation(two(rms[:, :]), zcols(o), ACT.Sqrt, bias=eps[:, 0:1], scale=1.0 / D).then_inc(root_ready, 1)

                def stage_k(g):
                    s, t = (g % 2) * HD, g // 2
                    if g == 0:
                        act.wait_ge(kv_rot, l * 2 + 2)
                    else:
                        side.wait_full(("sc", 4 * g - 1))
                    act.activation(k_hi[s:s + HD, :], krot[s:s + HD, t, 0:SEQ], ACT.Copy)
                    act.activation(k_hi[HD - s:2 * HD - s, :], krot[s:s + HD, t, 0:SEQ], ACT.Copy).then_inc(khi_ready, 1)

                def stage_q(u):
                    g, b = divmod(u, NBLK)
                    if u == 0:
                        act.wait_ge(q_rot, l * 8 + 8)
                    else:
                        side.wait_full(("sc", u - 1))
                    for s in range(2):
                        ins = act.activation(q_st[s * HD:(s + 1) * HD, s:GROUP:2, :],
                                             mix[s * HD:(s + 1) * HD, 2 * g:2 * g + 2, b * P:(b + 1) * P], ACT.Copy)
                    ins.then_inc(qhi_ready, 1)

                def stage_v(u):
                    g, b = divmod(u, NBLK)
                    if u == 0:
                        side.wait_read("v")
                    else:
                        side.wait_full(("pv", u - 1))
                    b0, nk = max(b - 1, 0), min(b + 1, 2)
                    act.activation(v_hi[:, 0:nk, :, :],
                                   v_tok[:, b0:b0 + nk, g * HD:(g + 1) * HD].unsqueeze(2).broadcast_to((P, nk, 2, HD)),
                                   ACT.Copy).then_inc(vhi_ready, 1)

                def probs_hi(u):
                    nk = min(u % NBLK + 1, 2)
                    side.wait_full(("tp", u))
                    act.activation(pt_hi[:, 0:nk, :], T[:, 0:nk, :], ACT.Copy).then_inc(pthi_ready, 1)

                def attended(u):
                    g, b = divmod(u, NBLK)
                    side.wait_full(("pv", u))
                    for s in range(2):
                        o = T[s * HD:(s + 1) * HD, 0, :].rearrange("p (i s q) -> p i s q", i=2, s=2)[:, :, s, :]
                        ins = act.activation(mix[s * HD:(s + 1) * HD, 2 * g:2 * g + 2, b * P:(b + 1) * P], o, ACT.Copy)
                    side.freed(("pv", u), ins)

                def exps(u):
                    w = P * min(u % NBLK + 1, 2)
                    act.wait_ge(max_ready, l * 16 + u + 1)
                    for hh in range(GROUP):
                        act.activation(prob[:, hh, 0:w], prob[:, hh, 0:w], ACT.Exp, bias=sm[:, u % 2, 2, hh:hh + 1], scale=SCALE,
                                       accum_out=sm[:, u % 2, 4, hh:hh + 1])
                    act.activation(es[:, :], sm[:, u % 2, 3, :], ACT.Exp).then_inc(exp_ready, 1)

                def sample_exps():
                    act.wait_ge(smax_ready, l + 1)
                    for q in range(4):
                        act.activation(ps[:, q, :], ps[:, q, :], ACT.Exp, bias=sms[:, 2, q:q + 1], scale=SCALE,
                                       accum_out=sms[:, 4, q:q + 1])
                    act.activation(ess[:, :], sms[:, 3, :], ACT.Exp).then_inc(sexp_ready, 1)

                def sample_probs_out():
                    side.wait_full("spt")
                    act.activation(pst[:, 0, :], T[:, 0, :], ACT.Copy)
                    side.freed("spt", act.activation(pst[0:NS, 1, :], T[0:NS, 1, :], ACT.Copy))

                def sample_attended():
                    side.wait_full("spv")
                    for p in range(2):
                        for kv in range(2):
                            for s in range(2):
                                t = 4 * p + 2 * kv
                                o = T[kv * HD:(kv + 1) * HD, 0, p * 256:(p + 1) * 256].rearrange(
                                    "p (b v i s t) -> p b v i s t", b=DB, v=2, i=2, s=2)
                                for i in range(2):
                                    ins = act.activation(
                                        mix[s * HD:(s + 1) * HD, t + i, SEQ:NTOK].rearrange("p (b t) -> p b t", b=DB),
                                        o[:, :, kv, i, s, :], ACT.Copy)
                    side.freed("spv", ins)

                def extend(g):
                    z_read(XB0 + g)
                    if g:
                        act.wait_ge(pooled_ready, l * 4 + g)
                    z = zr[:, g % 2, :]
                    tail = ext_a[:, HIST + SEQ:EXT].rearrange("p (b n) -> p b n", b=DB)
                    act.activation(ext_a[:, 0:HIST], zeros[:, :], ACT.Copy)
                    act.activation(ext_a[:, HIST:HIST + SEQ], z[:, 0:SEQ], ACT.Copy)
                    act.activation(tail[:, :, HIST:SEXT], z[:, SEQ:NTOK].rearrange("p (b t) -> p b t", b=DB), ACT.Copy)
                    act.activation(tail[:, :, 0:HIST], stt[:, g, :].rearrange("p (b t) -> p b t", b=DB), ACT.Copy)
                    act.activation(xb_keep[:, g, :], z[:, SEQ - HIST:NTOK], ACT.Copy).then_inc(ext_ready, 1)

                def tanh(n, j):
                    z_read(n)
                    if not isinstance(n, int) or n > GB0:
                        act.wait_ge(gate_done, l * 16 + n - GB0)
                    act.activation(th[:, :], zr[:, j, :], ACT.Tanh, scale=0.5).then_inc(gate_th, 1)

                split(KV0, 0)
                for t in range(KT):
                    act.wait_ge(x_ready, l * KT + t + 1)
                    if t == 0:
                        act.wait_ge(z_ready, l * NB + 1)
                    act.activation(h_hi[:, t, :], mix[:, t, :], ACT.Copy, scale=g_pre[:, l, t:t + 1]).then_inc(h_hi_ready, 1)
                    if t >= 3:
                        act.wait_ge(acc_done, l * 30 + t - 2)
                    act.activation(acc[:, :] if t == 0 else sq[:, t % 2, :], mix[:, t, :], ACT.Square).then_inc(sq_ready, 1)
                    if t == HK - 1:
                        split(KV0, 1)
                for n in range(KV0, Q0):
                    if n:
                        split(n, 1)
                    split(n + 1, 0)
                    if n == 0:
                        root("xsum", S)
                side.wait_full("v")
                side.freed("v", act.activation(v_tok.rearrange("p b (t f) -> p t b f", t=2),
                                               T[:, :, :].rearrange("p t (b f) -> p t b f", b=NBLK), ACT.Copy))
                side.wait_full("kvtail")
                act.wait_ge(park_out, 16 * (l + 1))
                act.activation(k_tail, S[:, 0, 0:256], ACT.Copy)
                act.activation(v_new[:, :], S[0:NS, 1, 0:256], ACT.Copy)
                side.freed("kvtail", act.activation(k_new, S[0:NS, 1, 256:512], ACT.Copy))
                for key, o, b0 in (("kc0", T, 0), ("kc1", S, 4)):
                    side.wait_full(key)
                    side.freed(key, act.activation(kct[:, :, b0:b0 + 4, 0:P], o[:, :, :].rearrange("p a (b k) -> p a b k", b=4), ACT.Copy))
                side.wait_full("wm")
                side.freed("wm", act.activation(wmt[:, :, :], T[:, 0, :].rearrange("p (h t) -> p h t", h=4), ACT.Copy))
                side.wait_full("state")
                side.freed("state", act.activation(stt[:, :, :], S[:, 0, 0:4 * DB * HIST].rearrange("p (g n) -> p g n", g=4), ACT.Copy))
                with act.Fori(0, XB0 - Q0) as i:
                    split(Q0 + i, 1)
                    split(Q0 + 1 + i, 0)
                stage_k(0)
                stage_q(0)
                for u in range(16):
                    n = XB0 + u
                    if u:
                        probs_hi(u - 1)
                    split(n, 1)
                    if u:
                        attended(u - 1)
                    stage_v(u)
                    if n > GB0:
                        tanh(n - 1, (n - 1) % 2)
                    exps(u)
                    if u == 0:
                        sample_exps()
                    if u == 1:
                        sample_probs_out()
                    if u == 2:
                        sample_attended()
                    split(n + 1, 0)
                    if u == 7:
                        side.wait_full("xbo")
                        side.freed("xbo", act.activation(xbo[:, :], T[0:HIST + NS, 0, :], ACT.Copy))
                    if u == 8:
                        for key, o, b0 in (("vt0", T, 0), ("vt1", S, 2)):
                            side.wait_full(key)
                            side.freed(key, act.activation(vn[:, b0:b0 + 2, :], o[:, :, :], ACT.Copy))
                        side.wait_full("vt2")
                        side.freed("vt2", act.activation(vn[0:NS, 4, :], T[0:NS, 0, :], ACT.Copy))
                    if u == 9:
                        act.wait_ge(var_ready, l + 1)
                        act.activation(rstd[:, 0:4], mv[:, 0:4, 1], ACT.Sqrt, bias=eps[:, 0:1])
                        act.activation(rstd[0:NS, 4:5], mv[0:NS, 4:5, 1], ACT.Sqrt, bias=eps[0:NS, 0:1]).then_inc(std_ready, 1)
                    if u < 15:
                        if (u + 1) % NBLK == 0:
                            stage_k((u + 1) // NBLK)
                        stage_q(u + 1)
                    if 1 <= u <= 4:
                        extend(u - 1)
                probs_hi(15)
                attended(15)
                with act.Fori(0, (OUT0 - GC0) // 2) as i:
                    for j in range(2):
                        n = GC0 + i * 2 + j
                        split(n, 1)
                        tanh(n - 1, 1 - j)
                        split(n + 1, 0)
                tanh(OUT0 - 1, 1)
                act.wait_ge(z_ready, l * NB + N_IN + 1)
                for i, k in enumerate(OUT_ORDER):
                    act.wait_ge(gate_done, l * 16 + i + 1)
                    act.activation(h_hi[:, k, :], mix[:, k, :], ACT.Copy, scale=0.5).then_inc(h_hi_ready, 1)
                    if i == HK - 1:
                        split(OUT0, 1)

                def y_square(n, j):
                    z_read(n)
                    act.wait_ge(acc_done, l * 30 + 15 + n - OUT0 - 2)
                    act.activation(sq[:, j, :], mix[:, n - OUT0, :] if isinstance(n, int) else mix[:, bass.ds(n - OUT0, 1), :].rearrange(
                        "p a n -> p (a n)"), ACT.Square).then_inc(sq_ready, 1)

                split(OUT0 + 1, 0)
                z_read(OUT0)
                act.activation(acc[:, :], mix[:, 0, :], ACT.Square).then_inc(sq_ready, 1)
                split(OUT0 + 1, 1)
                split(OUT0 + 2, 0)
                y_square(OUT0 + 1, 1)
                with act.Fori(0, (N_OUT - 4) // 2) as i:
                    for j in range(2):
                        n = OUT0 + 2 + i * 2 + j
                        split(n, 1)
                        split(n + 1, 0)
                        y_square(n, j)
                split(NB - 2, 1)
                split(NB - 1, 0)
                y_square(NB - 2, 0)
                split(NB - 1, 1)
                y_square(NB - 1, 1)
                root("ysum", T)

            for r in range(4 * (NBLK + 1)):
                b, q = divmod(r, 4)
                act.wait_ge(fin_full, r + 1)
                o = [Z[0], Z[1], S, T][r % 4]
                cols = slice(q * 512, (q + 1) * 512)
                if b < NBLK:
                    act.activation(stage[:, b, cols], o[:, 0, :], ACT.Copy).then_inc(fin_act, 1)
                else:
                    act.activation(stage_s[:, cols], o[0:NS, 0, :], ACT.Copy).then_inc(fin_act, 1)

        @block.vector
        def _(dve):
            dve.wait_ge(g_full, 1)
            for i, g in enumerate((g_pre, g_post)):
                dve.tensor_copy(g[:, :, :], T[:, 0, i * DEPTH * KT:(i + 1) * DEPTH * KT].rearrange("p (l t) -> p l t", l=DEPTH)).then_inc(g_ready, 1)
            for t in range(KT):
                dve.wait_ge(xt_act, t + 1)
                dve.tensor_copy(mix[:, t, SEQ:NTOK], [Z[0], Z[1], S, T][t % 4][:, 1, 0:NS]).then_inc(x_ready, 1)
            dve.wait_ge(const_in, 16 * CONSTS)
            with dve.Fori(0, DEPTH) as l:
                own = Own(dve, own_v, DVE_OWN)
                own.layer = l
                side = Sides(dve, l)

                def split(n, h):
                    dve.wait_ge(w_hi_ready, l * (2 * NB) + n * 2 + h + 1)
                    dve.tensor_tensor(w_lo[:, h, :, :], w_raw[:, h, :, :], w_hi[:, h, :, :].bitcast(F32), ALU.subtract).then_inc(w_split, 1)

                def z_out(n, j, dst):
                    dve.wait_ge(z_ready, l * NB + n + 2)
                    dve.tensor_tensor(two(dst), zcols(Z[j]), two(rms[:, :]), ALU.mult).then_inc(z_free, 1)

                def rotate(n, j, dst, done):
                    z = zr[:, j, :]
                    z_out(n, j, z)
                    dve.wait_ge(z_free, l * NB + n + 3)
                    own.mark(dve.tensor_tensor(dst, z, cos[:, :], ALU.mult))
                    for q in range(4):
                        a, b = q * 32, (q ^ 1) * 32
                        own.mark(dve.tensor_tensor(th[a:a + 32, :], z[b:b + 32, :], sin[b:b + 32, :], ALU.mult))
                    own.settle()
                    dve.tensor_tensor(dst, dst, th[:, :], ALU.add).then_inc(done, 1)

                def invert(key, count):
                    dve.wait_ge(root_ready, l * 2 + count)
                    side.freed(key, dve.reciprocal(rms[:, :], rms[:, :]))
                    side.wait_read(key)

                def stage_k(g):
                    s, t = (g % 2) * HD, g // 2
                    dve.wait_ge(khi_ready, l * 4 + g + 1)
                    for d in (s, HD - s):
                        ins = dve.tensor_tensor(k_lo[d:d + HD, :], krot[s:s + HD, t, 0:SEQ], k_hi[s:s + HD, :].bitcast(F32), ALU.subtract)
                    ins.then_inc(klo_ready, 1)

                def stage_q(u):
                    g, b = divmod(u, NBLK)
                    dve.wait_ge(qhi_ready, l * 16 + u + 1)
                    for s in range(2):
                        d = HD - s * HD
                        ins = dve.tensor_tensor(q_st[d:d + HD, s:GROUP:2, :], mix[s * HD:(s + 1) * HD, 2 * g:2 * g + 2, b * P:(b + 1) * P],
                                                q_st[s * HD:(s + 1) * HD, s:GROUP:2, :].bitcast(F32), ALU.subtract)
                    ins.then_inc(qlo_ready, 1)

                def stage_v(u):
                    g, b = divmod(u, NBLK)
                    b0, nk = max(b - 1, 0), min(b + 1, 2)
                    dve.wait_ge(vhi_ready, l * 16 + u + 1)
                    dve.tensor_tensor(v_lo[:, 0:nk, :, :],
                                      v_tok[:, b0:b0 + nk, g * HD:(g + 1) * HD].unsqueeze(2).broadcast_to((P, nk, 2, HD)),
                                      v_hi[:, 0:nk, :, :].bitcast(F32), ALU.subtract).then_inc(vlo_ready, 1)

                def probs_lo(u):
                    nk = min(u % NBLK + 1, 2)
                    dve.wait_ge(pthi_ready, l * 16 + u + 1)
                    side.freed(("tp", u), dve.tensor_tensor(pt_lo[:, 0:nk, :], T[:, 0:nk, :], pt_hi[:, 0:nk, :].bitcast(F32), ALU.subtract))

                def maxima(u):
                    b = u % NBLK
                    w = P * min(b + 1, 2)
                    mask = band[:, 2 * P - w:2 * P]
                    c = sm[:, u % 2, :, :]
                    side.wait_full(("sc", u))
                    apart(dve)
                    for hh in range(GROUP):
                        ins = dve.tensor_tensor_reduce(prob[:, hh, 0:w], S[:, hh // 2, (hh % 2) * 2 * P:(hh % 2) * 2 * P + w], mask,
                                                       1.0, NEG, ALU.add, ALU.max, c[:, 0, hh:hh + 1])
                    side.freed(("sc", u), ins)
                    side.wait_read(("sc", u))
                    own.mark(dve.scalar_tensor_tensor(c[:, 1, :], c[:, 0, :], SCALE, sink[:, 4 * (u // NBLK):4 * (u // NBLK) + 4],
                                                      ALU.mult, ALU.max))
                    own.settle()
                    own.mark(dve.tensor_scalar(c[:, 2, :], c[:, 1, :], -1.0, None, ALU.mult))
                    own.settle()
                    dve.tensor_tensor(c[:, 3, :], c[:, 2, :], sink[:, 4 * (u // NBLK):4 * (u // NBLK) + 4], ALU.add).then_inc(max_ready, 1)

                def denominators(u):
                    c = sm[:, u % 2, :, :]
                    dve.wait_ge(exp_ready, l * 16 + u + 1)
                    own.mark(dve.tensor_tensor(c[:, 1, :], c[:, 4, :], es[:, :], ALU.add))
                    own.settle()
                    dve.reciprocal(c[:, 5, :], c[:, 1, :]).then_inc(den_ready, 1)

                def sample_maxima():
                    side.wait_full("ssc")
                    side.freed("ssc", dve.tensor_tensor(
                        ps.rearrange("p (c a) k -> p c a k", c=2),
                        S[:, :, 0:2 * (P + NS)].rearrange("p c (a k) -> p c a k", a=2),
                        smask[:, :, :].unsqueeze(2).broadcast_to((P, 2, 2, P + NS)), ALU.add))
                    own.mark(dve.tensor_tensor(ssel[:, :, :], sink[:, :].rearrange("p (a e) -> p a e", a=2),
                                               sel[:, :].unsqueeze(1).broadcast_to((P, 2, 8)), ALU.mult))
                    own.settle()
                    own.mark(dve.tensor_reduce(ssink[:, :], ssel[:, :, :], AX_X, ALU.add))
                    side.wait_read("ssc")
                    own.mark(dve.tensor_reduce(sms[:, 0, :], ps, AX_X, ALU.max))
                    own.settle()
                    sk = ssink[:, :].unsqueeze(1).broadcast_to((P, 2, 2))

                    def col(i):
                        return sms[:, i, :].rearrange("p (c a) -> p c a", c=2)

                    own.mark(dve.scalar_tensor_tensor(col(1), col(0), SCALE, sk, ALU.mult, ALU.max))
                    own.settle()
                    own.mark(dve.tensor_scalar(sms[:, 2, :], sms[:, 1, :], -1.0, None, ALU.mult))
                    own.settle()
                    dve.tensor_tensor(col(3), col(2), sk, ALU.add).then_inc(smax_ready, 1)

                def sample_probs():
                    dve.wait_ge(sexp_ready, l + 1)
                    own.mark(dve.tensor_tensor(sms[:, 1, :], sms[:, 4, :], ess[:, :], ALU.add))
                    own.settle()
                    own.mark(dve.reciprocal(sms[:, 5, :], sms[:, 1, :]))
                    own.settle()
                    dve.tensor_tensor(ps, ps, sms[:, 5, :].unsqueeze(2).broadcast_to((P, 4, P + NS)), ALU.mult).then_inc(sprob_ready, 1)

                def gate(n, tile):
                    dve.wait_ge(gate_t, l * 16 + n - GB0 + 1)
                    dve.wait_ge(gate_th, l * 16 + n - GB0 + 1)
                    dve.scalar_tensor_tensor(tile, th[:, :], 1.0, tile, ALU.add, ALU.mult).then_inc(gate_done, 1)

                def tile_at(t):
                    return mix[:, bass.ds(t, 1), :].rearrange("p a n -> p (a n)")

                dve.wait_ge(w_hi_ready, l * (2 * NB) + 1)
                split(KV0, 0)
                for t in range(KT):
                    dve.wait_ge(h_hi_ready, l * 2 * KT + t + 1)
                    dve.scalar_tensor_tensor(h_lo[:, t, :], mix[:, t, :], g_pre[:, l, t:t + 1], h_hi[:, t, :].bitcast(F32),
                                             ALU.mult, ALU.subtract).then_inc(h_ready, 1)
                    if t == HK - 1:
                        split(KV0, 1)
                for n in range(KV0, Q0):
                    if n:
                        split(n, 1)
                    split(n + 1, 0)
                    if n == 0:
                        invert("xsum", 1)
                    if n < 2:
                        rotate(n, n % 2, krot[:, n, :], kv_rot)
                    else:
                        z_out(n, n % 2, zr[:, n % 2, :])
                dve.wait_ge(kv_rot, l * 2 + 2)
                for p in range(2):
                    dve.tensor_copy(kct[:, p, :, P:P + NS], krot[:, p, SEQ:NTOK].unsqueeze(1).broadcast_to((P, DB, NS))).then_inc(kct_new, 1)
                side.wait_full("kvtail")
                dve.wait_ge(park_out, 16 * (l + 1))
                apart(dve)
                with own.repeat((XB0 - Q0) // 2, 10) as i:
                    for j in range(2):
                        n = Q0 + i * 2 + j
                        split(n, 1)
                        split(n + 1, 0)
                        rotate(n, j, tile_at(i * 2 + j), q_rot)
                dve.wait_ge(q_rot, l * 8 + 8)
                for p in range(2):
                    for kv in range(2):
                        for s in range(2):
                            for i in range(2):
                                dve.tensor_copy(
                                    qbd[kv * HD:(kv + 1) * HD, p, :, :].rearrange("p b (v i s t) -> p b v i s t", v=2, i=2, s=2)[:, :, kv, i, s, :],
                                    mix[s * HD:(s + 1) * HD, 4 * p + 2 * kv + i, SEQ:NTOK].rearrange("p (b t) -> p b t", b=DB)
                                ).then_inc(qbd_ready, 1)
                stage_k(0)
                stage_q(0)
                dve.wait_ge(par_in, PARAMS * 16 * (l + 1))
                for u in range(16):
                    n = XB0 + u
                    if u:
                        probs_lo(u - 1)
                    split(n, 1)
                    if u == 0:
                        sample_maxima()
                    maxima(u)
                    stage_v(u)
                    if n > GB0:
                        gate(n - 1, mix[:, n - 1 - 16, :])
                    denominators(u)
                    if u == 0:
                        sample_probs()
                    split(n + 1, 0)
                    if 3 <= u <= 6:
                        g = u - 3
                        side.wait_full(("pm", g))
                        side.freed(("pm", g), dve.tensor_scalar(two(mix[:, 8 + g, :]), zcols(T), pscale[:, g:g + 1], None, ALU.mult))
                    if u >= 12:
                        hh = u - 12
                        side.wait_full(("sg", hh))
                        if hh:
                            dve.wait_ge(sg_out, l * 4 + hh)
                        own.mark(dve.tensor_tensor(tmp[:, 0:SEQ].rearrange("p (b t) -> p b t", b=NBLK),
                                                   T[:, 0, :].rearrange("p (b t) -> p b t", b=NBLK),
                                                   pars[:, 2, hh * P:(hh + 1) * P].unsqueeze(1).broadcast_to((P, NBLK, P)), ALU.add))
                        side.freed(("sg", hh), dve.tensor_tensor(
                            tmp[:, SEQ:NTOK].rearrange("p (b t) -> p b t", b=DB), T[:, 1, 0:NS].rearrange("p (b t) -> p b t", b=DB),
                            pars[:, 2, hh * P:hh * P + DT].unsqueeze(1).broadcast_to((P, DB, DT)), ALU.add))
                    if u == 9:
                        for key in ("vt0", "vt1", "vt2"):
                            side.wait_read(key)
                        for b in range(5):
                            r = P if b < NBLK else NS
                            own.mark(dve.bn_stats(stats[0:r, b, :], vn[0:r, b, :]))
                        own.settle()
                        apart(dve)
                        for b in range(5):
                            r = P if b < NBLK else NS
                            ins = dve.bn_aggr(mv[0:r, b, :], stats[0:r, b, :])
                        ins.then_inc(var_ready, 1)
                    if u == 10:
                        dve.wait_ge(std_ready, l + 1)
                        own.mark(dve.reciprocal(rstd[:, 0:4], rstd[:, 0:4]))
                        own.mark(dve.reciprocal(rstd[0:NS, 4:5], rstd[0:NS, 4:5]))
                        own.settle()
                        for b in range(5):
                            r = P if b < NBLK else NS
                            ins = dve.tensor_scalar(vn[0:r, b, :], vn[0:r, b, :], mv[0:r, b, 0:1], rstd[0:r, b:b + 1], ALU.subtract, ALU.mult)
                        ins.then_inc(ln_mid, 1)
                    if u < 15:
                        if (u + 1) % NBLK == 0:
                            stage_k((u + 1) // NBLK)
                        stage_q(u + 1)
                    if n < VS0:
                        if u >= 2:
                            dve.wait_ge(ext_ready, l * 4 + u - 1)
                        z_out(n, n % 2, zr[:, n % 2, :])
                    elif n < U0:
                        if n == VS0:
                            side.wait_full("spv")
                        z_out(n, n % 2, mix[:, 12 + n - VS0, :])
                    elif n < GB0:
                        if n == U0:
                            side.wait_full("vt2")
                            side.wait_full("vt1")
                        z_out(n, n % 2, mix[:, 12 + n - U0, :])
                    else:
                        if n == GB0:
                            dve.wait_ge(ext_ready, l * 4 + 4)
                        z_out(n, n % 2, zr[:, n % 2, :])
                probs_lo(15)
                dve.wait_ge(sg_out, l * 4 + 4)
                apart(dve)
                with dve.Fori(0, (GA0 - GC0) // 2) as i:
                    for j in range(2):
                        n = GC0 + i * 2 + j
                        split(n, 1)
                        gate(n - 1, tile_at(n - 17))
                        split(n + 1, 0)
                        z_out(n, j, zr[:, j, :])
                side.wait_read(("pv", 15))
                split(GA0, 1)
                gate(GA0 - 1, mix[:, 15, :])
                split(GA0 + 1, 0)
                z_out(GA0, 0, zr[:, 0, :])
                with dve.Fori(0, 3) as i:
                    for j in range(2):
                        n = GA0 + 1 + i * 2 + j
                        split(n, 1)
                        gate(n - 1, tile_at(i * 2 + j))
                        split(n + 1, 0)
                        z_out(n, 1 - j, zr[:, 1 - j, :])
                n = OUT0 - 1
                split(n, 1)
                gate(n - 1, mix[:, 6, :])
                split(n + 1, 0)
                z_out(n, 1, zr[:, 1, :])
                gate(n, mix[:, 7, :])
                for i, k in enumerate(OUT_ORDER):
                    dve.wait_ge(h_hi_ready, (l * 2 + 1) * KT + i + 1)
                    dve.scalar_tensor_tensor(h_lo[:, k, :], mix[:, k, :], 0.5, h_hi[:, k, :].bitcast(F32), ALU.mult,
                                             ALU.subtract).then_inc(h_ready, 1)
                    if i == HK - 1:
                        split(OUT0, 1)

                def y_out(n, j, dst):
                    dve.wait_ge(z_ready, l * NB + n + 2)
                    dve.tensor_copy(two(dst), zcols(Z[j])).then_inc(z_free, 1)

                for n in (OUT0, OUT0 + 1):
                    if n > OUT0:
                        split(n, 1)
                    split(n + 1, 0)
                    y_out(n, n % 2, mix[:, n - OUT0, :])
                with dve.Fori(0, (N_OUT - 4) // 2) as i:
                    for j in range(2):
                        n = OUT0 + 2 + i * 2 + j
                        split(n, 1)
                        split(n + 1, 0)
                        y_out(n, j, tile_at(i * 2 + j + 2))
                split(NB - 2, 1)
                split(NB - 1, 0)
                y_out(NB - 2, 0, mix[:, KT - 2, :])
                split(NB - 1, 1)
                y_out(NB - 1, 1, mix[:, KT - 1, :])
                invert("ysum", 2)
                dve.wait_ge(park_in, 16 * (l + 1))
                dve.wait_ge(sq_ready, l * 32 + 32)
                for t in range(KT):
                    own.mark(dve.scalar_tensor_tensor(mix[:, t, :], mix[:, t, :], g_post[:, l, t:t + 1], rms[:, :], ALU.mult, ALU.mult))
                    own.settle()
                    dve.tensor_tensor(mix[:, t, :], mix[:, t, :], x_old[:, t, :], ALU.add).then_inc(x_ready, 1)
                assert own.n == DVE_OWN, own.n

        @block.gpsimd
        def _(pool):
            for src, dst in ((c_ident, ident), (c_band, band), (c_cos, cos), (c_sin, sin), (c_smask, smask), (c_sel, sel), (c_fix, fix)):
                pool.dma_start(dst[tuple([slice(None)] * len(dst.shape))], src).then_inc(const_in, 16)
            for i, g in enumerate((norm_pre, norm_post)):
                pool.dma_start(g_raw[:, i, :], g.rearrange("l (t p) -> (l t) p", p=P)).then_inc(g_in, 16)
            pool.memset(ones[:, :], 1.0).then_inc(ready0, 1)
            pool.memset(qbd[:, :, :, :], 0.0).then_inc(ready0, 1)
            pool.memset(w4[:, :, :], 0.0).then_inc(ready0, 1)
            pool.memset(eps[:, :], EPS).then_inc(ready0, 1)
            pool.memset(zeros[:, :], 0.0).then_inc(ready0, 1)
            pool.memset(junk[:, 0:1], 0.0).then_inc(w_split, 2)
            pool.memset(junk[:, 1:2], 0.0).then_inc(z_free, 2)
            for i, start in enumerate((z_ready, w_half_used, s_free, t_free)):
                pool.memset(junk[:, 2 + i:3 + i], 0.0).then_inc(start, 1)
            pool.dma_start(nk_s[:, :, 0:P - DT], cache_k[:, :, DT:P]).then_inc(copy_out, 16)
            pool.dma_start(nv_s[:, :, 0:P - DT], cache_v[:, :, DT:P]).then_inc(copy_out, 16)
            pool.dma_start(npool_s[:, :, 0:HIST - DT], state_pool[:, :, DT:HIST]).then_inc(copy_out, 16)
            with pool.Fori(0, DEPTH) as l:
                own = Own(pool, own_p, POOL_OWN)
                own.layer = l
                side = Sides(pool, l)

                def add_square(i, phase, j):
                    pool.wait_ge(sq_ready, l * 32 + phase * 16 + i + 1)
                    if not isinstance(i, int) or i > 1:
                        pool.wait_ge(acc_done, l * 30 + phase * 15 + i - 1)
                    pool.tensor_tensor(acc[:, :], acc[:, :], sq[:, j, :], ALU.add).then_inc(acc_done, 1)

                def normalise(u):
                    w = P * min(u % NBLK + 1, 2)
                    pool.wait_ge(den_ready, l * 16 + u + 1)
                    apart(pool)
                    for hh in range(GROUP):
                        ins = pool.tensor_scalar(prob[:, hh, 0:w], prob[:, hh, 0:w], sm[:, u % 2, 5, hh:hh + 1], 1.0, ALU.mult, ALU.mult)
                    ins.then_inc(norm_ready, 1)

                def pool_windows(g):
                    pool.wait_ge(ext_ready, l * 4 + g + 1)
                    src, shift = ext_a, 1
                    for i in range(g + 1):
                        dst = (ext_b, ext_c)[i % 2]
                        own.mark(pool.tensor_tensor(dst[:, HIST:EXT], src[:, HIST:EXT], src[:, HIST - shift:EXT - shift], ALU.add)
                                 if g == i else
                                 pool.tensor_tensor(dst[:, 2 * shift - 1:EXT], src[:, 2 * shift - 1:EXT], src[:, shift - 1:EXT - shift], ALU.add))
                        own.settle()
                        src, shift = dst, 2 * shift
                    own.mark(pool.tensor_tensor(src[:, HIST:HIST + 16], src[:, HIST:HIST + 16], fix[:, g, :], ALU.mult))
                    own.settle()
                    if g == 0:
                        pool.wait_ge(kv_out, 64 * (l + 1))
                    tail = [x[:, HIST + SEQ:EXT].rearrange("p (b n) -> p b n", b=DB)[:, :, HIST:SEXT] for x in (src, ext_a)]
                    apart(pool)
                    own.mark(pool.tensor_scalar(src[:, HIST:EXT], src[:, HIST:EXT], 1.0 / POOLW[g], 0.0, ALU.mult, ALU.add))
                    own.settle()
                    pool.tensor_tensor(mix[:, 8 + g, 0:SEQ], src[:, HIST:HIST + SEQ], ext_a[:, HIST:HIST + SEQ], ALU.subtract)
                    pool.tensor_tensor(mix[:, 8 + g, SEQ:NTOK].rearrange("p (b t) -> p b t", b=DB), tail[0], tail[1],
                                       ALU.subtract).then_inc(pooled_ready, 1)

                def gate(n, j, tile):
                    pool.wait_ge(z_free, l * NB + n + 3)
                    pool.tensor_tensor(tile, tile, zr[:, j, :], ALU.mult).then_inc(gate_t, 1)

                def tile_at(t):
                    return mix[:, bass.ds(t, 1), :].rearrange("p a n -> p (a n)")

                for t in range(1, KT):
                    add_square(t, 0, t % 2)
                pool.wait_ge(x_ready, KT * (l + 1))
                apart(pool)
                pool.dma_start(x_park, mix[:, :, :].rearrange("p t n -> p (t n)")).then_inc(park_out, 16)
                pool.dma_start(sgw_raw, sgu_w[l].rearrange("h t s -> t h s")).then_inc(raw_in, 16)
                pool.dma_start(st_raw, state_pool[l].rearrange("b n c -> (b n) c")).then_inc(raw_in, 16)
                pool.wait_ge(park_out, 16 * (l + 1))
                pool.wait_ge(h_ready, l * 2 * KT + KT)
                apart(pool)
                pool.dma_start(cache, cache_k[l].rearrange("b n h d -> n b (h d)")).then_inc(kc_in, 16)
                pool.dma_start(pscale[:, :], pool_scale[l].rearrange("(g p) -> p g", p=P)).then_inc(par_in, 16)
                pool.dma_start(sink[:, :], sinks[l].partition_broadcast(P)).then_inc(par_in, 16)
                pool.dma_start(poolw[:, :, :], pool_w[l].rearrange("g c d -> c g d")).then_inc(par_in, 16)
                side.wait_full("kc0")
                side.wait_full("kc1")
                apart(pool)
                pool.dma_start(cache, cache_v[l].rearrange("b n h d -> n b (h d)")).then_inc(vc_in, 16)
                side.wait_read("v")
                apart(pool)
                pool.dma_start(nv_p[l, 0].rearrange("n h d -> n (h d)"), v_tok[:, NBLK - 1, :]).then_inc(kv_out, 16)
                side.wait_read("kvtail")
                apart(pool)
                pool.dma_start(nk_p[l, 0].rearrange("n h d -> n (h d)"), k_tail).then_inc(kv_out, 16)
                for dst, src in ((nk_s, k_new), (nv_s, v_new[:, :])):
                    pool.dma_start(dst[l, :, P - DT:P].rearrange("b t h d -> b t (h d)"), src).then_inc(kv_out, 16)
                side.wait_read("wm")
                apart(pool)
                pool.affine_select(out=wmt[:, :, :], in_=wmt[:, :, :], compare_op=ALU.is_ge, fill=0.0, base=0,
                                   pattern=[[0, 4], [1, P]], channel_multiplier=-1).then_inc(wm_masked, 1)
                pool.wait_ge(wm_masked, l + 1)
                apart(pool)
                for b in range(DB):
                    pool.dma_start(w4[b * DT:(b + 1) * DT, :, b * DT:(b + 1) * DT], wmt[0:DT, :, 0:DT]).then_inc(w4_in, 16)
                for u in range(16):
                    if 2 <= u <= 5:
                        pool_windows(u - 2)
                    if u == 6:
                        pool.wait_ge(pooled_ready, l * 4 + 4)
                        apart(pool)
                        for i, src in enumerate((ln_g[l], ln_b[l], sgu_b[l].rearrange("h t -> (h t)"))):
                            pool.dma_start(pars[:, i, :], src.partition_broadcast(P)).then_inc(lnp_in, 16)
                    if u == 8:
                        side.wait_read("xbo")
                        apart(pool)
                        pool.dma_start(npool_p[l, 0], xbo[0:HIST, :]).then_inc(xb_out, 16)
                        pool.dma_start(npool_s[l, :, HIST - DT:HIST], xbo[HIST:HIST + NS, :]).then_inc(xb_out, 16)
                    if u == 11:
                        pool.wait_ge(ln_mid, l + 1)
                        pool.wait_ge(lnp_in, 48 * (l + 1))
                        for i, op in enumerate((ALU.mult, ALU.add)):
                            own.mark(pool.tensor_tensor(vn[:, 0:4, :], vn[:, 0:4, :], pars[:, i, :].unsqueeze(1).broadcast_to((P, 4, SEQ)), op))
                            ins = pool.tensor_tensor(vn[0:NS, 4, :], vn[0:NS, 4, :], pars[0:NS, i, :], op)
                            if i == 0:
                                own.mark(ins)
                                own.settle()
                            else:
                                ins.then_inc(vn_ready, 1)
                        pool.wait_ge(vn_ready, l + 1)
                        apart(pool)
                        pool.dma_start(nchunk_s[l].rearrange("b t f -> (b t) f"), vn[0:NS, 4, :]).then_inc(vn_out, 16)
                    if u >= 13:
                        gate(XB0 + u - 1, (u - 1) % 2, mix[:, XB0 + u - 1 - 16, :])
                        hh = u - 13
                        side.wait_read(("sg", hh))
                        pool.tensor_tensor(mix[:, 12 + hh, :], mix[:, 12 + hh, :], tmp, ALU.mult).then_inc(sg_out, 1)
                    normalise(u)
                side.wait_read(("sg", 3))
                pool.tensor_tensor(mix[:, 15, :], mix[:, 15, :], tmp, ALU.mult).then_inc(sg_out, 1)
                with pool.Fori(0, (GA0 - GC0) // 2) as i:
                    for j in range(2):
                        gate(GC0 + i * 2 + j - 1, 1 - j, tile_at(i * 2 + j + 11))
                gate(GA0 - 1, 1, mix[:, 15, :])
                side.wait_read(("pv", 15))
                apart(pool)
                with pool.Fori(0, (OUT0 - GA0) // 2) as i:
                    for j in range(2):
                        gate(GA0 + i * 2 + j, j, tile_at(i * 2 + j))
                pool.wait_ge(gate_done, l * 16 + 16)
                pool.wait_ge(vn_out, 16 * (l + 1))
                pool.wait_ge(xb_out, 32 * (l + 1))
                pool.wait_ge(kv_out, 64 * (l + 1))
                apart(pool)
                pool.dma_start(arena[:, :], x_park).then_inc(park_in, 16)
                add_square(1, 1, 1)
                with pool.Fori(0, (N_OUT - 2) // 2) as i:
                    for j in range(2):
                        add_square(2 + i * 2 + j, 1, j)
                assert own.n == POOL_OWN, own.n
            for b in range(NBLK):
                pool.wait_ge(fin_act, 4 * b + 4)
                pool.dma_start(y_p[0, b * P:(b + 1) * P, :], stage[:, b, :]).then_inc(fin_out, 16)
            pool.wait_ge(fin_act, 4 * NBLK + 4)
            pool.dma_start(y_s.rearrange("b t f -> (b t) f"), stage_s).then_inc(fin_out, 16)
            pool.wait_ge(fin_out, 16 * (NBLK + 1))
            pool.wait_ge(kv_out, 64 * DEPTH)
            pool.wait_ge(xb_out, 32 * DEPTH)
            pool.wait_ge(vn_out, 16 * DEPTH)
            pool.wait_ge(park_out, 16 * DEPTH)
            pool.wait_ge(copy_out, 48)


def tables():
    r = np.arange(P)
    inv = (10000.0 ** (-np.arange(0, HD, 2) / HD)).astype(np.float32)
    pos = np.concatenate([np.arange(SEQ), np.tile(PAST + np.arange(DT), DB)]).astype(np.float32)
    ang = (inv[r % 32][:, None] * pos[None, :]).astype(np.float32)
    sign = np.where(r % HD < 32, 1.0, -1.0).astype(np.float32)[:, None]
    prev = np.where(r[None, :] > r[:, None], 0.0, NEG)
    same = np.where(r[None, :] <= r[:, None], 0.0, NEG)
    b, t = r // 32, r % DT
    smask = np.full((P, 2, P + NS), NEG, np.float32)
    for c in range(2):
        smask[:, c, 0:P] = np.where(r[None, :] > t[:, None], 0.0, NEG)
        nb, nt = np.arange(NS) // DT, np.arange(NS) % DT
        smask[:, c, P:] = np.where((nb[None, :] == (c * 4 + b)[:, None]) & (nt[None, :] <= t[:, None]), 0.0, NEG)
    sel = (((r % 32) // DT)[:, None] == np.arange(8)[None, :]).astype(np.float32)
    fix = np.stack([w / np.minimum(w, np.arange(16) + 1.0) for w in POOLW]).astype(np.float32)
    return {
        "c_cos": np.cos(ang), "c_sin": np.sin(ang) * sign, "c_band": np.concatenate([prev, same], 1).astype(np.float32),
        "c_smask": smask, "c_ident": np.eye(P, dtype=np.float32), "c_sel": sel, "c_fix": np.tile(fix[None], (P, 1, 1)),
    }


_INS = ["x_prompt", "x_sample", "cache_k", "cache_v", "state_pool", "w_in", "w_out", "norm_pre", "norm_post", "attn_sinks",
        "pool_w", "pool_scale", "sgu_ln_g", "sgu_ln_b", "sgu_w", "sgu_b"]
_OUTS = [(1, SEQ, D), (DB, DT, D), (DEPTH, 1, P, NKV, HD), (DEPTH, 1, P, NKV, HD), (DEPTH, 1, HIST, SEQ),
         (DEPTH, DB, P, NKV, HD), (DEPTH, DB, P, NKV, HD), (DEPTH, DB, HIST, SEQ), (DEPTH, DB, DT, SEQ)]


def kernel(**inputs):
    import concourse.bacc as _bacc
    from concourse.bass_utils import run_bass_kernel_spmd as _run

    nc = _bacc.Bacc("TRN2", target_bir_lowering=False, num_devices=1)
    arrays, args = {}, []
    for name, a in [(n, inputs[n]) for n in _INS] + list(tables().items()):
        a = np.ascontiguousarray(a)
        arrays[f"in_{name}_dram"] = a
        args.append(nc.dram_tensor(f"in_{name}_dram", a.shape, mybir.dt.from_np(a.dtype), kind="ExternalInput").ap())
    for i, shape in enumerate(_OUTS):
        args.append(nc.dram_tensor(f"out_{i}_dram", shape, F32, kind="ExternalOutput").ap())
    args.append(nc.dram_tensor("x_park", (P, KT * NTOK), F32, kind="Internal").ap())
    program(nc, *args)
    r = _run(nc, [arrays], core_ids=[0])
    return tuple(r.results[0][f"out_{i}_dram"] for i in range(len(_OUTS)))
```

```python
from contextlib import ExitStack, contextmanager

import numpy as np

import concourse.bass as bass
from concourse import mybir

F32 = mybir.dt.float32
F32R = mybir.dt.float32r
ALU = mybir.AluOpType
ACT = mybir.ActivationFunctionType
AX_X = mybir.AxisListType.X

P = 128
D = 2048
KT = D // P
DEPTH = 2
SEQ = 512
NBLK = SEQ // P
DB, DT = 8, 4
NS = DB * DT
NTOK = SEQ + NS
HALF = NTOK // 2
HD = 64
NH, NKV, GROUP = 16, 4, 4
SCALE = HD ** -0.5
POOLW = (2, 4, 8, 16)
HIST = 15
SEXT = HIST + DT
EXT = HIST + SEQ + DB * SEXT
PAST = 2048
EPS = 1e-6
NEG = -1.0e30

DIN = 5120
N_IN, N_OUT = DIN // P, D // P
NB = N_IN + N_OUT
KV0, Q0, XB0, VS0, U0, GB0, GC0, GA0, OUT0 = 0, 4, 12, 16, 20, 24, 28, 32, 40
COL = {KV0: 1024, Q0: 0, XB0: 2560, VS0: 4096, U0: 3584, GB0: 3072, GC0: 4608, GA0: 1536}
HK = KT // 2
OUT_ORDER = list(range(8, 16)) + list(range(0, 8))

SKEYS = ["kv2", "xsum", "kc1", "kvtail", "state"]
TKEYS = ["kv3", "kc0", "v", "wm"]
for _u in range(16):
    SKEYS.append(("sc", _u))
    if _u == 0:
        SKEYS.append("ssc")
    if _u:
        TKEYS.append(("pv", _u - 1))
    TKEYS += {2: ["spt"], 3: ["spv"], 4: [("pm", 0)], 5: [("pm", 1)], 6: [("pm", 2)], 7: [("pm", 3)],
              8: ["vt0", "vt2"], 9: ["xbo"], 12: [("sg", 0)], 13: [("sg", 1)], 14: [("sg", 2)], 15: [("sg", 3)]}.get(_u, [])
    if _u == 8:
        SKEYS.append("vt1")
    TKEYS.append(("tp", _u))
TKEYS += [("pv", 15), "ysum"]
S_TURN = {k: i for i, k in enumerate(SKEYS)}
T_TURN = {k: i for i, k in enumerate(TKEYS)}

DVE_OWN, POOL_OWN = 120, 21
ACC = 29
KVU = 2 * Q0
FIN_DVE = [t for t in range(KT) if t % 3 == 2]
PARAMS = 3
CONSTS = 6
MEMSETS = 5


def program(nc, x_p, x_s, cache_k, cache_v, state_pool, w_in, w_out, norm_pre, norm_post, sinks, pool_w, pool_scale,
            ln_g, ln_b, sgu_w, sgu_b, c_cos, c_sin, c_band, c_smask, c_ident, c_sel, c_fix,
            y_p, y_s, nk_p, nv_p, npool_p, nk_s, nv_s, npool_s, nchunk_s, x_park):
    with ExitStack() as ctx:
        ctx.enter_context(nc.allow_non_contiguous_dma(reason="small parameters, a few hundred words a layer"))

        def sb(name, shape, dt=F32):
            return ctx.enter_context(nc.sbuf_tensor(name, shape, dt))

        def sem(name):
            return ctx.enter_context(nc.semaphore(name))

        h_hi = sb("h_hi", [P, KT, NTOK], F32R)
        h_lo = sb("h_lo", [P, KT, NTOK], F32R)
        mix = sb("mix", [P, KT, NTOK])
        w_raw = sb("w_raw", [P, 2, HK, P])
        w_hi = sb("w_hi", [P, 2, HK, P], F32R)
        w_lo = sb("w_lo", [P, 2, HK, P], F32R)
        arena = sb("arena", [P, KT * NTOK])
        k_hi = sb("k_hi", [P, SEQ], F32R)
        k_lo = sb("k_lo", [P, SEQ], F32R)
        q_st = sb("q_st", [P, GROUP, P], F32R)
        pt_hi = sb("pt_hi", [P, 2, GROUP * P], F32R)
        pt_lo = sb("pt_lo", [P, 2, GROUP * P], F32R)
        v_hi = sb("v_hi", [P, 2, 2, HD], F32R)
        v_lo = sb("v_lo", [P, 2, 2, HD], F32R)
        cos = sb("cos", [P, NTOK])
        sin = sb("sin", [P, NTOK])
        band = sb("band", [P, 2 * P])
        smask = sb("smask", [P, 2, P + NS])
        ident = sb("ident", [P, P])
        ones = sb("ones", [P, P])
        rms = sb("rms", [P, NTOK])
        acc = sb("acc", [P, NTOK])
        pars = sb("pars", [P, 3, SEQ])
        wmt = sb("wmt", [P, 4, P])
        w4 = sb("w4", [NS, 4, NS])
        poolw = sb("poolw", [P, 4, P])
        qbd = sb("qbd", [P, 2, DB, 32])
        stt = sb("stt", [P, 4, DB * HIST])
        g_pre = sb("g_pre", [P, (DEPTH + 1) * KT])
        g_post = sb("g_post", [P, DEPTH * KT])
        pscale = sb("pscale", [P, 4])
        sink = sb("sink", [P, NH])
        sel = sb("sel", [P, 8])
        fix = sb("fix", [P, 4, 16])
        v_new = sb("v_new", [NS, 4 * HD])
        xbo = sb("xbo", [HIST + NS, SEQ])
        xb_keep = sb("xb_keep", [P, 4, HIST + NS])
        eps = sb("eps", [P, 1])
        eps2 = sb("eps2", [P, 1])
        zeros = sb("zeros", [P, HIST])
        junk = sb("junk", [P, 6])
        sm = sb("sm", [P, 2, 6, GROUP])
        sms = sb("sms", [P, 8, 4])
        ssel = sb("ssel", [P, 2, 8])
        ssink = sb("ssink", [P, 2])
        es = sb("es", [P, GROUP])
        ess = sb("ess", [P, 4])
        stats = sb("stats", [P, 5, 6])
        mv = sb("mv", [P, 5, 2])
        rstd = sb("rstd", [P, 5])

        at = [0]

        def part(n):
            at[0] += n
            assert at[0] <= KT * NTOK
            return arena[:, at[0] - n:at[0]]

        zr = part(2 * NTOK).rearrange("p (a n) -> p a n", a=2)
        krot = part(2 * NTOK).rearrange("p (a n) -> p a n", a=2)
        v_tok = part(NBLK * 4 * HD).rearrange("p (b f) -> p b f", b=NBLK)
        prob = part(GROUP * 2 * P).rearrange("p (h k) -> p h k", h=GROUP)
        late = part(2 * DB * (P + NS))
        kct = late.rearrange("p (a b k) -> p a b k", a=2, b=DB)
        ps = late[:, 0:4 * (P + NS)].rearrange("p (a k) -> p a k", a=4)
        pst = late[:, 4 * (P + NS):4 * (P + NS) + 1024].rearrange("p (a k) -> p a k", a=2)
        vn = late.rearrange("p (b f) -> p b f", b=5)
        ext_a = part(EXT)
        ext_b = part(EXT)
        th = part(NTOK)
        ext_c = pars[:, :, :].rearrange("p a n -> p (a n)")[:, 0:EXT]
        sq = pars[:, :, :].rearrange("p a n -> p (a n)")[:, 0:2 * NTOK].rearrange("p (a n) -> p a n", a=2)
        tmp = ext_a[:, 0:NTOK]
        x_old = arena[:, :].rearrange("p (t n) -> p t n", t=KT)
        stage = arena[:, 0:NBLK * D].rearrange("p (b f) -> p b f", b=NBLK)
        g_raw = arena[0:DEPTH * KT, NBLK * D:NBLK * D + 2 * P].rearrange("p (a n) -> p a n", a=2)
        stage_s = mix[0:NS, 12:16, :].rearrange("p a n -> p (a n)")[:, 0:D]
        stage_y = [(w_raw[:, :, :, :].rearrange("p a b c -> p (a b c)") if q == 0 else
                    arena[:, (q - 1) * 4 * NTOK:(q - 1) * 4 * NTOK + D]).rearrange("p (b f) -> p b f", b=NBLK) for q in range(4)]
        stage_ys = [pars[0:NS, q, :] if q < 3 else acc[0:NS, 0:SEQ] for q in range(4)]
        cache = mix[:, 12:16, :].rearrange("p a n -> p (a n)")[:, 0:DB * 4 * HD].rearrange("p (b f) -> p b f", b=DB)
        outs = mix[:, 8:10, :].rearrange("p a n -> p (a n)")
        k_tail, k_new = outs[:, 0:256], outs[0:NS, 256:512]
        sgw_raw = prob[:, 0:2, :].rearrange("p h k -> p (h k)").rearrange("p (h s) -> p h s", h=4)
        st_raw = prob[0:DB * HIST, 2:4, :].rearrange("p h k -> p (h k)")

        Z = [ctx.enter_context(nc.psum_tensor(f"z{j}", [P, 2, 512], F32)) for j in range(2)]
        S = ctx.enter_context(nc.psum_tensor("side_s", [P, 2, 512], F32))
        T = ctx.enter_context(nc.psum_tensor("side_t", [P, 2, 512], F32))

        ident_in, const_in, x_in, g_in, w4_in, par_in, lnp_in, raw_in, kc_in, vc_in, park_in = (sem(n) for n in (
            "ident_in", "const_in", "x_in", "g_in", "w4_in", "par_in", "lnp_in", "raw_in", "kc_in", "vc_in", "park_in"))
        x_quarter_in = [sem(f"x_quarter_in{q}") for q in range(4)]
        w_landed = [sem("w_landed0"), sem("w_landed1")]
        park_out, kv_out, xb_out, vn_out, fin_out, copy_out = (sem(n) for n in (
            "park_out", "kv_out", "xb_out", "vn_out", "fin_out", "copy_out"))
        ready0, g_full, g_ready, xt_full, xt_act = (sem(n) for n in ("ready0", "g_full", "g_ready", "xt_full", "xt_act"))
        x_ready = sem("x_ready")
        upd_ready = sem("upd_ready")
        fin_added = sem("fin_added")
        w_hi_ready = sem("w_hi_ready")
        w_split = sem("w_split")
        w_half_used = sem("w_half_used")
        z_ready = sem("z_ready")
        z_free = sem("z_free")
        h_hi_ready, h_ready = sem("h_hi_ready"), sem("h_ready")
        sq_ready, acc_done = sem("sq_ready"), sem("acc_done")
        s_full, s_free, t_full, t_free = sem("s_full"), sem("s_free"), sem("t_full"), sem("t_free")
        kv_rot, q_rot, kct_new = sem("kv_rot"), sem("q_rot"), sem("kct_new")
        v_ready = sem("v_ready")
        wm_masked, qbd_ready = sem("wm_masked"), sem("qbd_ready")
        khi_ready, klo_ready, qhi_ready, qlo_ready, vhi_ready, vlo_ready, pthi_ready = (sem(n) for n in (
            "khi_ready", "klo_ready", "qhi_ready", "qlo_ready", "vhi_ready", "vlo_ready", "pthi_ready"))
        max_ready, exp_ready, den_ready, norm_ready, smax_ready, sexp_ready, sprob_ready = (sem(n) for n in (
            "max_ready", "exp_ready", "den_ready", "norm_ready", "smax_ready", "sexp_ready", "sprob_ready"))
        ext_ready, pooled_ready = sem("ext_ready"), sem("pooled_ready")
        var_ready, std_ready, ln_mid, vn_ready, sg_out = (sem(n) for n in ("var_ready", "std_ready", "ln_mid", "vn_ready", "sg_out"))
        gate_th, gate_t, gate_done = sem("gate_th"), sem("gate_t"), sem("gate_done")
        fin_full, fin_act = sem("fin_full"), sem("fin_act")
        own_v, own_p = sem("own_v"), sem("own_p")

        block = ctx.enter_context(nc.Block())

        def apart(eng):
            eng.nop(nofuse=True)

        class Own:

            def __init__(self, eng, s, per_layer):
                self.eng, self.s, self.per, self.n, self.extra, self.layer = eng, s, per_layer, 0, 0, None

            def mark(self, ins):
                ins.then_inc(self.s, 1)
                self.n += 1

            def settle(self):
                self.eng.wait_ge(self.s, self.layer * self.per + self.extra + self.n)

            @contextmanager
            def repeat(self, times, per_pass):
                first = self.n
                with self.eng.Fori(0, times) as i:
                    self.extra = i * per_pass
                    yield i
                assert self.n - first == per_pass, (self.n - first, per_pass)
                self.extra, self.n = 0, first + times * per_pass

        def two(ap):
            return ap.rearrange("p (c n) -> p c n", c=2)

        def zcols(z):
            return z[:, :, 0:HALF]

        class Sides:

            def __init__(self, eng, layer):
                self.eng, self.layer = eng, layer

            def _(self, key):
                if key in S_TURN:
                    return s_full, s_free, self.layer * len(SKEYS) + S_TURN[key]
                return t_full, t_free, self.layer * len(TKEYS) + T_TURN[key]

            def wait_free(self, key):
                _, free, turn = self._(key)
                self.eng.wait_ge(free, turn + 1)

            def wait_full(self, key):
                full, _, turn = self._(key)
                self.eng.wait_ge(full, turn + 1)

            def wait_read(self, key):
                _, free, turn = self._(key)
                self.eng.wait_ge(free, turn + 2)

            def filled(self, key, ins):
                ins.then_inc(self._(key)[0], 1)

            def freed(self, key, ins):
                ins.then_inc(self._(key)[1], 1)

        @block.sync
        def _(sp):
            for q in range(4):
                c = slice(q * SEQ, (q + 1) * SEQ)
                sp.dma_start(stage[:, :, c], x_p[:, :, c].rearrange("a (b p) f -> p (a b) f", p=P)).then_inc(x_quarter_in[q], 16)
                if q == 0:
                    sp.dma_start(stage_s, x_s.rearrange("b t f -> (b t) f")).then_inc(x_in, 16)
            with sp.Fori(0, DEPTH) as l:
                def load_in(n, col):
                    for h in range(2):
                        sp.wait_ge(w_split, l * (2 * NB) + n * 2 + h + 1)
                        apart(sp)
                        sp.dma_start(w_raw[:, h, :, :],
                                     w_in[l, h * HK * P:(h + 1) * HK * P, bass.ds(col, P)].rearrange("(k p) c -> p k c", p=P)
                                     ).then_inc(w_landed[h], 16)

                def load_out(n, col):
                    for h in range(2):
                        r0 = OUT_ORDER[h * HK] * P
                        sp.wait_ge(w_split, l * (2 * NB) + n * 2 + h + 1)
                        apart(sp)
                        sp.dma_start(w_raw[:, h, :, :],
                                     w_out[l, r0:r0 + HK * P, bass.ds(col, P)].rearrange("(k p) c -> p k c", p=P)
                                     ).then_inc(w_landed[h], 16)

                with sp.Fori(0, KVU // 2) as i:
                    for h in range(2):
                        sp.wait_ge(w_split, l * (2 * NB) + i * 2 + h + 1)
                        apart(sp)
                        sp.dma_start(w_raw[:, h, :, :].rearrange("p a c -> p (a c)").rearrange("p (k c) -> p k c", k=2),
                                     w_in[l, bass.ds((i * 2 + h) * (2 * P), 2 * P), COL[KV0]:COL[KV0] + 4 * P].rearrange("(k p) c -> p k c", p=P)
                                     ).then_inc(w_landed[h], 16)
                starts = [Q0, XB0, VS0, U0, GB0, GC0, GA0, OUT0]
                for a, b in zip(starts[:-1], starts[1:]):
                    with sp.Fori(0, b - a) as i:
                        load_in(a + i, COL[a] + i * P)
                with sp.Fori(0, N_OUT) as i:
                    load_out(OUT0 + i, i * P)
            for q in range(4):
                c = slice(q * SEQ, (q + 1) * SEQ)
                sp.wait_ge(fin_act, 4 * q + 4)
                sp.dma_start(y_p[:, :, c].rearrange("a (b p) f -> p (a b) f", p=P), stage_y[q]).then_inc(fin_out, 16)
                sp.dma_start(y_s[:, :, c].rearrange("b t f -> (b t) f"), stage_ys[q]).then_inc(fin_out, 16)
            sp.wait_ge(fin_out, 16 * 8)

        @block.tensor
        def _(pe):
            pe.wait_ge(ident_in, 16)
            pe.wait_ge(ready0, MEMSETS)
            pairs = [Z[0], Z[1], S, T]
            pe.wait_ge(g_in, 32)
            for i in range(2):
                mm = pe.transpose(T[:, 0, i * DEPTH * KT:(i + 1) * DEPTH * KT], g_raw[:, i, :], ident[0:DEPTH * KT, 0:DEPTH * KT])
            mm.then_inc(g_full, 1)
            for t in range(KT):
                o = pairs[t % 4]
                if t % 4 == 0:
                    pe.wait_ge(x_quarter_in[t // 4], 16)
                if t == 0:
                    pe.wait_ge(x_in, 16)
                if t == 3:
                    pe.wait_ge(g_ready, 2)
                if t >= 4:
                    pe.wait_ge(x_ready, t - 3)
                for b in range(NBLK):
                    pe.transpose(o[:, 0, b * P:(b + 1) * P], stage[:, b, t * P:(t + 1) * P], ident[:, :])
                pe.transpose(o[:, 1, 0:NS], stage_s[:, t * P:(t + 1) * P], ident[0:NS, 0:NS]).then_inc(xt_full, 1)
            pe.wait_ge(x_ready, KT)

            with pe.Fori(0, DEPTH) as l:
                side = Sides(pe, l)

                def run(n, j, phase=0, first=False, mids=None, base=0):
                    mids = mids or {}
                    pe.wait_ge(z_free, l * NB + (Q0 if isinstance(n, int) and n == Q0 else n + 1))
                    for i in range(KT):
                        h, kk = divmod(i, HK)
                        if kk == 0:
                            pe.wait_ge(w_split, l * (2 * NB) + n * 2 + h + 3)
                        if first:
                            pe.wait_ge(h_ready, (l * 2 + phase) * KT + i + 1)
                        for w, x in ((w_hi, h_hi), (w_hi, h_lo), (w_lo, h_hi)):
                            for c in range(2):
                                mm = pe.matmul(Z[j][:, c, 0:HALF], w[:, h, kk, :], x[:, i, c * HALF:(c + 1) * HALF],
                                               start=(i == 0 and w is w_hi and x is h_hi), stop=(i == KT - 1 and w is w_lo))
                        if i == HK - 1:
                            mm.then_inc(w_half_used, 1)
                        if i == KT - 1:
                            mm.then_inc(z_ready, 1)
                        if i in mids:
                            mids[i]()

                def turn_many(key, moves):
                    side.wait_free(key)
                    apart(pe)
                    for o, i in moves:
                        mm = pe.transpose(o, i, ident[0:i.shape[0], 0:i.shape[0]])
                    side.filled(key, mm)

                def rms_sum(key, o, count):
                    pe.wait_ge(acc_done, l * ACC + count)
                    side.wait_free(key)
                    whole = key == "xsum"
                    for c in range(2):
                        mm = pe.matmul(o[:, c, 0:HALF], ones[:, :], acc[:, c * HALF:(c + 1) * HALF], start=True, stop=whole)
                    if not whole:
                        pe.wait_ge(sq_ready, l * 32 + 32)
                        for c in range(2):
                            mm = pe.matmul(o[:, c, 0:HALF], ones[:, :], sq[:, 1, c * HALF:(c + 1) * HALF], start=False, stop=True)
                    side.filled(key, mm)

                def scores(u):
                    g, b = divmod(u, NBLK)
                    side.wait_free(("sc", u))
                    pe.wait_ge(qlo_ready, l * 16 + u + 1)
                    if b == 0:
                        pe.wait_ge(klo_ready, l * 4 + g + 1)
                    k0 = max(b - 1, 0) * P
                    w = (b + 1) * P - k0
                    for hh in range(GROUP):
                        o = S[:, hh // 2, (hh % 2) * 2 * P:(hh % 2) * 2 * P + w]
                        for kk in (k_hi, k_lo):
                            mm = pe.matmul(o, q_st[:, hh, :], kk[:, k0:k0 + w], start=(kk is k_hi), stop=(kk is k_lo))
                    side.filled(("sc", u), mm)

                def turn_probs(u):
                    b = u % NBLK
                    pe.wait_ge(norm_ready, l * 16 + u + 1)
                    nk = 1 if b == 0 else 2
                    turn_many(("tp", u), [(T[:, kb, hh * P:(hh + 1) * P], prob[:, hh, kb * P:(kb + 1) * P])
                                          for kb in range(nk) for hh in range(GROUP)])

                def values(u):
                    b = u % NBLK
                    side.wait_read(("tp", u))
                    pe.wait_ge(vlo_ready, l * 16 + u + 1)
                    side.wait_free(("pv", u))
                    nk = 1 if b == 0 else 2
                    terms = [(v, p, kb) for kb in range(nk) for v, p in ((v_hi, pt_hi), (v_hi, pt_lo), (v_lo, pt_hi))]
                    for i, (v, p, kb) in enumerate(terms):
                        mm = pe.matmul(T[:, 0, :], v[:, kb, :, :], p[:, kb, :], start=(i == 0), stop=(i == len(terms) - 1))
                    side.filled(("pv", u), mm)

                def pool_mm(g):
                    pe.wait_ge(pooled_ready, l * 4 + g + 1)
                    side.wait_free(("pm", g))
                    for c in range(2):
                        mm = pe.matmul(T[:, c, 0:HALF], poolw[:, g, :], mix[:, 8 + g, c * HALF:(c + 1) * HALF], start=True, stop=True)
                    side.filled(("pm", g), mm)

                def turn_xb():
                    pe.wait_ge(ext_ready, l * 4 + 4)
                    turn_many("xbo", [(T[0:HIST + NS, 0, g * P:(g + 1) * P], xb_keep[:, g, :]) for g in range(4)])

                def turn_vs(key):
                    pe.wait_ge(z_free, l * NB + VS0 + 3 + 3)
                    if key == "vt2":
                        turn_many(key, [(T[0:NS, 0, t * P:(t + 1) * P], mix[:, 12 + t, SEQ:NTOK]) for t in range(4)])
                    else:
                        o, b0 = (T, 0) if key == "vt0" else (S, 2)
                        turn_many(key, [(o[:, b, t * P:(t + 1) * P], mix[:, 12 + t, (b0 + b) * P:(b0 + b + 1) * P])
                                        for b in range(2) for t in range(4)])

                def spatial(hh):
                    pe.wait_ge(vn_ready, l + 1)
                    pe.wait_ge(wm_masked, l + 1)
                    pe.wait_ge(w4_in, DB * 16 * (l + 1))
                    side.wait_free(("sg", hh))
                    for b in range(NBLK):
                        pe.matmul(T[:, 0, b * P:(b + 1) * P], vn[:, b, hh * P:(hh + 1) * P], wmt[:, hh, :], start=True, stop=True)
                    mm = pe.matmul(T[:, 1, 0:NS], vn[0:NS, 4, hh * P:(hh + 1) * P], w4[:, hh, :], start=True, stop=True)
                    side.filled(("sg", hh), mm)

                def sample_scores():
                    pe.wait_ge(qbd_ready, l * 16 + 16)
                    pe.wait_ge(kct_new, l * 2 + 2)
                    side.wait_read("kc0")
                    side.wait_read("kc1")
                    side.wait_free("ssc")
                    for b in range(DB):
                        r = (b % 4) * 32
                        for p in range(2):
                            mm = pe.matmul(S[r:r + 32, b // 4, p * (P + NS):(p + 1) * (P + NS)], qbd[:, p, b, :], kct[:, p, b, :],
                                           start=True, stop=True)
                    side.filled("ssc", mm)

                def sample_turn():
                    pe.wait_ge(sprob_ready, l + 1)
                    turn_many("spt", [(T[:, 0, q * P:(q + 1) * P], ps[:, q, 0:P]) for q in range(4)]
                              + [(T[0:NS, 1, q * P:(q + 1) * P], ps[:, q, P:P + NS]) for q in range(4)])

                def sample_values():
                    side.wait_read("spt")
                    pe.wait_ge(vc_in, 16 * (l + 1))
                    side.wait_free("spv")
                    new = pst[0:NS, 1, :].rearrange("p (c a r) -> p c a r", c=2, a=2)
                    for p in range(2):
                        pe.matmul(T[:, 0, p * 256:(p + 1) * 256].rearrange("p (c r) -> p c r", c=2), v_new[:, p * P:(p + 1) * P],
                                  new[:, :, p, :], start=True, stop=False)
                        for b in range(DB):
                            c0 = (b // 4) * 256 + p * P + (b % 4) * 32
                            mm = pe.matmul(T[:, 0, p * 256 + b * 32:p * 256 + (b + 1) * 32], cache[:, b, p * P:(p + 1) * P],
                                           pst[:, 0, c0:c0 + 32], start=False, stop=(b == DB - 1))
                    side.filled("spv", mm)

                pe.wait_ge(z_free, l * NB + 2)
                side.wait_free("kv2")
                side.wait_free("kv3")
                outs4 = (Z[0], Z[1], S, T)
                for m in range(KVU):
                    pe.wait_ge(w_split, l * (2 * NB) + m + 3)
                    for kk in range(2):
                        k = 2 * m + kk
                        pe.wait_ge(h_ready, l * (2 * KT) + k + 1)
                        last = k == KT - 1
                        for b in (2, 3, 0, 1):
                            for w, x in ((w_hi, h_hi), (w_hi, h_lo), (w_lo, h_hi)):
                                for c in range(2):
                                    mm = pe.matmul(outs4[b][:, c, 0:HALF], w[:, m % 2, kk * 4 + b, :], x[:, k, c * HALF:(c + 1) * HALF],
                                                   start=(k == 0 and w is w_hi and x is h_hi), stop=(last and w is w_lo))
                            if last and b >= 2:
                                side.filled("kv2" if b == 2 else "kv3", mm)
                    mm.then_inc(z_ready if m % 2 else w_half_used, 1)
                def cached(key, o, b0):
                    pe.wait_ge(kc_in, 16 * (l + 1))
                    turn_many(key, [(o[:, p, b * P:(b + 1) * P], cache[:, b0 + b, p * P:(p + 1) * P]) for p in range(2) for b in range(4)])

                def turn_v():
                    pe.wait_ge(v_ready, l * 2 + 2)
                    turn_many("v", [(T[:, t, b * P:(b + 1) * P], zr[:, t, b * P:(b + 1) * P]) for t in range(2) for b in range(NBLK)])

                def turn_wm():
                    pe.wait_ge(raw_in, 32 * (l + 1))
                    turn_many("wm", [(T[:, 0, h * P:(h + 1) * P], sgw_raw[:, h, :]) for h in range(4)])

                def turn_kv():
                    pe.wait_ge(kv_rot, l * 2 + 2)
                    turn_many("kvtail", [(S[:, 0, t * P:(t + 1) * P], krot[:, t, SEQ - P:SEQ]) for t in range(2)]
                              + [(S[0:NS, 1, t * P:(t + 1) * P], zr[:, t, SEQ:NTOK]) for t in range(2)]
                              + [(S[0:NS, 1, 256 + t * P:256 + (t + 1) * P], krot[:, t, SEQ:NTOK]) for t in range(2)])

                run(Q0, 0, mids={1: lambda: rms_sum("xsum", S, 15), 5: lambda: cached("kc0", T, 0), 9: lambda: cached("kc1", S, 4),
                                 14: turn_v})
                run(Q0 + 1, 1, mids={3: turn_wm, 9: turn_kv, 13: lambda: turn_many(
                    "state", [(S[:, 0, g * DB * HIST:(g + 1) * DB * HIST], st_raw[:, g * P:(g + 1) * P]) for g in range(4)])})
                with pe.Fori(1, (XB0 - Q0) // 2) as i:
                    for j in range(2):
                        run(Q0 + i * 2 + j, j)
                for u in range(16):
                    extra = {0: sample_scores, 2: sample_turn, 3: sample_values, 4: lambda: pool_mm(0), 5: lambda: pool_mm(1),
                             6: lambda: pool_mm(2), 7: lambda: pool_mm(3), 8: lambda: turn_vs("vt0"), 9: turn_xb, 12: lambda: spatial(0), 13: lambda: spatial(1),
                             14: lambda: spatial(2), 15: lambda: spatial(3)}
                    mids = {4: (lambda u=u: values(u - 1)) if u else (lambda: None)}
                    if u in extra:
                        mids[8] = extra[u]
                    if u == 8:
                        mids[11] = lambda: turn_vs("vt1")
                        mids[13] = lambda: turn_vs("vt2")
                    scores(u)
                    run(XB0 + u, u % 2, mids=mids)
                    turn_probs(u)
                run(GC0, 0, mids={4: lambda: values(15)})
                run(GC0 + 1, 1)
                with pe.Fori(1, (OUT0 - GC0) // 2) as i:
                    for j in range(2):
                        run(GC0 + i * 2 + j, j)
                for n in (OUT0, OUT0 + 1):
                    run(n, n % 2, phase=1, first=(n == OUT0))
                with pe.Fori(0, (N_OUT - 4) // 2) as i:
                    for j in range(2):
                        run(OUT0 + 2 + i * 2 + j, j, phase=1)
                for n in (NB - 2, NB - 1):
                    run(n, n % 2, phase=1)
                rms_sum("ysum", T, ACC)

            for t in range(KT):
                o = pairs[t % 4]
                by_dve = sum(i <= t for i in FIN_DVE)
                pe.wait_ge(x_ready, DEPTH * KT + t + 1 - by_dve)
                if by_dve:
                    pe.wait_ge(fin_added, by_dve)
                if t >= 4:
                    pe.wait_ge(fin_act, t - 3)
                for b in range(NBLK):
                    pe.transpose(o[:, 0, b * P:(b + 1) * P], mix[:, t, b * P:(b + 1) * P], ident[:, :])
                pe.transpose(o[0:NS, 1, 0:P], mix[:, t, SEQ:NTOK], ident[:, :]).then_inc(fin_full, 1)

        @block.scalar
        def _(act):
            for t in range(KT):
                act.wait_ge(xt_full, t + 1)
                act.activation(mix[:, t, 0:SEQ], [Z[0], Z[1], S, T][t % 4][:, 0, :], ACT.Copy).then_inc(xt_act, 1)
            act.wait_ge(ready0, MEMSETS)

            def split_of(l, n, h):
                act.wait_ge(w_landed[h], (l * NB + n + 1) * 16)
                act.wait_ge(z_ready if h else w_half_used, l * NB + n + 1)
                act.activation(w_hi[:, h, :, :], w_raw[:, h, :, :], ACT.Copy).then_inc(w_hi_ready, 1)

            def x_parts(l):
                for t in range(KT):
                    act.wait_ge(x_ready, l * KT + t + 1)
                    act.activation(h_hi[:, t, :], mix[:, t, :], ACT.Copy,
                                   scale=g_pre[:, t + KT * l:t + KT * l + 1] if isinstance(l, int) else g_pre[:, bass.ds(l * KT + t, 1)]
                                   ).then_inc(h_hi_ready, 1)
                    if t >= 3:
                        act.wait_ge(acc_done, l * ACC + t - 2)
                    act.activation(acc[:, :] if t == 0 else sq[:, t % 2, :], mix[:, t, :], ACT.Square).then_inc(sq_ready, 1)
                    if t == 0 and isinstance(l, int):
                        split_of(l, 0, 1)
                    if t and t % 3 == 0:
                        split_of(l, *divmod(t // 3 + 1, 2))

            split_of(0, 0, 0)
            x_parts(0)
            with act.Fori(0, DEPTH) as l:
                side = Sides(act, l)

                def split(n, h):
                    split_of(l, n, h)

                def z_read(n):
                    act.wait_ge(z_free, l * NB + n + 3)

                def root(key, o):
                    side.wait_full(key)
                    side.freed(key, act.activation(two(rms[:, :]), zcols(o), ACT.Sqrt, bias=eps[:, 0:1], scale=1.0 / D))

                def stage_k(g):
                    s, t = (g % 2) * HD, g // 2
                    if g == 0:
                        act.wait_ge(kv_rot, l * 2 + 2)
                    else:
                        side.wait_full(("sc", 4 * g - 1))
                    act.activation(k_hi[s:s + HD, :], krot[s:s + HD, t, 0:SEQ], ACT.Copy)
                    act.activation(k_hi[HD - s:2 * HD - s, :], krot[s:s + HD, t, 0:SEQ], ACT.Copy).then_inc(khi_ready, 1)

                def stage_q(u):
                    g, b = divmod(u, NBLK)
                    if u == 0:
                        act.wait_ge(q_rot, l * 8 + 2)
                    else:
                        side.wait_full(("sc", u - 1))
                    for s in range(2):
                        ins = act.activation(q_st[s * HD:(s + 1) * HD, s:GROUP:2, :],
                                             mix[s * HD:(s + 1) * HD, 2 * g:2 * g + 2, b * P:(b + 1) * P], ACT.Copy)
                    ins.then_inc(qhi_ready, 1)

                def stage_v(u):
                    g, b = divmod(u, NBLK)
                    if u == 0:
                        side.wait_read("v")
                    else:
                        side.wait_full(("pv", u - 1))
                    b0, nk = max(b - 1, 0), min(b + 1, 2)
                    act.activation(v_hi[:, 0:nk, :, :],
                                   v_tok[:, b0:b0 + nk, g * HD:(g + 1) * HD].unsqueeze(2).broadcast_to((P, nk, 2, HD)),
                                   ACT.Copy).then_inc(vhi_ready, 1)

                def probs_hi(u):
                    nk = min(u % NBLK + 1, 2)
                    side.wait_full(("tp", u))
                    act.activation(pt_hi[:, 0:nk, :], T[:, 0:nk, :], ACT.Copy).then_inc(pthi_ready, 1)

                def attended(u):
                    g, b = divmod(u, NBLK)
                    side.wait_full(("pv", u))
                    for s in range(2):
                        o = T[s * HD:(s + 1) * HD, 0, :].rearrange("p (i s q) -> p i s q", i=2, s=2)[:, :, s, :]
                        ins = act.activation(mix[s * HD:(s + 1) * HD, 2 * g:2 * g + 2, b * P:(b + 1) * P], o, ACT.Copy)
                    side.freed(("pv", u), ins)

                def exps(u):
                    w = P * min(u % NBLK + 1, 2)
                    act.wait_ge(max_ready, l * 16 + u + 1)
                    for hh in range(GROUP):
                        act.activation(prob[:, hh, 0:w], prob[:, hh, 0:w], ACT.Exp, bias=sm[:, u % 2, 2, hh:hh + 1], scale=SCALE,
                                       accum_out=sm[:, u % 2, 4, hh:hh + 1])
                    act.activation(es[:, :], sm[:, u % 2, 3, :], ACT.Exp).then_inc(exp_ready, 1)

                def sample_exps():
                    act.wait_ge(smax_ready, l + 1)
                    for q in range(4):
                        act.activation(ps[:, q, :], ps[:, q, :], ACT.Exp, bias=sms[:, 2, q:q + 1], scale=SCALE,
                                       accum_out=sms[:, 4, q:q + 1])
                    act.activation(ess[:, :], sms[:, 3, :], ACT.Exp).then_inc(sexp_ready, 1)

                def sample_probs_out():
                    side.wait_full("spt")
                    act.activation(pst[:, 0, :], T[:, 0, :], ACT.Copy)
                    side.freed("spt", act.activation(pst[0:NS, 1, :], T[0:NS, 1, :], ACT.Copy))

                def sample_attended():
                    side.wait_full("spv")
                    for p in range(2):
                        for kv in range(2):
                            for s in range(2):
                                t = 4 * p + 2 * kv
                                o = T[kv * HD:(kv + 1) * HD, 0, p * 256:(p + 1) * 256].rearrange(
                                    "p (b v i s t) -> p b v i s t", b=DB, v=2, i=2, s=2)
                                for i in range(2):
                                    ins = act.activation(
                                        mix[s * HD:(s + 1) * HD, t + i, SEQ:NTOK].rearrange("p (b t) -> p b t", b=DB),
                                        o[:, :, kv, i, s, :], ACT.Copy)
                    side.freed("spv", ins)

                def extend(g):
                    z_read(XB0 + g)
                    if g:
                        act.wait_ge(pooled_ready, l * 4 + g)
                    z = zr[:, g % 2, :]
                    tail = ext_a[:, HIST + SEQ:EXT].rearrange("p (b n) -> p b n", b=DB)
                    act.activation(ext_a[:, 0:HIST], zeros[:, :], ACT.Copy)
                    act.activation(ext_a[:, HIST:HIST + SEQ], z[:, 0:SEQ], ACT.Copy)
                    act.activation(tail[:, :, HIST:SEXT], z[:, SEQ:NTOK].rearrange("p (b t) -> p b t", b=DB), ACT.Copy)
                    act.activation(tail[:, :, 0:HIST], stt[:, g, :].rearrange("p (b t) -> p b t", b=DB), ACT.Copy)
                    act.activation(xb_keep[:, g, :], z[:, SEQ - HIST:NTOK], ACT.Copy).then_inc(ext_ready, 1)

                def tanh(n, j):
                    z_read(n)
                    if not isinstance(n, int) or n > GB0:
                        act.wait_ge(gate_done, l * 16 + n - GB0)
                    act.activation(th[:, :], zr[:, j, :], ACT.Tanh, scale=0.5).then_inc(gate_th, 1)

                split(Q0 - 1, 1)
                split(Q0, 0)
                for key, o, j in (("kv2", S, 0), ("kv3", T, 1)):
                    side.wait_full(key)
                    side.freed(key, act.activation(two(zr[:, j, :]), zcols(o), ACT.Copy))
                split(Q0, 1)
                root("xsum", S)

                def cached(key, o, b0):
                    side.wait_full(key)
                    side.freed(key, act.activation(kct[:, :, b0:b0 + 4, 0:P], o[:, :, :].rearrange("p a (b k) -> p a b k", b=4), ACT.Copy))

                cached("kc0", T, 0)
                split(Q0 + 1, 0)
                cached("kc1", S, 4)
                side.wait_full("v")
                side.freed("v", act.activation(v_tok.rearrange("p b (t f) -> p t b f", t=2),
                                               T[:, :, :].rearrange("p t (b f) -> p t b f", b=NBLK), ACT.Copy))
                split(Q0 + 1, 1)
                side.wait_full("wm")
                side.freed("wm", act.activation(wmt[:, :, :], T[:, 0, :].rearrange("p (h t) -> p h t", h=4), ACT.Copy))
                split(Q0 + 2, 0)
                side.wait_full("kvtail")
                act.wait_ge(park_out, 16 * (l + 1))
                act.activation(k_tail, S[:, 0, 0:256], ACT.Copy)
                act.activation(v_new[:, :], S[0:NS, 1, 0:256], ACT.Copy)
                side.freed("kvtail", act.activation(k_new, S[0:NS, 1, 256:512], ACT.Copy))
                side.wait_full("state")
                side.freed("state", act.activation(stt[:, :, :], S[:, 0, 0:4 * DB * HIST].rearrange("p (g n) -> p g n", g=4), ACT.Copy))
                with act.Fori(2, XB0 - Q0 - 2) as i:
                    split(Q0 + i, 1)
                    split(Q0 + 1 + i, 0)
                for n in (XB0 - 2, XB0 - 1):
                    split(n, 1)
                    split(n + 1, 0)
                    if n == XB0 - 2:
                        stage_k(0)
                    else:
                        stage_q(0)
                for u in range(16):
                    n = XB0 + u
                    if u:
                        probs_hi(u - 1)
                    split(n, 1)
                    if u:
                        attended(u - 1)
                    stage_v(u)
                    if n > GB0:
                        tanh(n - 1, (n - 1) % 2)
                    exps(u)
                    if u == 1:
                        sample_exps()
                    split(n + 1, 0)
                    if u < 15:
                        if (u + 1) % NBLK == 0:
                            stage_k((u + 1) // NBLK)
                        stage_q(u + 1)
                    if u == 2:
                        sample_probs_out()
                    if u == 3:
                        sample_attended()
                    if u == 9:
                        side.wait_full("xbo")
                        side.freed("xbo", act.activation(xbo[:, :], T[0:HIST + NS, 0, :], ACT.Copy))
                    if u == 8:
                        for key, o, b0 in (("vt0", T, 0), ("vt1", S, 2)):
                            side.wait_full(key)
                            side.freed(key, act.activation(vn[:, b0:b0 + 2, :], o[:, :, :], ACT.Copy))
                        side.wait_full("vt2")
                        side.freed("vt2", act.activation(vn[0:NS, 4, :], T[0:NS, 0, :], ACT.Copy))
                    if u == 9:
                        act.wait_ge(var_ready, l + 1)
                        act.activation(rstd[:, 0:4], mv[:, 0:4, 1], ACT.Sqrt, bias=eps[:, 0:1])
                        act.activation(rstd[0:NS, 4:5], mv[0:NS, 4:5, 1], ACT.Sqrt, bias=eps[0:NS, 0:1]).then_inc(std_ready, 1)
                    if 1 <= u <= 4:
                        extend(u - 1)
                probs_hi(15)
                for n in (GC0, GC0 + 1):
                    split(n, 1)
                    if n == GC0:
                        attended(15)
                    tanh(n - 1, (n - 1) % 2)
                    split(n + 1, 0)
                with act.Fori(1, (OUT0 - GC0) // 2) as i:
                    for j in range(2):
                        n = GC0 + i * 2 + j
                        split(n, 1)
                        tanh(n - 1, 1 - j)
                        split(n + 1, 0)
                act.wait_ge(w_half_used, l * NB + N_IN + 1)
                for i, k in enumerate(OUT_ORDER):
                    if i == HK:
                        split(OUT0, 1)
                        tanh(OUT0 - 1, 1)
                    act.wait_ge(gate_done, l * 16 + i + 1)
                    act.activation(h_hi[:, i, :], mix[:, k, :], ACT.Copy, scale=0.5).then_inc(h_hi_ready, 1)

                def y_square(n, j):
                    act.wait_ge(z_ready, l * NB + n + 2)
                    act.wait_ge(acc_done, l * ACC + 15 + n - OUT0 - 2)
                    act.activation(two(sq[:, j, :]), zcols(Z[j]), ACT.Square).then_inc(sq_ready, 1)

                split(OUT0 + 1, 0)
                act.wait_ge(z_ready, l * NB + OUT0 + 2)
                act.activation(two(acc[:, :]), zcols(Z[0]), ACT.Square).then_inc(sq_ready, 1)
                split(OUT0 + 1, 1)
                split(OUT0 + 2, 0)
                y_square(OUT0 + 1, 1)
                with act.Fori(0, (N_OUT - 4) // 2) as i:
                    for j in range(2):
                        n = OUT0 + 2 + i * 2 + j
                        split(n, 1)
                        split(n + 1, 0)
                        y_square(n, j)
                split(NB - 2, 1)
                split(NB - 1, 0)
                y_square(NB - 2, 0)
                split(NB - 1, 1)
                act.activation(eps2[:, :], eps[:, :], ACT.Sqrt)
                with act.If(l < DEPTH - 1):
                    split_of(l + 1, 0, 0)
                y_square(NB - 1, 1)
                root("ysum", T)
                with act.If(l < DEPTH - 1):
                    split_of(l + 1, 0, 1)
                    x_parts(l + 1)

            for t in range(KT):
                q, c = t // 4, t % 4 * P
                o = [Z[0], Z[1], S, T][t % 4]
                act.wait_ge(fin_full, t + 1)
                act.activation(stage_y[q][:, :, c:c + P], o[:, 0, :].rearrange("p (b f) -> p b f", b=NBLK), ACT.Copy)
                act.activation(stage_ys[q][:, c:c + P], o[0:NS, 1, 0:P], ACT.Copy).then_inc(fin_act, 1)

        @block.vector
        def _(dve):
            dve.wait_ge(g_full, 1)
            for i, g in enumerate((g_pre, g_post)):
                dve.tensor_copy(g[:, 0:DEPTH * KT], T[:, 0, i * DEPTH * KT:(i + 1) * DEPTH * KT]).then_inc(g_ready, 1)
            for t in range(KT):
                dve.wait_ge(xt_act, t + 1)
                dve.tensor_copy(mix[:, t, SEQ:NTOK], [Z[0], Z[1], S, T][t % 4][:, 1, 0:NS]).then_inc(x_ready, 1)

            def split_of(l, n, h):
                dve.wait_ge(w_hi_ready, l * (2 * NB) + n * 2 + h + 1)
                dve.tensor_tensor(w_lo[:, h, :, :], w_raw[:, h, :, :], w_hi[:, h, :, :].bitcast(F32), ALU.subtract).then_inc(w_split, 1)

            def normalise_y(t):
                dve.tensor_tensor(mix[:, t, :], mix[:, t, :], rms[:, :], ALU.mult).then_inc(upd_ready, 1)

            def x_parts(l):
                first = isinstance(l, int)
                split_of(l, 0, 0)
                if not first:
                    split_of(l, 0, 1)
                for step in range(KT + 2):
                    if step < KT and not first:
                        normalise_y(step)
                    t = step - 2
                    if t < 0:
                        continue
                    dve.wait_ge(h_hi_ready, l * (2 * KT) + t + 1)
                    dve.scalar_tensor_tensor(h_lo[:, t, :], mix[:, t, :], g_pre[:, t:t + 1] if first else g_pre[:, bass.ds(l * KT + t, 1)],
                                             h_hi[:, t, :].bitcast(F32), ALU.mult, ALU.subtract).then_inc(h_ready, 1)
                    if t == 0 and first:
                        split_of(l, 0, 1)
                    if t % 4 == 3:
                        dve.wait_ge(sq_ready, l * 32 + t + 1)
                        dve.wait_ge(acc_done, l * ACC + t - 1)
                        dve.tensor_tensor(acc[:, :], acc[:, :], sq[:, t % 2, :], ALU.add).then_inc(acc_done, 1)
                    if t and t % 3 == 0:
                        split_of(l, *divmod(t // 3 + 1, 2))

            x_parts(0)
            dve.wait_ge(const_in, 16 * CONSTS)
            with dve.Fori(0, DEPTH) as l:
                own = Own(dve, own_v, DVE_OWN)
                own.layer = l
                side = Sides(dve, l)

                def split(n, h):
                    split_of(l, n, h)

                def z_out(n, j, dst):
                    dve.wait_ge(z_ready, l * NB + n + 2)
                    dve.tensor_tensor(two(dst), zcols(Z[j]), two(rms[:, :]), ALU.mult).then_inc(z_free, 1)

                def rotate(n, j, dst, done):
                    z = zr[:, j, :]
                    z_out(n, j, z)
                    dve.wait_ge(z_free, l * NB + n + 3)
                    own.mark(dve.tensor_tensor(dst, z, cos[:, :], ALU.mult))
                    for q in range(4):
                        a, b = q * 32, (q ^ 1) * 32
                        own.mark(dve.tensor_tensor(th[a:a + 32, :], z[b:b + 32, :], sin[b:b + 32, :], ALU.mult))
                    own.settle()
                    dve.tensor_tensor(dst, dst, th[:, :], ALU.add).then_inc(done, 1)

                def invert(key):
                    side.wait_read(key)
                    own.mark(dve.reciprocal(rms[:, :], rms[:, :]))
                    own.settle()

                def rotate_k(t):
                    k = krot[:, t, :]
                    own.mark(dve.tensor_tensor(k, k, rms[:, :], ALU.mult))
                    own.settle()
                    for q in range(4):
                        a, b = q * 32, (q ^ 1) * 32
                        own.mark(dve.tensor_tensor(th[a:a + 32, :], k[b:b + 32, :], sin[b:b + 32, :], ALU.mult))
                    own.settle()
                    own.mark(dve.tensor_tensor(k, k, cos[:, :], ALU.mult))
                    own.settle()
                    dve.tensor_tensor(k, k, th[:, :], ALU.add).then_inc(kv_rot, 1)

                def stage_k(g):
                    s, t = (g % 2) * HD, g // 2
                    dve.wait_ge(khi_ready, l * 4 + g + 1)
                    for d in (s, HD - s):
                        ins = dve.tensor_tensor(k_lo[d:d + HD, :], krot[s:s + HD, t, 0:SEQ], k_hi[s:s + HD, :].bitcast(F32), ALU.subtract)
                    ins.then_inc(klo_ready, 1)

                def stage_q(u):
                    g, b = divmod(u, NBLK)
                    dve.wait_ge(qhi_ready, l * 16 + u + 1)
                    for s in range(2):
                        d = HD - s * HD
                        ins = dve.tensor_tensor(q_st[d:d + HD, s:GROUP:2, :], mix[s * HD:(s + 1) * HD, 2 * g:2 * g + 2, b * P:(b + 1) * P],
                                                q_st[s * HD:(s + 1) * HD, s:GROUP:2, :].bitcast(F32), ALU.subtract)
                    ins.then_inc(qlo_ready, 1)

                def stage_v(u):
                    g, b = divmod(u, NBLK)
                    b0, nk = max(b - 1, 0), min(b + 1, 2)
                    dve.wait_ge(vhi_ready, l * 16 + u + 1)
                    dve.tensor_tensor(v_lo[:, 0:nk, :, :],
                                      v_tok[:, b0:b0 + nk, g * HD:(g + 1) * HD].unsqueeze(2).broadcast_to((P, nk, 2, HD)),
                                      v_hi[:, 0:nk, :, :].bitcast(F32), ALU.subtract).then_inc(vlo_ready, 1)

                def probs_lo(u):
                    nk = min(u % NBLK + 1, 2)
                    dve.wait_ge(pthi_ready, l * 16 + u + 1)
                    side.freed(("tp", u), dve.tensor_tensor(pt_lo[:, 0:nk, :], T[:, 0:nk, :], pt_hi[:, 0:nk, :].bitcast(F32), ALU.subtract))

                def maxima(u):
                    b = u % NBLK
                    w = P * min(b + 1, 2)
                    mask = band[:, 2 * P - w:2 * P]
                    c = sm[:, u % 2, :, :]
                    side.wait_full(("sc", u))
                    apart(dve)
                    for hh in range(GROUP):
                        ins = dve.tensor_tensor_reduce(prob[:, hh, 0:w], S[:, hh // 2, (hh % 2) * 2 * P:(hh % 2) * 2 * P + w], mask,
                                                       1.0, NEG, ALU.add, ALU.max, c[:, 0, hh:hh + 1])
                    side.freed(("sc", u), ins)
                    side.wait_read(("sc", u))
                    own.mark(dve.scalar_tensor_tensor(c[:, 1, :], c[:, 0, :], SCALE, sink[:, 4 * (u // NBLK):4 * (u // NBLK) + 4],
                                                      ALU.mult, ALU.max))
                    own.settle()
                    own.mark(dve.tensor_scalar(c[:, 2, :], c[:, 1, :], -1.0, None, ALU.mult))
                    own.settle()
                    dve.tensor_tensor(c[:, 3, :], c[:, 2, :], sink[:, 4 * (u // NBLK):4 * (u // NBLK) + 4], ALU.add).then_inc(max_ready, 1)

                def denominators(u):
                    c = sm[:, u % 2, :, :]
                    dve.wait_ge(exp_ready, l * 16 + u + 1)
                    own.mark(dve.tensor_tensor(c[:, 1, :], c[:, 4, :], es[:, :], ALU.add))
                    own.settle()
                    dve.reciprocal(c[:, 5, :], c[:, 1, :]).then_inc(den_ready, 1)

                def sample_queries():
                    dve.wait_ge(q_rot, l * 8 + 8)
                    for p in range(2):
                        for kv in range(2):
                            for s in range(2):
                                for i in range(2):
                                    dve.tensor_copy(
                                        qbd[kv * HD:(kv + 1) * HD, p, :, :].rearrange("p b (v i s t) -> p b v i s t", v=2, i=2, s=2)[:, :, kv, i, s, :],
                                        mix[s * HD:(s + 1) * HD, 4 * p + 2 * kv + i, SEQ:NTOK].rearrange("p (b t) -> p b t", b=DB)
                                    ).then_inc(qbd_ready, 1)

                def sample_maxima():
                    side.wait_full("ssc")
                    side.freed("ssc", dve.tensor_tensor(
                        ps.rearrange("p (c a) k -> p c a k", c=2),
                        S[:, :, 0:2 * (P + NS)].rearrange("p c (a k) -> p c a k", a=2),
                        smask[:, :, :].unsqueeze(2).broadcast_to((P, 2, 2, P + NS)), ALU.add))
                    own.mark(dve.tensor_tensor(ssel[:, :, :], sink[:, :].rearrange("p (a e) -> p a e", a=2),
                                               sel[:, :].unsqueeze(1).broadcast_to((P, 2, 8)), ALU.mult))
                    own.settle()
                    own.mark(dve.tensor_reduce(ssink[:, :], ssel[:, :, :], AX_X, ALU.add))
                    side.wait_read("ssc")
                    own.mark(dve.tensor_reduce(sms[:, 0, :], ps, AX_X, ALU.max))
                    own.settle()
                    sk = ssink[:, :].unsqueeze(1).broadcast_to((P, 2, 2))

                    def col(i):
                        return sms[:, i, :].rearrange("p (c a) -> p c a", c=2)

                    own.mark(dve.scalar_tensor_tensor(col(1), col(0), SCALE, sk, ALU.mult, ALU.max))
                    own.settle()
                    own.mark(dve.tensor_scalar(sms[:, 2, :], sms[:, 1, :], -1.0, None, ALU.mult))
                    own.settle()
                    dve.tensor_tensor(col(3), col(2), sk, ALU.add).then_inc(smax_ready, 1)

                def sample_probs():
                    dve.wait_ge(sexp_ready, l + 1)
                    own.mark(dve.tensor_tensor(sms[:, 1, :], sms[:, 4, :], ess[:, :], ALU.add))
                    own.settle()
                    own.mark(dve.reciprocal(sms[:, 5, :], sms[:, 1, :]))
                    own.settle()
                    dve.tensor_tensor(ps, ps, sms[:, 5, :].unsqueeze(2).broadcast_to((P, 4, P + NS)), ALU.mult).then_inc(sprob_ready, 1)

                def gate(n, tile):
                    dve.wait_ge(gate_t, l * 16 + n - GB0 + 1)
                    dve.wait_ge(gate_th, l * 16 + n - GB0 + 1)
                    dve.scalar_tensor_tensor(tile, th[:, :], 1.0, tile, ALU.add, ALU.mult).then_inc(gate_done, 1)

                def tile_at(t):
                    return mix[:, bass.ds(t, 1), :].rearrange("p a n -> p (a n)")

                split(Q0 - 1, 1)
                split(Q0, 0)
                dve.wait_ge(z_ready, l * NB + Q0 + 1)
                for j in range(2):
                    ins = dve.tensor_copy(two(krot[:, j, :]), zcols(Z[j]))
                    ins.then_inc(z_free, 2)
                split(Q0, 1)
                invert("xsum")
                split(Q0 + 1, 0)
                side.wait_read("kv3")
                for t in range(2):
                    dve.tensor_tensor(zr[:, t, :], zr[:, t, :], rms[:, :], ALU.mult).then_inc(v_ready, 1)
                dve.wait_ge(z_free, l * NB + Q0 + 2)
                rotate_k(0)
                split(Q0 + 1, 1)
                rotate_k(1)
                split(Q0 + 2, 0)
                dve.wait_ge(kv_rot, l * 2 + 2)
                for p in range(2):
                    dve.tensor_copy(kct[:, p, :, P:P + NS], krot[:, p, SEQ:NTOK].unsqueeze(1).broadcast_to((P, DB, NS))).then_inc(kct_new, 1)
                side.wait_full("kvtail")
                dve.wait_ge(park_out, 16 * (l + 1))
                for n in (Q0, Q0 + 1):
                    rotate(n, n % 2, mix[:, n - Q0, :], q_rot)
                apart(dve)
                with own.repeat((XB0 - Q0) // 2 - 2, 10) as i:
                    for j in range(2):
                        n = Q0 + 2 + i * 2 + j
                        split(n, 1)
                        split(n + 1, 0)
                        rotate(n, j, tile_at(i * 2 + j + 2), q_rot)
                for n in (XB0 - 2, XB0 - 1):
                    split(n, 1)
                    split(n + 1, 0)
                    if n == XB0 - 2:
                        stage_k(0)
                    else:
                        stage_q(0)
                    rotate(n, n % 2, mix[:, n - Q0, :], q_rot)
                dve.wait_ge(par_in, PARAMS * 16 * (l + 1))
                for u in range(16):
                    n = XB0 + u
                    if u:
                        probs_lo(u - 1)
                    split(n, 1)
                    if u == 0:
                        sample_queries()
                    maxima(u)
                    stage_v(u)
                    if n > GB0:
                        gate(n - 1, mix[:, n - 1 - 16, :])
                    denominators(u)
                    if u == 1:
                        sample_probs()
                    split(n + 1, 0)
                    if u < 15:
                        if (u + 1) % NBLK == 0:
                            stage_k((u + 1) // NBLK)
                        stage_q(u + 1)
                    if u == 0:
                        sample_maxima()
                    if 4 <= u <= 7:
                        g = u - 4
                        side.wait_full(("pm", g))
                        side.freed(("pm", g), dve.tensor_scalar(two(mix[:, 8 + g, :]), zcols(T), pscale[:, g:g + 1], None, ALU.mult))
                    if u >= 12:
                        hh = u - 12
                        side.wait_full(("sg", hh))
                        if hh:
                            dve.wait_ge(sg_out, l * 4 + hh)
                        own.mark(dve.tensor_tensor(tmp[:, 0:SEQ].rearrange("p (b t) -> p b t", b=NBLK),
                                                   T[:, 0, :].rearrange("p (b t) -> p b t", b=NBLK),
                                                   pars[:, 2, hh * P:(hh + 1) * P].unsqueeze(1).broadcast_to((P, NBLK, P)), ALU.add))
                        side.freed(("sg", hh), dve.tensor_tensor(
                            tmp[:, SEQ:NTOK].rearrange("p (b t) -> p b t", b=DB), T[:, 1, 0:NS].rearrange("p (b t) -> p b t", b=DB),
                            pars[:, 2, hh * P:hh * P + DT].unsqueeze(1).broadcast_to((P, DB, DT)), ALU.add))
                    if u == 9:
                        for key in ("vt0", "vt1", "vt2"):
                            side.wait_read(key)
                        for b in range(5):
                            r = P if b < NBLK else NS
                            own.mark(dve.bn_stats(stats[0:r, b, :], vn[0:r, b, :]))
                        own.settle()
                        apart(dve)
                        for b in range(5):
                            r = P if b < NBLK else NS
                            ins = dve.bn_aggr(mv[0:r, b, :], stats[0:r, b, :])
                        ins.then_inc(var_ready, 1)
                    if u == 10:
                        dve.wait_ge(std_ready, l + 1)
                        own.mark(dve.reciprocal(rstd[:, 0:4], rstd[:, 0:4]))
                        own.mark(dve.reciprocal(rstd[0:NS, 4:5], rstd[0:NS, 4:5]))
                        own.settle()
                        for b in range(5):
                            r = P if b < NBLK else NS
                            ins = dve.tensor_scalar(vn[0:r, b, :], vn[0:r, b, :], mv[0:r, b, 0:1], rstd[0:r, b:b + 1], ALU.subtract, ALU.mult)
                        ins.then_inc(ln_mid, 1)
                    if n < VS0:
                        if u >= 2:
                            dve.wait_ge(ext_ready, l * 4 + u - 1)
                        z_out(n, n % 2, zr[:, n % 2, :])
                    elif n < U0:
                        if n == VS0:
                            side.wait_full("spv")
                        z_out(n, n % 2, mix[:, 12 + n - VS0, :])
                    elif n < GB0:
                        if n == U0:
                            side.wait_full("vt2")
                            side.wait_full("vt1")
                        z_out(n, n % 2, mix[:, 12 + n - U0, :])
                    else:
                        if n == GB0:
                            dve.wait_ge(ext_ready, l * 4 + 4)
                        z_out(n, n % 2, zr[:, n % 2, :])
                probs_lo(15)
                dve.wait_ge(sg_out, l * 4 + 4)
                apart(dve)
                with dve.Fori(0, (GA0 - GC0) // 2) as i:
                    for j in range(2):
                        n = GC0 + i * 2 + j
                        split(n, 1)
                        gate(n - 1, tile_at(n - 17))
                        split(n + 1, 0)
                        z_out(n, j, zr[:, j, :])
                side.wait_read(("pv", 15))
                split(GA0, 1)
                gate(GA0 - 1, mix[:, 15, :])
                split(GA0 + 1, 0)
                z_out(GA0, 0, zr[:, 0, :])
                with dve.Fori(0, 3) as i:
                    for j in range(2):
                        n = GA0 + 1 + i * 2 + j
                        split(n, 1)
                        gate(n - 1, tile_at(i * 2 + j))
                        split(n + 1, 0)
                        z_out(n, 1 - j, zr[:, 1 - j, :])
                n = OUT0 - 1
                split(n, 1)
                gate(n - 1, mix[:, 6, :])
                split(n + 1, 0)
                for i, k in enumerate(OUT_ORDER):
                    if i == HK:
                        z_out(n, 1, zr[:, 1, :])
                        split(OUT0, 1)
                        gate(n, mix[:, 7, :])
                    dve.wait_ge(h_hi_ready, (l * 2 + 1) * KT + i + 1)
                    dve.scalar_tensor_tensor(h_lo[:, i, :], mix[:, k, :], 0.5, h_hi[:, i, :].bitcast(F32), ALU.mult,
                                             ALU.subtract).then_inc(h_ready, 1)

                def y_out(n, j, dst):
                    dve.wait_ge(sq_ready, l * 32 + 16 + n - OUT0 + 1)
                    dve.tensor_scalar(two(dst), zcols(Z[j]), g_post[:, bass.ds(l * KT + n - OUT0, 1)], None, ALU.mult).then_inc(z_free, 1)

                for n in (OUT0, OUT0 + 1):
                    if n > OUT0:
                        split(n, 1)
                    split(n + 1, 0)
                    y_out(n, n % 2, mix[:, n - OUT0, :])
                with dve.Fori(0, (N_OUT - 4) // 2) as i:
                    for j in range(2):
                        n = OUT0 + 2 + i * 2 + j
                        split(n, 1)
                        split(n + 1, 0)
                        y_out(n, j, tile_at(i * 2 + j + 2))
                split(NB - 2, 1)
                split(NB - 1, 0)
                y_out(NB - 2, 0, mix[:, KT - 2, :])
                split(NB - 1, 1)
                y_out(NB - 1, 1, mix[:, KT - 1, :])
                invert("ysum")
                assert own.n == DVE_OWN, own.n
                dve.wait_ge(z_free, l * NB + NB + 2)
                apart(dve)
                with dve.If(l < DEPTH - 1):
                    x_parts(l + 1)

            dve.wait_ge(z_free, DEPTH * NB + 2)
            dve.wait_ge(park_in, 16 * DEPTH)
            for t in range(KT):
                normalise_y(t)
                if t in FIN_DVE:
                    dve.wait_ge(upd_ready, (DEPTH - 1) * KT + t + 1)
                    dve.tensor_tensor(mix[:, t, :], mix[:, t, :], x_old[:, t, :], ALU.add).then_inc(fin_added, 1)

        @block.gpsimd
        def _(pool):
            pool.dma_start(ident[:, :], c_ident).then_inc(ident_in, 16)
            for i, g in enumerate((norm_pre, norm_post)):
                pool.dma_start(g_raw[:, i, :], g.rearrange("l (t p) -> (l t) p", p=P)).then_inc(g_in, 16)
            pool.memset(ones[:, :], 1.0).then_inc(ready0, 1)
            pool.memset(qbd[:, :, :, :], 0.0).then_inc(ready0, 1)
            pool.memset(w4[:, :, :], 0.0).then_inc(ready0, 1)
            pool.memset(eps[:, :], EPS).then_inc(ready0, 1)
            pool.memset(zeros[:, :], 0.0).then_inc(ready0, 1)
            pool.memset(junk[:, 0:1], 0.0).then_inc(w_split, 2)
            pool.memset(junk[:, 1:2], 0.0).then_inc(z_free, 2)
            for i, start in enumerate((z_ready, w_half_used, s_free, t_free)):
                pool.memset(junk[:, 2 + i:3 + i], 0.0).then_inc(start, 1)
            for q in range(4):
                pool.wait_ge(x_quarter_in[q], 16)
            for src, dst in ((c_band, band), (c_cos, cos), (c_sin, sin), (c_smask, smask), (c_sel, sel), (c_fix, fix)):
                pool.dma_start(dst[tuple([slice(None)] * len(dst.shape))], src).then_inc(const_in, 16)
            pool.dma_start(nk_s[:, :, 0:P - DT], cache_k[:, :, DT:P]).then_inc(copy_out, 16)
            pool.dma_start(nv_s[:, :, 0:P - DT], cache_v[:, :, DT:P]).then_inc(copy_out, 16)
            pool.dma_start(npool_s[:, :, 0:HIST - DT], state_pool[:, :, DT:HIST]).then_inc(copy_out, 16)

            def add_square(l, i, phase, j):
                pool.wait_ge(sq_ready, l * 32 + phase * 16 + i + 1)
                if not isinstance(i, int) or i > 1:
                    pool.wait_ge(acc_done, l * ACC + phase * 15 + i - 1)
                pool.tensor_tensor(acc[:, :], acc[:, :], sq[:, j, :], ALU.add).then_inc(acc_done, 1)

            def residual(l, t):
                pool.wait_ge(upd_ready, (l - 1) * KT + t + 1)
                pool.tensor_tensor(mix[:, t, :], mix[:, t, :], x_old[:, t, :], ALU.add).then_inc(x_ready, 1)

            def x_parts(l):
                first = isinstance(l, int)
                for step in range(KT + 2):
                    if step < KT and not first:
                        residual(l, step)
                    t = step - 2
                    if t > 0 and t % 4 != 3:
                        add_square(l, t, 0, t % 2)

            x_parts(0)
            with pool.Fori(0, DEPTH) as l:
                own = Own(pool, own_p, POOL_OWN)
                own.layer = l
                side = Sides(pool, l)

                def normalise(u):
                    w = P * min(u % NBLK + 1, 2)
                    pool.wait_ge(den_ready, l * 16 + u + 1)
                    apart(pool)
                    for hh in range(GROUP):
                        ins = pool.tensor_scalar(prob[:, hh, 0:w], prob[:, hh, 0:w], sm[:, u % 2, 5, hh:hh + 1], 1.0, ALU.mult, ALU.mult)
                    ins.then_inc(norm_ready, 1)

                def pool_windows(g):
                    pool.wait_ge(ext_ready, l * 4 + g + 1)
                    src, shift = ext_a, 1
                    for i in range(g + 1):
                        dst = (ext_b, ext_c)[i % 2]
                        own.mark(pool.tensor_tensor(dst[:, HIST:EXT], src[:, HIST:EXT], src[:, HIST - shift:EXT - shift], ALU.add)
                                 if g == i else
                                 pool.tensor_tensor(dst[:, 2 * shift - 1:EXT], src[:, 2 * shift - 1:EXT], src[:, shift - 1:EXT - shift], ALU.add))
                        own.settle()
                        src, shift = dst, 2 * shift
                    own.mark(pool.tensor_tensor(src[:, HIST:HIST + 16], src[:, HIST:HIST + 16], fix[:, g, :], ALU.mult))
                    own.settle()
                    if g == 0:
                        pool.wait_ge(kv_out, 64 * (l + 1))
                    tail = [x[:, HIST + SEQ:EXT].rearrange("p (b n) -> p b n", b=DB)[:, :, HIST:SEXT] for x in (src, ext_a)]
                    apart(pool)
                    own.mark(pool.tensor_scalar(src[:, HIST:EXT], src[:, HIST:EXT], 1.0 / POOLW[g], 0.0, ALU.mult, ALU.add))
                    own.settle()
                    pool.tensor_tensor(mix[:, 8 + g, 0:SEQ], src[:, HIST:HIST + SEQ], ext_a[:, HIST:HIST + SEQ], ALU.subtract)
                    pool.tensor_tensor(mix[:, 8 + g, SEQ:NTOK].rearrange("p (b t) -> p b t", b=DB), tail[0], tail[1],
                                       ALU.subtract).then_inc(pooled_ready, 1)

                def gate(n, j, tile):
                    pool.wait_ge(z_free, l * NB + n + 3)
                    pool.tensor_tensor(tile, tile, zr[:, j, :], ALU.mult).then_inc(gate_t, 1)

                def tile_at(t):
                    return mix[:, bass.ds(t, 1), :].rearrange("p a n -> p (a n)")

                pool.wait_ge(x_ready, KT * (l + 1))
                apart(pool)
                pool.dma_start(x_park, mix[:, :, :].rearrange("p t n -> p (t n)")).then_inc(park_out, 16)
                pool.dma_start(sgw_raw, sgu_w[l].rearrange("h t s -> t h s")).then_inc(raw_in, 16)
                pool.dma_start(st_raw, state_pool[l].rearrange("b n c -> (b n) c")).then_inc(raw_in, 16)
                pool.wait_ge(park_out, 16 * (l + 1))
                pool.wait_ge(h_ready, l * 2 * KT + KT)
                pool.wait_ge(sq_ready, l * 32 + KT)
                apart(pool)
                pool.dma_start(cache, cache_k[l].rearrange("b n h d -> n b (h d)")).then_inc(kc_in, 16)
                pool.dma_start(pscale[:, :], pool_scale[l].rearrange("(g p) -> p g", p=P)).then_inc(par_in, 16)
                pool.dma_start(sink[:, :], sinks[l].partition_broadcast(P)).then_inc(par_in, 16)
                pool.dma_start(poolw[:, :, :], pool_w[l].rearrange("g c d -> c g d")).then_inc(par_in, 16)
                side.wait_full("kc0")
                side.wait_full("kc1")
                apart(pool)
                pool.dma_start(cache, cache_v[l].rearrange("b n h d -> n b (h d)")).then_inc(vc_in, 16)
                side.wait_read("v")
                apart(pool)
                pool.dma_start(nv_p[l, 0].rearrange("n h d -> n (h d)"), v_tok[:, NBLK - 1, :]).then_inc(kv_out, 16)
                side.wait_read("kvtail")
                apart(pool)
                pool.dma_start(nk_p[l, 0].rearrange("n h d -> n (h d)"), k_tail).then_inc(kv_out, 16)
                for dst, src in ((nk_s, k_new), (nv_s, v_new[:, :])):
                    pool.dma_start(dst[l, :, P - DT:P].rearrange("b t h d -> b t (h d)"), src).then_inc(kv_out, 16)
                side.wait_read("wm")
                apart(pool)
                pool.affine_select(out=wmt[:, :, :], in_=wmt[:, :, :], compare_op=ALU.is_ge, fill=0.0, base=0,
                                   pattern=[[0, 4], [1, P]], channel_multiplier=-1).then_inc(wm_masked, 1)
                pool.wait_ge(wm_masked, l + 1)
                apart(pool)
                for b in range(DB):
                    pool.dma_start(w4[b * DT:(b + 1) * DT, :, b * DT:(b + 1) * DT], wmt[0:DT, :, 0:DT]).then_inc(w4_in, 16)
                for u in range(16):
                    if 2 <= u <= 5:
                        pool_windows(u - 2)
                    if u == 6:
                        pool.wait_ge(pooled_ready, l * 4 + 4)
                        apart(pool)
                        for i, src in enumerate((ln_g[l], ln_b[l], sgu_b[l].rearrange("h t -> (h t)"))):
                            pool.dma_start(pars[:, i, :], src.partition_broadcast(P)).then_inc(lnp_in, 16)
                    if u == 10:
                        side.wait_read("xbo")
                        apart(pool)
                        pool.dma_start(npool_p[l, 0], xbo[0:HIST, :]).then_inc(xb_out, 16)
                        pool.dma_start(npool_s[l, :, HIST - DT:HIST], xbo[HIST:HIST + NS, :]).then_inc(xb_out, 16)
                    if u == 11:
                        pool.wait_ge(ln_mid, l + 1)
                        pool.wait_ge(lnp_in, 48 * (l + 1))
                        for i, op in enumerate((ALU.mult, ALU.add)):
                            own.mark(pool.tensor_tensor(vn[:, 0:4, :], vn[:, 0:4, :], pars[:, i, :].unsqueeze(1).broadcast_to((P, 4, SEQ)), op))
                            ins = pool.tensor_tensor(vn[0:NS, 4, :], vn[0:NS, 4, :], pars[0:NS, i, :], op)
                            if i == 0:
                                own.mark(ins)
                                own.settle()
                            else:
                                ins.then_inc(vn_ready, 1)
                        pool.wait_ge(vn_ready, l + 1)
                        apart(pool)
                        pool.dma_start(nchunk_s[l].rearrange("b t f -> (b t) f"), vn[0:NS, 4, :]).then_inc(vn_out, 16)
                    if u >= 13:
                        gate(XB0 + u - 1, (u - 1) % 2, mix[:, XB0 + u - 1 - 16, :])
                        hh = u - 13
                        side.wait_read(("sg", hh))
                        pool.tensor_tensor(mix[:, 12 + hh, :], mix[:, 12 + hh, :], tmp, ALU.mult).then_inc(sg_out, 1)
                    normalise(u)
                side.wait_read(("sg", 3))
                pool.tensor_tensor(mix[:, 15, :], mix[:, 15, :], tmp, ALU.mult).then_inc(sg_out, 1)
                with pool.Fori(0, (GA0 - GC0) // 2) as i:
                    for j in range(2):
                        gate(GC0 + i * 2 + j - 1, 1 - j, tile_at(i * 2 + j + 11))
                gate(GA0 - 1, 1, mix[:, 15, :])
                side.wait_read(("pv", 15))
                apart(pool)
                with pool.Fori(0, (OUT0 - GA0) // 2) as i:
                    for j in range(2):
                        gate(GA0 + i * 2 + j, j, tile_at(i * 2 + j))
                pool.wait_ge(gate_done, l * 16 + 16)
                pool.wait_ge(vn_out, 16 * (l + 1))
                pool.wait_ge(xb_out, 32 * (l + 1))
                pool.wait_ge(kv_out, 64 * (l + 1))
                apart(pool)
                pool.dma_start(arena[:, :], x_park).then_inc(park_in, 16)
                add_square(l, 1, 1, 1)
                with pool.Fori(0, (N_OUT - 4) // 2) as i:
                    for j in range(2):
                        add_square(l, 2 + i * 2 + j, 1, j)
                add_square(l, N_OUT - 2, 1, 0)
                assert own.n == POOL_OWN, own.n
                with pool.If(l < DEPTH - 1):
                    pool.wait_ge(park_in, 16 * (l + 1))
                    x_parts(l + 1)
            pool.wait_ge(park_in, 16 * DEPTH)
            for t in range(KT):
                if t not in FIN_DVE:
                    residual(DEPTH, t)
            pool.wait_ge(kv_out, 64 * DEPTH)
            pool.wait_ge(xb_out, 32 * DEPTH)
            pool.wait_ge(vn_out, 16 * DEPTH)
            pool.wait_ge(park_out, 16 * DEPTH)
            pool.wait_ge(copy_out, 48)


def tables():
    r = np.arange(P)
    inv = (10000.0 ** (-np.arange(0, HD, 2) / HD)).astype(np.float32)
    pos = np.concatenate([np.arange(SEQ), np.tile(PAST + np.arange(DT), DB)]).astype(np.float32)
    ang = (inv[r % 32][:, None] * pos[None, :]).astype(np.float32)
    sign = np.where(r % HD < 32, 1.0, -1.0).astype(np.float32)[:, None]
    prev = np.where(r[None, :] > r[:, None], 0.0, NEG)
    same = np.where(r[None, :] <= r[:, None], 0.0, NEG)
    b, t = r // 32, r % DT
    smask = np.full((P, 2, P + NS), NEG, np.float32)
    for c in range(2):
        smask[:, c, 0:P] = np.where(r[None, :] > t[:, None], 0.0, NEG)
        nb, nt = np.arange(NS) // DT, np.arange(NS) % DT
        smask[:, c, P:] = np.where((nb[None, :] == (c * 4 + b)[:, None]) & (nt[None, :] <= t[:, None]), 0.0, NEG)
    sel = (((r % 32) // DT)[:, None] == np.arange(8)[None, :]).astype(np.float32)
    fix = np.stack([w / np.minimum(w, np.arange(16) + 1.0) for w in POOLW]).astype(np.float32)
    return {
        "c_cos": np.cos(ang), "c_sin": np.sin(ang) * sign, "c_band": np.concatenate([prev, same], 1).astype(np.float32),
        "c_smask": smask, "c_ident": np.eye(P, dtype=np.float32), "c_sel": sel, "c_fix": np.tile(fix[None], (P, 1, 1)),
    }


_INS = ["x_prompt", "x_sample", "cache_k", "cache_v", "state_pool", "w_in", "w_out", "norm_pre", "norm_post", "attn_sinks",
        "pool_w", "pool_scale", "sgu_ln_g", "sgu_ln_b", "sgu_w", "sgu_b"]
_OUTS = [(1, SEQ, D), (DB, DT, D), (DEPTH, 1, P, NKV, HD), (DEPTH, 1, P, NKV, HD), (DEPTH, 1, HIST, SEQ),
         (DEPTH, DB, P, NKV, HD), (DEPTH, DB, P, NKV, HD), (DEPTH, DB, HIST, SEQ), (DEPTH, DB, DT, SEQ)]


def kernel(**inputs):
    import concourse.bacc as _bacc
    from concourse.bass_utils import run_bass_kernel_spmd as _run

    nc = _bacc.Bacc("TRN2", target_bir_lowering=False, num_devices=1)
    arrays, args = {}, []
    for name, a in [(n, inputs[n]) for n in _INS] + list(tables().items()):
        a = np.ascontiguousarray(a)
        arrays[f"in_{name}_dram"] = a
        args.append(nc.dram_tensor(f"in_{name}_dram", a.shape, mybir.dt.from_np(a.dtype), kind="ExternalInput").ap())
    for i, shape in enumerate(_OUTS):
        args.append(nc.dram_tensor(f"out_{i}_dram", shape, F32, kind="ExternalOutput").ap())
    args.append(nc.dram_tensor("x_park", (P, KT * NTOK), F32, kind="Internal").ap())
    program(nc, *args)
    r = _run(nc, [arrays], core_ids=[0])
    return tuple(r.results[0][f"out_{i}_dram"] for i in range(len(_OUTS)))
```

```python
from contextlib import ExitStack, contextmanager

import numpy as np

import concourse.bass as bass
from concourse import mybir

F32 = mybir.dt.float32
F32R = mybir.dt.float32r
ALU = mybir.AluOpType
ACT = mybir.ActivationFunctionType
AX_X = mybir.AxisListType.X

P = 128
D = 2048
KT = D // P
DEPTH = 2
SEQ = 512
NBLK = SEQ // P
DB, DT = 8, 4
NS = DB * DT
NTOK = SEQ + NS
HALF = NTOK // 2
HD = 64
NH, NKV, GROUP = 16, 4, 4
SCALE = HD ** -0.5
POOLW = (2, 4, 8, 16)
HIST = 15
SEXT = HIST + DT
EXT = HIST + SEQ + DB * SEXT
PAST = 2048
EPS = 1e-6
NEG = -1.0e30

DIN = 5120
N_IN, N_OUT = DIN // P, D // P
NB = N_IN + N_OUT
KV0, Q0, XB0, VS0, U0, GB0, GC0, GA0, OUT0 = 0, 4, 12, 16, 20, 24, 28, 32, 40
COL = {KV0: 1024, Q0: 0, XB0: 2560, VS0: 4096, U0: 3584, GB0: 3072, GC0: 4608, GA0: 1536}
QUART = NTOK // 4
HK = KT // 2
OUT_ORDER = list(range(8, 16)) + list(range(0, 8))

SKEYS = ["kv2", "xsum", "kc1", "kvtail", "state"]
TKEYS = ["kv3", "kc0", "v", "wm"]
for _u in range(16):
    SKEYS.append(("sc", _u))
    if _u == 0:
        SKEYS.append("ssc")
    if _u:
        TKEYS.append(("pv", _u - 1))
    TKEYS += {2: ["spt"], 3: ["spv"], 4: [("pm", 0)], 5: [("pm", 1)], 6: [("pm", 2)], 7: [("pm", 3)],
              8: ["vt0", "vt2"], 9: ["xbo"], 12: [("sg", 0)], 13: [("sg", 1)], 14: [("sg", 2)], 15: [("sg", 3)]}.get(_u, [])
    if _u == 8:
        SKEYS.append("vt1")
    TKEYS.append(("tp", _u))
SKEYS.append("ysum")
TKEYS += [("pv", 15), "ynorm"]
S_TURN = {k: i for i, k in enumerate(SKEYS)}
T_TURN = {k: i for i, k in enumerate(TKEYS)}

DVE_OWN, POOL_OWN = 119, 21
ACC = 29
KVU = 2 * Q0
TURN_DVE = (12, 14)
UNIT_AT = {3: 2, 5: 3, 8: 4, 10: 5, 13: 6}
EARLY = 3
FIN_DVE = (3, 5, 8, 10, 13, 15)
PARAMS = 3
CONSTS = 6
MEMSETS = 5


def program(nc, x_p, x_s, cache_k, cache_v, state_pool, w_in, w_out, norm_pre, norm_post, sinks, pool_w, pool_scale,
            ln_g, ln_b, sgu_w, sgu_b, c_cos, c_sin, c_band, c_smask, c_ident, c_sel, c_fix,
            y_p, y_s, nk_p, nv_p, npool_p, nk_s, nv_s, npool_s, nchunk_s, x_park):
    with ExitStack() as ctx:
        ctx.enter_context(nc.allow_non_contiguous_dma(reason="small parameters, a few hundred words a layer"))

        def sb(name, shape, dt=F32):
            return ctx.enter_context(nc.sbuf_tensor(name, shape, dt))

        def sem(name):
            return ctx.enter_context(nc.semaphore(name))

        h_hi = sb("h_hi", [P, KT, NTOK], F32R)
        h_lo = sb("h_lo", [P, KT, NTOK], F32R)
        mix = sb("mix", [P, KT, NTOK])
        w_raw = sb("w_raw", [P, 2, HK, P])
        w_hi = sb("w_hi", [P, 2, HK, P], F32R)
        w_lo = sb("w_lo", [P, 2, HK, P], F32R)
        arena = sb("arena", [P, KT * NTOK])
        k_hi = sb("k_hi", [P, SEQ], F32R)
        k_lo = sb("k_lo", [P, SEQ], F32R)
        q_st = sb("q_st", [P, GROUP, P], F32R)
        pt_hi = sb("pt_hi", [P, 2, GROUP * P], F32R)
        pt_lo = sb("pt_lo", [P, 2, GROUP * P], F32R)
        v_st = sb("v_st", [P, 2, 2, HD], F32R)
        cos = sb("cos", [P, NTOK])
        sin = sb("sin", [P, NTOK])
        band = sb("band", [P, 2 * P])
        smask = sb("smask", [P, 2, P + NS])
        ident = sb("ident", [P, P])
        ones = sb("ones", [P, P])
        rms = sb("rms", [P, NTOK])
        acc = sb("acc", [P, NTOK])
        pars = sb("pars", [P, 3, SEQ])
        wmt = sb("wmt", [P, 4, P])
        w4 = sb("w4", [NS, 4, NS])
        poolw = sb("poolw", [P, 4, P])
        qbd = sb("qbd", [P, 2, DB, 32])
        stt = sb("stt", [P, 4, DB * HIST])
        g_pre = sb("g_pre", [P, (DEPTH + 1) * KT])
        g_post = sb("g_post", [P, DEPTH * KT])
        pscale = sb("pscale", [P, 4])
        sink = sb("sink", [P, NH])
        sel = sb("sel", [P, 8])
        fix = sb("fix", [P, 4, 16])
        v_new = sb("v_new", [NS, 4 * HD])
        xbo = sb("xbo", [HIST + NS, SEQ])
        xb_keep = sb("xb_keep", [P, 4, HIST + NS])
        eps = sb("eps", [P, 1])
        eps2 = sb("eps2", [P, 1])
        ynorm = sb("ynorm", [P, QUART])
        zeros = sb("zeros", [P, HIST])
        junk = sb("junk", [P, 6])
        sm = sb("sm", [P, 2, 6, GROUP])
        sms = sb("sms", [P, 8, 4])
        ssel = sb("ssel", [P, 2, 8])
        ssink = sb("ssink", [P, 2])
        es = sb("es", [P, GROUP])
        ess = sb("ess", [P, 4])
        stats = sb("stats", [P, 5, 6])
        mv = sb("mv", [P, 5, 2])
        rstd = sb("rstd", [P, 5])

        at = [0]

        def part(n):
            at[0] += n
            assert at[0] <= KT * NTOK
            return arena[:, at[0] - n:at[0]]

        zr = part(2 * NTOK).rearrange("p (a n) -> p a n", a=2)
        krot = part(2 * NTOK).rearrange("p (a n) -> p a n", a=2)
        v_tok = part(NBLK * 4 * HD).rearrange("p (b f) -> p b f", b=NBLK)
        prob = part(GROUP * 2 * P).rearrange("p (h k) -> p h k", h=GROUP)
        late = part(2 * DB * (P + NS))
        kct = late.rearrange("p (a b k) -> p a b k", a=2, b=DB)
        ps = late[:, 0:4 * (P + NS)].rearrange("p (a k) -> p a k", a=4)
        pst = late[:, 4 * (P + NS):4 * (P + NS) + 1024].rearrange("p (a k) -> p a k", a=2)
        vn = late.rearrange("p (b f) -> p b f", b=5)
        ext_a = part(EXT)
        ext_b = part(EXT)
        th = part(NTOK)
        ext_c = pars[:, :, :].rearrange("p a n -> p (a n)")[:, 0:EXT]
        sq = pars[:, :, :].rearrange("p a n -> p (a n)")[:, 0:2 * NTOK].rearrange("p (a n) -> p a n", a=2)
        tmp = (ext_a[:, 0:NTOK], ext_b[:, 0:NTOK])
        x_old = arena[:, :].rearrange("p (t n) -> p t n", t=KT)
        stage = arena[:, 0:NBLK * D].rearrange("p (b f) -> p b f", b=NBLK)
        g_raw = arena[0:DEPTH * KT, NBLK * D:NBLK * D + 2 * P].rearrange("p (a n) -> p a n", a=2)
        stage_s = mix[0:NS, 12:16, :].rearrange("p a n -> p (a n)")[:, 0:D]
        stage_y = [(w_raw[:, :, :, :].rearrange("p a b c -> p (a b c)") if q == 0 else
                    arena[:, (q - 1) * 4 * NTOK:(q - 1) * 4 * NTOK + D]).rearrange("p (b f) -> p b f", b=NBLK) for q in range(4)]
        stage_ys = [pars[0:NS, q, :] if q < 3 else acc[0:NS, 0:SEQ] for q in range(4)]
        cache = mix[:, 12:16, :].rearrange("p a n -> p (a n)")[:, 0:DB * 4 * HD].rearrange("p (b f) -> p b f", b=DB)
        outs = mix[:, 8:10, :].rearrange("p a n -> p (a n)")
        k_tail, k_new = outs[:, 0:256], outs[0:NS, 256:512]
        sgw_raw = prob[:, 0:2, :].rearrange("p h k -> p (h k)").rearrange("p (h s) -> p h s", h=4)
        st_raw = prob[0:DB * HIST, 2:4, :].rearrange("p h k -> p (h k)")

        Z = [ctx.enter_context(nc.psum_tensor(f"z{j}", [P, 2, 512], F32)) for j in range(2)]
        S = ctx.enter_context(nc.psum_tensor("side_s", [P, 2, 512], F32))
        T = ctx.enter_context(nc.psum_tensor("side_t", [P, 2, 512], F32))

        ident_in, const_in, x_in, g_in, w4_in, par_in, lnp_in, raw_in, kc_in, vc_in, park_in = (sem(n) for n in (
            "ident_in", "const_in", "x_in", "g_in", "w4_in", "par_in", "lnp_in", "raw_in", "kc_in", "vc_in", "park_in"))
        x_quarter_in = [sem(f"x_quarter_in{q}") for q in range(4)]
        w_landed = [sem("w_landed0"), sem("w_landed1")]
        park_out, kv_out, xb_out, vn_out, fin_out, copy_out = (sem(n) for n in (
            "park_out", "kv_out", "xb_out", "vn_out", "fin_out", "copy_out"))
        ready0, g_full, g_ready, xt_full, xt_act = (sem(n) for n in ("ready0", "g_full", "g_ready", "xt_full", "xt_act"))
        x_ready = sem("x_ready")
        upd_ready = sem("upd_ready")
        fin_added = sem("fin_added")
        w_hi_ready = sem("w_hi_ready")
        w_split = sem("w_split")
        w_half_used = sem("w_half_used")
        z_ready = sem("z_ready")
        z_free = sem("z_free")
        h_hi_ready, h_ready = sem("h_hi_ready"), sem("h_ready")
        sq_ready, acc_done = sem("sq_ready"), sem("acc_done")
        s_full, s_free, t_full, t_free = sem("s_full"), sem("s_free"), sem("t_full"), sem("t_free")
        kv_rot, q_rot, kct_new = sem("kv_rot"), sem("q_rot"), sem("kct_new")
        att_ready = sem("att_ready")
        ynorm_ready = sem("ynorm_ready")
        v_ready = sem("v_ready")
        wm_masked, qbd_ready = sem("wm_masked"), sem("qbd_ready")
        khi_ready, klo_ready, qhi_ready, qlo_ready, vhi_ready, vlo_ready, pthi_ready = (sem(n) for n in (
            "khi_ready", "klo_ready", "qhi_ready", "qlo_ready", "vhi_ready", "vlo_ready", "pthi_ready"))
        max_ready, exp_ready, den_ready, norm_ready, smax_ready, sexp_ready, sprob_ready = (sem(n) for n in (
            "max_ready", "exp_ready", "den_ready", "norm_ready", "smax_ready", "sexp_ready", "sprob_ready"))
        ext_ready, pooled_ready = sem("ext_ready"), sem("pooled_ready")
        var_ready, std_ready, ln_mid, vn_ready, sg_out = (sem(n) for n in ("var_ready", "std_ready", "ln_mid", "vn_ready", "sg_out"))
        gate_th, gate_t, gate_done = sem("gate_th"), sem("gate_t"), sem("gate_done")
        fin_full, fin_act = sem("fin_full"), sem("fin_act")
        own_v, own_p = sem("own_v"), sem("own_p")

        block = ctx.enter_context(nc.Block())

        def apart(eng):
            eng.nop(nofuse=True)

        class Own:

            def __init__(self, eng, s, per_layer):
                self.eng, self.s, self.per, self.n, self.extra, self.layer = eng, s, per_layer, 0, 0, None

            def mark(self, ins):
                ins.then_inc(self.s, 1)
                self.n += 1

            def settle(self):
                self.eng.wait_ge(self.s, self.layer * self.per + self.extra + self.n)

            @contextmanager
            def repeat(self, times, per_pass):
                first = self.n
                with self.eng.Fori(0, times) as i:
                    self.extra = i * per_pass
                    yield i
                assert self.n - first == per_pass, (self.n - first, per_pass)
                self.extra, self.n = 0, first + times * per_pass

        def two(ap):
            return ap.rearrange("p (c n) -> p c n", c=2)

        def zcols(z):
            return z[:, :, 0:HALF]

        class Sides:

            def __init__(self, eng, layer):
                self.eng, self.layer = eng, layer

            def _(self, key):
                if key in S_TURN:
                    return s_full, s_free, self.layer * len(SKEYS) + S_TURN[key]
                return t_full, t_free, self.layer * len(TKEYS) + T_TURN[key]

            def wait_free(self, key):
                _, free, turn = self._(key)
                self.eng.wait_ge(free, turn + 1)

            def wait_full(self, key):
                full, _, turn = self._(key)
                self.eng.wait_ge(full, turn + 1)

            def wait_read(self, key):
                _, free, turn = self._(key)
                self.eng.wait_ge(free, turn + 2)

            def filled(self, key, ins):
                ins.then_inc(self._(key)[0], 1)

            def freed(self, key, ins):
                ins.then_inc(self._(key)[1], 1)

        @block.sync
        def _(sp):
            sp.dma_start(ident[:, :], c_ident).then_inc(ident_in, 16)
            for q in range(4):
                c = slice(q * SEQ, (q + 1) * SEQ)
                sp.dma_start(stage[:, :, c], x_p[:, :, c].rearrange("a (b p) f -> p (a b) f", p=P)).then_inc(x_quarter_in[q], 16)
                if q == 0:
                    sp.dma_start(stage_s, x_s.rearrange("b t f -> (b t) f")).then_inc(x_in, 16)
            with sp.Fori(0, DEPTH) as l:
                def load_in(n, col):
                    for h in range(2):
                        sp.wait_ge(w_split, l * (2 * NB) + n * 2 + h + 1)
                        apart(sp)
                        sp.dma_start(w_raw[:, h, :, :],
                                     w_in[l, h * HK * P:(h + 1) * HK * P, bass.ds(col, P)].rearrange("(k p) c -> p k c", p=P)
                                     ).then_inc(w_landed[h], 16)

                def load_out(n, col):
                    for h in range(2):
                        r0 = OUT_ORDER[h * HK] * P
                        sp.wait_ge(w_split, l * (2 * NB) + n * 2 + h + 1)
                        apart(sp)
                        sp.dma_start(w_raw[:, h, :, :],
                                     w_out[l, r0:r0 + HK * P, bass.ds(col, P)].rearrange("(k p) c -> p k c", p=P)
                                     ).then_inc(w_landed[h], 16)

                with sp.Fori(0, KVU // 2) as i:
                    for h in range(2):
                        sp.wait_ge(w_split, l * (2 * NB) + i * 2 + h + 1)
                        apart(sp)
                        sp.dma_start(w_raw[:, h, :, :].rearrange("p a c -> p (a c)").rearrange("p (k c) -> p k c", k=2),
                                     w_in[l, bass.ds((i * 2 + h) * (2 * P), 2 * P), COL[KV0]:COL[KV0] + 4 * P].rearrange("(k p) c -> p k c", p=P)
                                     ).then_inc(w_landed[h], 16)
                starts = [Q0, XB0, VS0, U0, GB0, GC0, GA0, OUT0]
                for a, b in zip(starts[:-1], starts[1:]):
                    with sp.Fori(0, b - a) as i:
                        load_in(a + i, COL[a] + i * P)
                with sp.Fori(0, N_OUT) as i:
                    load_out(OUT0 + i, i * P)
            for e in range(8):
                q, h = e // 2, slice(e % 2 * SEQ // 2, (e % 2 + 1) * SEQ // 2)
                sp.wait_ge(fin_act, 2 * e + 2)
                sp.dma_start(y_p[:, :, q * SEQ + h.start:q * SEQ + h.stop].rearrange("a (b p) f -> p (a b) f", p=P),
                             stage_y[q][:, :, h]).then_inc(fin_out, 16)
                if e % 2:
                    sp.dma_start(y_s[:, :, q * SEQ:(q + 1) * SEQ].rearrange("b t f -> (b t) f"), stage_ys[q]).then_inc(fin_out, 16)
            sp.wait_ge(fin_out, 16 * 12)

        @block.tensor
        def _(pe):
            pe.wait_ge(ident_in, 16)
            pe.wait_ge(ready0, MEMSETS)
            pairs = [Z[0], Z[1], S, T]
            for t in range(KT):
                o = pairs[t % 4]
                if t % 4 == 0:
                    pe.wait_ge(x_quarter_in[t // 4], 16)
                if t == 0:
                    pe.wait_ge(x_in, 16)
                if t >= 4:
                    pe.wait_ge(x_ready, t - 3)
                if t == 10:
                    pe.wait_ge(x_ready, 8)
                    pe.wait_ge(g_in, 32)
                    for i in range(2):
                        mm = pe.transpose(T[:, 0, i * DEPTH * KT:(i + 1) * DEPTH * KT], g_raw[:, i, :], ident[0:DEPTH * KT, 0:DEPTH * KT])
                    mm.then_inc(g_full, 1)
                if t == 11:
                    pe.wait_ge(g_ready, 2)
                for b in range(NBLK):
                    pe.transpose(o[:, 0, b * P:(b + 1) * P], stage[:, b, t * P:(t + 1) * P], ident[:, :])
                pe.transpose(o[:, 1, 0:NS], stage_s[:, t * P:(t + 1) * P], ident[0:NS, 0:NS]).then_inc(xt_full, 1)
            pe.wait_ge(x_ready, KT)

            with pe.Fori(0, DEPTH) as l:
                side = Sides(pe, l)

                def run(n, j, phase=0, first=False, mids=None, base=0):
                    mids = mids or {}
                    pe.wait_ge(z_free, l * NB + (Q0 if isinstance(n, int) and n == Q0 else n + 1))
                    for i in range(KT):
                        h, kk = divmod(i, HK)
                        if kk == 0:
                            pe.wait_ge(w_split, l * (2 * NB) + n * 2 + h + 3)
                        if first:
                            pe.wait_ge(h_ready, (l * 2 + phase) * KT + i + 1)
                        for w, x in ((w_hi, h_hi), (w_hi, h_lo), (w_lo, h_hi)):
                            for c in range(2):
                                mm = pe.matmul(Z[j][:, c, 0:HALF], w[:, h, kk, :], x[:, i, c * HALF:(c + 1) * HALF],
                                               start=(i == 0 and w is w_hi and x is h_hi), stop=(i == KT - 1 and w is w_lo))
                        if i == HK - 1:
                            mm.then_inc(w_half_used, 1)
                        if i == KT - 1:
                            mm.then_inc(z_ready, 1)
                        if i in mids:
                            mids[i]()

                def turn_many(key, moves):
                    side.wait_free(key)
                    apart(pe)
                    for o, i in moves:
                        mm = pe.transpose(o, i, ident[0:i.shape[0], 0:i.shape[0]])
                    side.filled(key, mm)

                def x_sum():
                    pe.wait_ge(acc_done, l * ACC + 15)
                    side.wait_free("xsum")
                    for c in range(2):
                        mm = pe.matmul(S[:, c, 0:HALF], ones[:, :], acc[:, c * HALF:(c + 1) * HALF], start=True, stop=True)
                    side.filled("xsum", mm)

                def y_sum():
                    pe.wait_ge(acc_done, l * ACC + ACC)
                    side.wait_free("ysum")
                    for q in range(4):
                        pe.matmul(S[q * 32:(q + 1) * 32, 0, 0:QUART], ones[:, 0:32], acc[:, q * QUART:(q + 1) * QUART],
                                  start=True, stop=False)
                    pe.wait_ge(sq_ready, l * 32 + 32)
                    for q in range(4):
                        mm = pe.matmul(S[q * 32:(q + 1) * 32, 0, 0:QUART], ones[:, 0:32], sq[:, 1, q * QUART:(q + 1) * QUART],
                                       start=False, stop=True)
                    side.filled("ysum", mm)

                def y_norm():
                    pe.wait_ge(ynorm_ready, l + 1)
                    side.wait_free("ynorm")
                    for q in range(4):
                        mm = pe.matmul(T[:, q // 2, q % 2 * QUART:(q % 2 + 1) * QUART], ident[:, 32 * q:32 * q + 1].broadcast_to((P, P)),
                                       ynorm[:, :], start=True, stop=True)
                    side.filled("ynorm", mm)

                def scores(u):
                    g, b = divmod(u, NBLK)
                    side.wait_free(("sc", u))
                    pe.wait_ge(qlo_ready, l * 16 + u + 1)
                    if b == 0:
                        pe.wait_ge(klo_ready, l * 4 + g + 1)
                    k0 = max(b - 1, 0) * P
                    w = (b + 1) * P - k0
                    for hh in range(GROUP):
                        o = S[:, hh // 2, (hh % 2) * 2 * P:(hh % 2) * 2 * P + w]
                        for kk in (k_hi, k_lo):
                            mm = pe.matmul(o, q_st[:, hh, :], kk[:, k0:k0 + w], start=(kk is k_hi), stop=(kk is k_lo))
                    side.filled(("sc", u), mm)

                def turn_probs(u):
                    b = u % NBLK
                    pe.wait_ge(norm_ready, l * 16 + u + 1)
                    nk = 1 if b == 0 else 2
                    turn_many(("tp", u), [(T[:, kb, hh * P:(hh + 1) * P], prob[:, hh, kb * P:(kb + 1) * P])
                                          for kb in range(nk) for hh in range(GROUP)])

                def values(u):
                    b = u % NBLK
                    side.wait_read(("tp", u))
                    pe.wait_ge(vlo_ready, l * 16 + u + 1)
                    side.wait_free(("pv", u))
                    nk = 1 if b == 0 else 2
                    terms = [(p, kb) for kb in range(nk) for p in (pt_hi, pt_lo)]
                    for i, (p, kb) in enumerate(terms):
                        mm = pe.matmul(T[:, 0, :], v_st[:, kb, :, :], p[:, kb, :], start=(i == 0), stop=(i == len(terms) - 1))
                    side.filled(("pv", u), mm)

                def pool_mm(g):
                    pe.wait_ge(pooled_ready, l * 4 + g + 1)
                    side.wait_free(("pm", g))
                    for c in range(2):
                        mm = pe.matmul(T[:, c, 0:HALF], poolw[:, g, :], mix[:, 8 + g, c * HALF:(c + 1) * HALF], start=True, stop=True)
                    side.filled(("pm", g), mm)

                def turn_xb():
                    pe.wait_ge(ext_ready, l * 4 + 4)
                    turn_many("xbo", [(T[0:HIST + NS, 0, g * P:(g + 1) * P], xb_keep[:, g, :]) for g in range(4)])

                def turn_vs(key):
                    pe.wait_ge(z_free, l * NB + VS0 + 3 + 3)
                    if key == "vt2":
                        turn_many(key, [(T[0:NS, 0, t * P:(t + 1) * P], mix[:, 12 + t, SEQ:NTOK]) for t in range(4)])
                    else:
                        o, b0 = (T, 0) if key == "vt0" else (S, 2)
                        turn_many(key, [(o[:, b, t * P:(t + 1) * P], mix[:, 12 + t, (b0 + b) * P:(b0 + b + 1) * P])
                                        for b in range(2) for t in range(4)])

                def spatial(hh):
                    pe.wait_ge(vn_ready, l + 1)
                    pe.wait_ge(wm_masked, l + 1)
                    pe.wait_ge(w4_in, DB * 16 * (l + 1))
                    side.wait_free(("sg", hh))
                    for b in range(NBLK):
                        pe.matmul(T[:, 0, b * P:(b + 1) * P], vn[:, b, hh * P:(hh + 1) * P], wmt[:, hh, :], start=True, stop=True)
                    mm = pe.matmul(T[:, 1, 0:NS], vn[0:NS, 4, hh * P:(hh + 1) * P], w4[:, hh, :], start=True, stop=True)
                    side.filled(("sg", hh), mm)

                def sample_scores():
                    pe.wait_ge(qbd_ready, l * 16 + 16)
                    pe.wait_ge(kct_new, l * 2 + 2)
                    side.wait_read("kc0")
                    side.wait_read("kc1")
                    side.wait_free("ssc")
                    for b in range(DB):
                        r = (b % 4) * 32
                        for p in range(2):
                            mm = pe.matmul(S[r:r + 32, b // 4, p * (P + NS):(p + 1) * (P + NS)], qbd[:, p, b, :], kct[:, p, b, :],
                                           start=True, stop=True)
                    side.filled("ssc", mm)

                def sample_turn():
                    pe.wait_ge(sprob_ready, l + 1)
                    turn_many("spt", [(T[:, 0, q * P:(q + 1) * P], ps[:, q, 0:P]) for q in range(4)]
                              + [(T[0:NS, 1, q * P:(q + 1) * P], ps[:, q, P:P + NS]) for q in range(4)])

                def sample_values():
                    side.wait_read("spt")
                    pe.wait_ge(vc_in, 16 * (l + 1))
                    side.wait_free("spv")
                    new = pst[0:NS, 1, :].rearrange("p (c a r) -> p c a r", c=2, a=2)
                    for p in range(2):
                        pe.matmul(T[:, 0, p * 256:(p + 1) * 256].rearrange("p (c r) -> p c r", c=2), v_new[:, p * P:(p + 1) * P],
                                  new[:, :, p, :], start=True, stop=False)
                        for b in range(DB):
                            c0 = (b // 4) * 256 + p * P + (b % 4) * 32
                            mm = pe.matmul(T[:, 0, p * 256 + b * 32:p * 256 + (b + 1) * 32], cache[:, b, p * P:(p + 1) * P],
                                           pst[:, 0, c0:c0 + 32], start=False, stop=(b == DB - 1))
                    side.filled("spv", mm)

                pe.wait_ge(z_free, l * NB + 2)
                side.wait_free("kv2")
                side.wait_free("kv3")
                outs4 = (Z[0], Z[1], S, T)
                for m in range(KVU):
                    pe.wait_ge(w_split, l * (2 * NB) + m + 3)
                    for kk in range(2):
                        k = 2 * m + kk
                        pe.wait_ge(h_ready, l * (2 * KT) + k + 1)
                        last = k == KT - 1
                        for b in (2, 3, 0, 1):
                            for w, x in ((w_hi, h_hi), (w_hi, h_lo), (w_lo, h_hi)):
                                for c in range(2):
                                    mm = pe.matmul(outs4[b][:, c, 0:HALF], w[:, m % 2, kk * 4 + b, :], x[:, k, c * HALF:(c + 1) * HALF],
                                                   start=(k == 0 and w is w_hi and x is h_hi), stop=(last and w is w_lo))
                            if last and b >= 2:
                                side.filled("kv2" if b == 2 else "kv3", mm)
                    mm.then_inc(z_ready if m % 2 else w_half_used, 1)
                def cached(key, o, b0):
                    pe.wait_ge(kc_in, 16 * (l + 1))
                    turn_many(key, [(o[:, p, b * P:(b + 1) * P], cache[:, b0 + b, p * P:(p + 1) * P]) for p in range(2) for b in range(4)])

                def turn_v():
                    pe.wait_ge(v_ready, l * 2 + 2)
                    turn_many("v", [(T[:, t, b * P:(b + 1) * P], zr[:, t, b * P:(b + 1) * P]) for t in range(2) for b in range(NBLK)])

                def turn_wm():
                    pe.wait_ge(raw_in, 32 * (l + 1))
                    turn_many("wm", [(T[:, 0, h * P:(h + 1) * P], sgw_raw[:, h, :]) for h in range(4)])

                def turn_kv():
                    pe.wait_ge(kv_rot, l * 2 + 2)
                    turn_many("kvtail", [(S[:, 0, t * P:(t + 1) * P], krot[:, t, SEQ - P:SEQ]) for t in range(2)]
                              + [(S[0:NS, 1, t * P:(t + 1) * P], zr[:, t, SEQ:NTOK]) for t in range(2)]
                              + [(S[0:NS, 1, 256 + t * P:256 + (t + 1) * P], krot[:, t, SEQ:NTOK]) for t in range(2)])

                run(Q0, 0, mids={1: x_sum, 5: lambda: cached("kc0", T, 0), 9: lambda: cached("kc1", S, 4),
                                 14: turn_v})
                run(Q0 + 1, 1, mids={3: turn_wm, 9: turn_kv, 13: lambda: turn_many(
                    "state", [(S[:, 0, g * DB * HIST:(g + 1) * DB * HIST], st_raw[:, g * P:(g + 1) * P]) for g in range(4)])})
                with pe.Fori(1, (XB0 - Q0) // 2) as i:
                    for j in range(2):
                        run(Q0 + i * 2 + j, j)
                for u in range(16):
                    extra = {0: sample_scores, 2: sample_turn, 3: sample_values, 4: lambda: pool_mm(0), 5: lambda: pool_mm(1),
                             6: lambda: pool_mm(2), 7: lambda: pool_mm(3), 8: lambda: turn_vs("vt0"), 9: turn_xb, 12: lambda: spatial(0), 13: lambda: spatial(1),
                             14: lambda: spatial(2), 15: lambda: spatial(3)}
                    mids = {4: (lambda u=u: values(u - 1)) if u else (lambda: None)}
                    if u in extra:
                        mids[8] = extra[u]
                    if u == 8:
                        mids[11] = lambda: turn_vs("vt1")
                        mids[13] = lambda: turn_vs("vt2")
                    scores(u)
                    run(XB0 + u, u % 2, mids=mids)
                    turn_probs(u)
                run(GC0, 0, mids={4: lambda: values(15)})
                run(GC0 + 1, 1)
                with pe.Fori(1, (OUT0 - GC0) // 2) as i:
                    for j in range(2):
                        run(GC0 + i * 2 + j, j)
                for n in (OUT0, OUT0 + 1):
                    run(n, n % 2, phase=1, first=(n == OUT0))
                with pe.Fori(0, (N_OUT - 4) // 2) as i:
                    for j in range(2):
                        run(OUT0 + 2 + i * 2 + j, j, phase=1)
                for n in (NB - 2, NB - 1):
                    run(n, n % 2, phase=1)
                y_sum()
                y_norm()

            for t in range(KT):
                o = pairs[t % 4]
                by_dve = sum(i <= t for i in FIN_DVE)
                if t in FIN_DVE:
                    pe.wait_ge(fin_added, by_dve)
                else:
                    pe.wait_ge(x_ready, DEPTH * KT + t + 1 - by_dve)
                if t >= 4:
                    pe.wait_ge(fin_act, t - 3)
                for b in range(NBLK + 1):
                    c = slice(b * P, min((b + 1) * P, NTOK))
                    dst = o[:, 0, c] if b < NBLK else o[0:NS, 1, 0:P]
                    mm = pe.transpose(dst, mix[:, t, c], ident[:, :])
                mm.then_inc(fin_full, 1)

        @block.scalar
        def _(act):
            def split_of(l, n, h):
                act.wait_ge(w_landed[h], (l * NB + n + 1) * 16)
                act.wait_ge(z_ready if h else w_half_used, l * NB + n + 1)
                act.activation(w_hi[:, h, :, :], w_raw[:, h, :, :], ACT.Copy).then_inc(w_hi_ready, 1)

            def x_parts(l, tiles=range(KT)):
                for t in tiles:
                    act.wait_ge(x_ready, l * KT + t + 1)
                    act.activation(h_hi[:, t, :], mix[:, t, :], ACT.Copy,
                                   scale=g_pre[:, t + KT * l:t + KT * l + 1] if isinstance(l, int) else g_pre[:, bass.ds(l * KT + t, 1)]
                                   ).then_inc(h_hi_ready, 1)
                    if t >= 3:
                        act.wait_ge(acc_done, l * ACC + t - 2)
                    act.activation(acc[:, :] if t == 0 else sq[:, t % 2, :], mix[:, t, :], ACT.Square).then_inc(sq_ready, 1)
                    if t == 1 and isinstance(l, int):
                        split_of(l, 0, 1)
                    if t in UNIT_AT:
                        split_of(l, *divmod(UNIT_AT[t], 2))

            for t in [t for t in range(KT) if t not in TURN_DVE]:
                act.wait_ge(xt_full, t + 1)
                act.activation(mix[:, t, 0:SEQ], [Z[0], Z[1], S, T][t % 4][:, 0, :], ACT.Copy).then_inc(xt_act, 1)
                if t == 11:
                    act.wait_ge(g_ready, 2)
                    x_parts(0, [0])
            split_of(0, 0, 0)
            act.wait_ge(ready0, MEMSETS)
            x_parts(0, range(1, KT))
            with act.Fori(0, DEPTH) as l:
                side = Sides(act, l)

                def split(n, h):
                    split_of(l, n, h)

                def z_read(n):
                    act.wait_ge(z_free, l * NB + n + 3)

                def root(key, dst, src):
                    side.wait_full(key)
                    side.freed(key, act.activation(dst, src, ACT.Sqrt, bias=eps[:, 0:1], scale=1.0 / D))

                def stage_k(g):
                    s, t = (g % 2) * HD, g // 2
                    if g == 0:
                        act.wait_ge(kv_rot, l * 2 + 2)
                    else:
                        side.wait_full(("sc", 4 * g - 1))
                    act.activation(k_hi[s:s + HD, :], krot[s:s + HD, t, 0:SEQ], ACT.Copy)
                    act.activation(k_hi[HD - s:2 * HD - s, :], krot[s:s + HD, t, 0:SEQ], ACT.Copy).then_inc(khi_ready, 1)

                def stage_q(u):
                    g, b = divmod(u, NBLK)
                    if u == 0:
                        act.wait_ge(q_rot, l * 8 + 2)
                    else:
                        side.wait_full(("sc", u - 1))
                    for s in range(2):
                        ins = act.activation(q_st[s * HD:(s + 1) * HD, s:GROUP:2, :],
                                             mix[s * HD:(s + 1) * HD, 2 * g:2 * g + 2, b * P:(b + 1) * P], ACT.Copy)
                    ins.then_inc(qhi_ready, 1)

                def stage_v(u):
                    g, b = divmod(u, NBLK)
                    if u == 0:
                        side.wait_read("v")
                    else:
                        side.wait_full(("pv", u - 1))
                    b0, nk = max(b - 1, 0), min(b + 1, 2)
                    act.activation(v_st[:, 0:nk, 0, :], v_tok[:, b0:b0 + nk, g * HD:(g + 1) * HD], ACT.Copy).then_inc(vhi_ready, 1)

                def probs_hi(u):
                    nk = min(u % NBLK + 1, 2)
                    side.wait_full(("tp", u))
                    act.activation(pt_hi[:, 0:nk, :], T[:, 0:nk, :], ACT.Copy).then_inc(pthi_ready, 1)

                def attended(u):
                    g, b = divmod(u, NBLK)
                    side.wait_full(("pv", u))
                    for s in range(2):
                        o = T[0:HD, 0, :].rearrange("p (i s q) -> p i s q", i=2, s=2)[:, :, s, :]
                        ins = act.activation(mix[s * HD:(s + 1) * HD, 2 * g:2 * g + 2, b * P:(b + 1) * P], o, ACT.Copy)
                    ins.then_inc(att_ready, 1)

                def exps(u):
                    w = P * min(u % NBLK + 1, 2)
                    act.wait_ge(max_ready, l * 16 + u + 1)
                    for hh in range(GROUP):
                        act.activation(prob[:, hh, 0:w], prob[:, hh, 0:w], ACT.Exp, bias=sm[:, u % 2, 2, hh:hh + 1], scale=SCALE,
                                       accum_out=sm[:, u % 2, 4, hh:hh + 1])
                    act.activation(es[:, :], sm[:, u % 2, 3, :], ACT.Exp).then_inc(exp_ready, 1)

                def sample_exps():
                    act.wait_ge(smax_ready, l + 1)
                    for q in range(4):
                        act.activation(ps[:, q, :], ps[:, q, :], ACT.Exp, bias=sms[:, 2, q:q + 1], scale=SCALE,
                                       accum_out=sms[:, 4, q:q + 1])
                    act.activation(ess[:, :], sms[:, 3, :], ACT.Exp).then_inc(sexp_ready, 1)

                def sample_probs_out():
                    side.wait_full("spt")
                    act.activation(pst[:, 0, :], T[:, 0, :], ACT.Copy)
                    side.freed("spt", act.activation(pst[0:NS, 1, :], T[0:NS, 1, :], ACT.Copy))

                def sample_attended():
                    side.wait_full("spv")
                    for p in range(2):
                        for kv in range(2):
                            for s in range(2):
                                t = 4 * p + 2 * kv
                                o = T[kv * HD:(kv + 1) * HD, 0, p * 256:(p + 1) * 256].rearrange(
                                    "p (b v i s t) -> p b v i s t", b=DB, v=2, i=2, s=2)
                                for i in range(2):
                                    ins = act.activation(
                                        mix[s * HD:(s + 1) * HD, t + i, SEQ:NTOK].rearrange("p (b t) -> p b t", b=DB),
                                        o[:, :, kv, i, s, :], ACT.Copy)
                    side.freed("spv", ins)

                def extend(g):
                    z_read(XB0 + g)
                    if g:
                        act.wait_ge(pooled_ready, l * 4 + g)
                    z = zr[:, g % 2, :]
                    tail = ext_a[:, HIST + SEQ:EXT].rearrange("p (b n) -> p b n", b=DB)
                    act.activation(ext_a[:, 0:HIST], zeros[:, :], ACT.Copy)
                    act.activation(ext_a[:, HIST:HIST + SEQ], z[:, 0:SEQ], ACT.Copy)
                    act.activation(tail[:, :, HIST:SEXT], z[:, SEQ:NTOK].rearrange("p (b t) -> p b t", b=DB), ACT.Copy)
                    act.activation(tail[:, :, 0:HIST], stt[:, g, :].rearrange("p (b t) -> p b t", b=DB), ACT.Copy)
                    act.activation(xb_keep[:, g, :], z[:, SEQ - HIST:NTOK], ACT.Copy).then_inc(ext_ready, 1)

                def tanh(n, j):
                    z_read(n)
                    if not isinstance(n, int) or n > GB0:
                        act.wait_ge(gate_done, l * 16 + n - GB0)
                    act.activation(th[:, :], zr[:, j, :], ACT.Tanh, scale=0.5).then_inc(gate_th, 1)

                split(Q0 - 1, 1)
                split(Q0, 0)
                for key, o, j in (("kv2", S, 0), ("kv3", T, 1)):
                    side.wait_full(key)
                    side.freed(key, act.activation(two(zr[:, j, :]), zcols(o), ACT.Copy))
                split(Q0, 1)
                root("xsum", two(rms[:, :]), zcols(S))

                def cached(key, o, b0):
                    side.wait_full(key)
                    side.freed(key, act.activation(kct[:, :, b0:b0 + 4, 0:P], o[:, :, :].rearrange("p a (b k) -> p a b k", b=4), ACT.Copy))

                cached("kc0", T, 0)
                split(Q0 + 1, 0)
                cached("kc1", S, 4)
                side.wait_full("v")
                side.freed("v", act.activation(v_tok.rearrange("p b (t f) -> p t b f", t=2),
                                               T[:, :, :].rearrange("p t (b f) -> p t b f", b=NBLK), ACT.Copy))
                split(Q0 + 1, 1)
                side.wait_full("wm")
                side.freed("wm", act.activation(wmt[:, :, :], T[:, 0, :].rearrange("p (h t) -> p h t", h=4), ACT.Copy))
                split(Q0 + 2, 0)
                side.wait_full("kvtail")
                act.wait_ge(park_out, 64 * (l + 1))
                act.activation(k_tail, S[:, 0, 0:256], ACT.Copy)
                act.activation(v_new[:, :], S[0:NS, 1, 0:256], ACT.Copy)
                side.freed("kvtail", act.activation(k_new, S[0:NS, 1, 256:512], ACT.Copy))
                side.wait_full("state")
                side.freed("state", act.activation(stt[:, :, :], S[:, 0, 0:4 * DB * HIST].rearrange("p (g n) -> p g n", g=4), ACT.Copy))
                with act.Fori(2, XB0 - Q0 - 2) as i:
                    split(Q0 + i, 1)
                    split(Q0 + 1 + i, 0)
                for n in (XB0 - 2, XB0 - 1):
                    split(n, 1)
                    split(n + 1, 0)
                    if n == XB0 - 2:
                        stage_k(0)
                    else:
                        stage_q(0)
                for u in range(16):
                    n = XB0 + u
                    if u:
                        probs_hi(u - 1)
                    split(n, 1)
                    if u:
                        attended(u - 1)
                    stage_v(u)
                    exps(u)
                    if n > GB0:
                        tanh(n - 1, (n - 1) % 2)
                    if u == 1:
                        sample_exps()
                    split(n + 1, 0)
                    if u < 15:
                        if (u + 1) % NBLK == 0:
                            stage_k((u + 1) // NBLK)
                        stage_q(u + 1)
                    if u == 2:
                        sample_probs_out()
                    if u == 3:
                        sample_attended()
                    if u == 9:
                        side.wait_full("xbo")
                        side.freed("xbo", act.activation(xbo[:, :], T[0:HIST + NS, 0, :], ACT.Copy))
                    if u == 8:
                        for key, o, b0 in (("vt0", T, 0), ("vt1", S, 2)):
                            side.wait_full(key)
                            side.freed(key, act.activation(vn[:, b0:b0 + 2, :], o[:, :, :], ACT.Copy))
                        side.wait_full("vt2")
                        side.freed("vt2", act.activation(vn[0:NS, 4, :], T[0:NS, 0, :], ACT.Copy))
                    if u == 9:
                        act.wait_ge(var_ready, l + 1)
                        act.activation(rstd[:, 0:4], mv[:, 0:4, 1], ACT.Sqrt, bias=eps[:, 0:1])
                        act.activation(rstd[0:NS, 4:5], mv[0:NS, 4:5, 1], ACT.Sqrt, bias=eps[0:NS, 0:1]).then_inc(std_ready, 1)
                    if 1 <= u <= 4:
                        extend(u - 1)
                probs_hi(15)
                for n in (GC0, GC0 + 1):
                    split(n, 1)
                    if n == GC0:
                        attended(15)
                    tanh(n - 1, (n - 1) % 2)
                    split(n + 1, 0)
                with act.Fori(1, (OUT0 - GC0) // 2) as i:
                    for j in range(2):
                        n = GC0 + i * 2 + j
                        split(n, 1)
                        tanh(n - 1, 1 - j)
                        split(n + 1, 0)
                act.wait_ge(w_half_used, l * NB + N_IN + 1)
                for i, k in enumerate(OUT_ORDER):
                    if i == HK:
                        split(OUT0, 1)
                        tanh(OUT0 - 1, 1)
                    act.wait_ge(gate_done, l * 16 + i + 1)
                    act.activation(h_hi[:, i, :], mix[:, k, :], ACT.Copy, scale=0.5).then_inc(h_hi_ready, 1)

                def y_square(n, j):
                    act.wait_ge(z_ready, l * NB + n + 2)
                    act.wait_ge(acc_done, l * ACC + 15 + n - OUT0 - 2)
                    act.activation(two(sq[:, j, :]), zcols(Z[j]), ACT.Square).then_inc(sq_ready, 1)

                split(OUT0 + 1, 0)
                act.wait_ge(z_ready, l * NB + OUT0 + 2)
                act.activation(two(acc[:, :]), zcols(Z[0]), ACT.Square).then_inc(sq_ready, 1)
                split(OUT0 + 1, 1)
                split(OUT0 + 2, 0)
                y_square(OUT0 + 1, 1)
                with act.Fori(0, (N_OUT - 4) // 2) as i:
                    for j in range(2):
                        n = OUT0 + 2 + i * 2 + j
                        split(n, 1)
                        split(n + 1, 0)
                        y_square(n, j)
                split(NB - 2, 1)
                split(NB - 1, 0)
                y_square(NB - 2, 0)
                split(NB - 1, 1)
                act.activation(eps2[:, :], eps[:, :], ACT.Sqrt)
                with act.If(l < DEPTH - 1):
                    split_of(l + 1, 0, 0)
                y_square(NB - 1, 1)
                root("ysum", ynorm[:, :], S[:, 0, 0:QUART])
                with act.If(l < DEPTH - 1):
                    split_of(l + 1, 0, 1)
                    x_parts(l + 1)

            for t in range(KT):
                q, c = t // 4, t % 4 * P
                o = [Z[0], Z[1], S, T][t % 4]
                act.wait_ge(fin_full, t + 1)
                act.activation(stage_y[q][:, :, c:c + P], o[:, 0, :].rearrange("p (b f) -> p b f", b=NBLK), ACT.Copy)
                act.activation(stage_ys[q][:, c:c + P], o[0:NS, 1, 0:P], ACT.Copy).then_inc(fin_act, 1)

        @block.vector
        def _(dve):
            def split_of(l, n, h):
                dve.wait_ge(w_hi_ready, l * (2 * NB) + n * 2 + h + 1)
                dve.tensor_tensor(w_lo[:, h, :, :], w_raw[:, h, :, :], w_hi[:, h, :, :].bitcast(F32), ALU.subtract).then_inc(w_split, 1)

            def normalise_y(t):
                dve.tensor_tensor(mix[:, t, :], mix[:, t, :], rms[:, :], ALU.mult).then_inc(upd_ready, 1)

            def x_parts(l, steps=range(KT + 2)):
                first = isinstance(l, int)
                for step in steps:
                    if EARLY <= step < KT and not first:
                        normalise_y(step)
                    t = step - 2
                    if t < 0:
                        continue
                    dve.wait_ge(h_hi_ready, l * (2 * KT) + t + 1)
                    dve.scalar_tensor_tensor(h_lo[:, t, :], mix[:, t, :], g_pre[:, t:t + 1] if first else g_pre[:, bass.ds(l * KT + t, 1)],
                                             h_hi[:, t, :].bitcast(F32), ALU.mult, ALU.subtract).then_inc(h_ready, 1)
                    if t == (1 if first else 0):
                        split_of(l, 0, 1)
                    if t % 2 == 1:
                        dve.wait_ge(sq_ready, l * 32 + t + 1)
                        if t > 1:
                            dve.wait_ge(acc_done, l * ACC + t - 1)
                        dve.tensor_tensor(acc[:, :], acc[:, :], sq[:, t % 2, :], ALU.add).then_inc(acc_done, 1)
                    if t in UNIT_AT:
                        split_of(l, *divmod(UNIT_AT[t], 2))

            for t in range(KT):
                if t == 10:
                    dve.wait_ge(g_full, 1)
                    for i, g in enumerate((g_pre, g_post)):
                        dve.tensor_copy(g[:, 0:DEPTH * KT], T[:, 0, i * DEPTH * KT:(i + 1) * DEPTH * KT]).then_inc(g_ready, 1)
                o = [Z[0], Z[1], S, T][t % 4]
                if t in TURN_DVE:
                    dve.wait_ge(xt_full, t + 1)
                    dve.tensor_copy(mix[:, t, 0:SEQ], o[:, 0, :])
                else:
                    dve.wait_ge(xt_act, t + 1 - sum(i < t for i in TURN_DVE))
                dve.tensor_copy(mix[:, t, SEQ:NTOK], o[:, 1, 0:NS]).then_inc(x_ready, 1)
                if t == 11:
                    x_parts(0, [2])
            split_of(0, 0, 0)
            x_parts(0, range(3, KT + 2))
            dve.wait_ge(const_in, 16 * CONSTS)
            with dve.Fori(0, DEPTH) as l:
                own = Own(dve, own_v, DVE_OWN)
                own.layer = l
                side = Sides(dve, l)

                def split(n, h):
                    split_of(l, n, h)

                def z_out(n, j, dst):
                    dve.wait_ge(z_ready, l * NB + n + 2)
                    dve.tensor_tensor(two(dst), zcols(Z[j]), two(rms[:, :]), ALU.mult).then_inc(z_free, 1)

                def rotate(n, j, dst, done, then=None):
                    z = zr[:, j, :]
                    z_out(n, j, z)
                    if then:
                        then()
                    dve.wait_ge(z_free, l * NB + n + 3)
                    own.mark(dve.tensor_tensor(dst, z, cos[:, :], ALU.mult))
                    for q in range(4):
                        a, b = q * 32, (q ^ 1) * 32
                        own.mark(dve.tensor_tensor(th[a:a + 32, :], z[b:b + 32, :], sin[b:b + 32, :], ALU.mult))
                    own.settle()
                    dve.tensor_tensor(dst, dst, th[:, :], ALU.add).then_inc(done, 1)

                def invert(key):
                    side.wait_read(key)
                    own.mark(dve.reciprocal(rms[:, :], rms[:, :]))
                    own.settle()

                def rotate_k(t):
                    k = krot[:, t, :]
                    own.mark(dve.tensor_tensor(k, k, rms[:, :], ALU.mult))
                    own.settle()
                    for q in range(4):
                        a, b = q * 32, (q ^ 1) * 32
                        own.mark(dve.tensor_tensor(th[a:a + 32, :], k[b:b + 32, :], sin[b:b + 32, :], ALU.mult))
                    own.settle()
                    own.mark(dve.tensor_tensor(k, k, cos[:, :], ALU.mult))
                    own.settle()
                    dve.tensor_tensor(k, k, th[:, :], ALU.add).then_inc(kv_rot, 1)

                def stage_k(g):
                    s, t = (g % 2) * HD, g // 2
                    dve.wait_ge(khi_ready, l * 4 + g + 1)
                    for d in (s, HD - s):
                        ins = dve.tensor_tensor(k_lo[d:d + HD, :], krot[s:s + HD, t, 0:SEQ], k_hi[s:s + HD, :].bitcast(F32), ALU.subtract)
                    ins.then_inc(klo_ready, 1)

                def stage_q(u):
                    g, b = divmod(u, NBLK)
                    dve.wait_ge(qhi_ready, l * 16 + u + 1)
                    for s in range(2):
                        d = HD - s * HD
                        ins = dve.tensor_tensor(q_st[d:d + HD, s:GROUP:2, :], mix[s * HD:(s + 1) * HD, 2 * g:2 * g + 2, b * P:(b + 1) * P],
                                                q_st[s * HD:(s + 1) * HD, s:GROUP:2, :].bitcast(F32), ALU.subtract)
                    ins.then_inc(qlo_ready, 1)

                def stage_v(u):
                    g, b = divmod(u, NBLK)
                    b0, nk = max(b - 1, 0), min(b + 1, 2)
                    dve.wait_ge(vhi_ready, l * 16 + u + 1)
                    dve.tensor_tensor(v_st[:, 0:nk, 1, :], v_tok[:, b0:b0 + nk, g * HD:(g + 1) * HD],
                                      v_st[:, 0:nk, 0, :].bitcast(F32), ALU.subtract).then_inc(vlo_ready, 1)

                def attended(u):
                    g, b = divmod(u, NBLK)
                    dve.wait_ge(att_ready, l * 16 + u + 1)
                    for s in range(2):
                        o = mix[s * HD:(s + 1) * HD, 2 * g:2 * g + 2, b * P:(b + 1) * P]
                        ins = dve.tensor_tensor(o, o, T[HD:2 * HD, 0, :].rearrange("p (i s q) -> p i s q", i=2, s=2)[:, :, s, :], ALU.add)
                    side.freed(("pv", u), ins)

                def probs_lo(u):
                    nk = min(u % NBLK + 1, 2)
                    dve.wait_ge(pthi_ready, l * 16 + u + 1)
                    side.freed(("tp", u), dve.tensor_tensor(pt_lo[:, 0:nk, :], T[:, 0:nk, :], pt_hi[:, 0:nk, :].bitcast(F32), ALU.subtract))

                def maxima(u):
                    b = u % NBLK
                    w = P * min(b + 1, 2)
                    mask = band[:, 2 * P - w:2 * P]
                    c = sm[:, u % 2, :, :]
                    side.wait_full(("sc", u))
                    apart(dve)
                    for hh in range(GROUP):
                        ins = dve.tensor_tensor_reduce(prob[:, hh, 0:w], S[:, hh // 2, (hh % 2) * 2 * P:(hh % 2) * 2 * P + w], mask,
                                                       1.0, NEG, ALU.add, ALU.max, c[:, 0, hh:hh + 1])
                    side.freed(("sc", u), ins)
                    side.wait_read(("sc", u))
                    own.mark(dve.scalar_tensor_tensor(c[:, 1, :], c[:, 0, :], SCALE, sink[:, 4 * (u // NBLK):4 * (u // NBLK) + 4],
                                                      ALU.mult, ALU.max))
                    own.settle()
                    own.mark(dve.tensor_scalar(c[:, 2, :], c[:, 1, :], -1.0, None, ALU.mult))
                    own.settle()
                    dve.tensor_tensor(c[:, 3, :], c[:, 2, :], sink[:, 4 * (u // NBLK):4 * (u // NBLK) + 4], ALU.add).then_inc(max_ready, 1)

                def denominators(u):
                    c = sm[:, u % 2, :, :]
                    dve.wait_ge(exp_ready, l * 16 + u + 1)
                    own.mark(dve.tensor_tensor(c[:, 1, :], c[:, 4, :], es[:, :], ALU.add))
                    own.settle()
                    dve.reciprocal(c[:, 5, :], c[:, 1, :]).then_inc(den_ready, 1)

                def sample_queries(t0, t1):
                    dve.wait_ge(q_rot, l * 8 + t1)
                    for t in range(t0, t1):
                        p, kv, i = t // 4, t // 2 % 2, t % 2
                        for s in range(2):
                            dve.tensor_copy(
                                qbd[kv * HD:(kv + 1) * HD, p, :, :].rearrange("p b (v i s t) -> p b v i s t", v=2, i=2, s=2)[:, :, kv, i, s, :],
                                mix[s * HD:(s + 1) * HD, t, SEQ:NTOK].rearrange("p (b t) -> p b t", b=DB)
                            ).then_inc(qbd_ready, 1)

                def sample_maxima():
                    side.wait_full("ssc")
                    side.freed("ssc", dve.tensor_tensor(
                        ps.rearrange("p (c a) k -> p c a k", c=2),
                        S[:, :, 0:2 * (P + NS)].rearrange("p c (a k) -> p c a k", a=2),
                        smask[:, :, :].unsqueeze(2).broadcast_to((P, 2, 2, P + NS)), ALU.add))
                    own.mark(dve.tensor_tensor(ssel[:, :, :], sink[:, :].rearrange("p (a e) -> p a e", a=2),
                                               sel[:, :].unsqueeze(1).broadcast_to((P, 2, 8)), ALU.mult))
                    own.settle()
                    own.mark(dve.tensor_reduce(ssink[:, :], ssel[:, :, :], AX_X, ALU.add))
                    side.wait_read("ssc")
                    own.mark(dve.tensor_reduce(sms[:, 0, :], ps, AX_X, ALU.max))
                    own.settle()
                    sk = ssink[:, :].unsqueeze(1).broadcast_to((P, 2, 2))

                    def col(i):
                        return sms[:, i, :].rearrange("p (c a) -> p c a", c=2)

                    own.mark(dve.scalar_tensor_tensor(col(1), col(0), SCALE, sk, ALU.mult, ALU.max))
                    own.settle()
                    own.mark(dve.tensor_scalar(sms[:, 2, :], sms[:, 1, :], -1.0, None, ALU.mult))
                    own.settle()
                    dve.tensor_tensor(col(3), col(2), sk, ALU.add).then_inc(smax_ready, 1)

                def sample_probs():
                    dve.wait_ge(sexp_ready, l + 1)
                    own.mark(dve.tensor_tensor(sms[:, 1, :], sms[:, 4, :], ess[:, :], ALU.add))
                    own.settle()
                    own.mark(dve.reciprocal(sms[:, 5, :], sms[:, 1, :]))
                    own.settle()
                    dve.tensor_tensor(ps, ps, sms[:, 5, :].unsqueeze(2).broadcast_to((P, 4, P + NS)), ALU.mult).then_inc(sprob_ready, 1)

                def gate(n, tile):
                    dve.wait_ge(gate_t, l * 16 + n - GB0 + 1)
                    dve.wait_ge(gate_th, l * 16 + n - GB0 + 1)
                    dve.scalar_tensor_tensor(tile, th[:, :], 1.0, tile, ALU.add, ALU.mult).then_inc(gate_done, 1)

                def tile_at(t):
                    return mix[:, bass.ds(t, 1), :].rearrange("p a n -> p (a n)")

                split(Q0 - 1, 1)
                split(Q0, 0)
                dve.wait_ge(z_ready, l * NB + Q0 + 1)
                for j in range(2):
                    ins = dve.tensor_copy(two(krot[:, j, :]), zcols(Z[j]))
                    ins.then_inc(z_free, 2)
                split(Q0, 1)
                invert("xsum")
                split(Q0 + 1, 0)
                side.wait_read("kv3")
                for t in range(2):
                    dve.tensor_tensor(zr[:, t, :], zr[:, t, :], rms[:, :], ALU.mult).then_inc(v_ready, 1)
                dve.wait_ge(z_free, l * NB + Q0 + 2)
                rotate_k(0)
                split(Q0 + 1, 1)
                rotate_k(1)
                split(Q0 + 2, 0)
                dve.wait_ge(kv_rot, l * 2 + 2)
                for p in range(2):
                    dve.tensor_copy(kct[:, p, :, P:P + NS], krot[:, p, SEQ:NTOK].unsqueeze(1).broadcast_to((P, DB, NS))).then_inc(kct_new, 1)
                side.wait_full("kvtail")
                dve.wait_ge(park_out, 64 * (l + 1))
                rotate(Q0, 0, mix[:, 0, :], q_rot)
                rotate(Q0 + 1, 1, mix[:, 1, :], q_rot, lambda: split(Q0 + 2, 1))
                apart(dve)
                with own.repeat((XB0 - Q0) // 2 - 2, 10) as i:
                    for j in range(2):
                        n = Q0 + 2 + i * 2 + j
                        split(n + 1, 0)
                        rotate(n, j, tile_at(i * 2 + j + 2), q_rot, lambda: split(n + 1, 1))
                for n in (XB0 - 2, XB0 - 1):
                    split(n + 1, 0)
                    if n == XB0 - 2:
                        stage_k(0)
                    else:
                        stage_q(0)
                        sample_queries(0, 7)
                    rotate(n, n % 2, mix[:, n - Q0, :], q_rot, lambda: split(n + 1, 1))
                dve.wait_ge(par_in, PARAMS * 16 * (l + 1))
                for u in range(16):
                    n = XB0 + u
                    if u:
                        probs_lo(u - 1)
                    if u == 0:
                        sample_queries(7, 8)
                    else:
                        split(n, 1)
                    maxima(u)
                    stage_v(u)
                    if u:
                        attended(u - 1)
                    denominators(u)
                    if u == 1:
                        sample_probs()
                    split(n + 1, 0)
                    if u < 15:
                        if (u + 1) % NBLK == 0:
                            stage_k((u + 1) // NBLK)
                        stage_q(u + 1)
                    if u == 0:
                        sample_maxima()
                    if 4 <= u <= 7:
                        g = u - 4
                        side.wait_full(("pm", g))
                        side.freed(("pm", g), dve.tensor_scalar(two(mix[:, 8 + g, :]), zcols(T), pscale[:, g:g + 1], None, ALU.mult))
                    if u >= 12:
                        hh = u - 12
                        side.wait_full(("sg", hh))
                        if hh >= 2:
                            dve.wait_ge(sg_out, l * 4 + hh - 1)
                        own.mark(dve.tensor_tensor(tmp[hh % 2][:, 0:SEQ].rearrange("p (b t) -> p b t", b=NBLK),
                                                   T[:, 0, :].rearrange("p (b t) -> p b t", b=NBLK),
                                                   pars[:, 2, hh * P:(hh + 1) * P].unsqueeze(1).broadcast_to((P, NBLK, P)), ALU.add))
                        side.freed(("sg", hh), dve.tensor_tensor(
                            tmp[hh % 2][:, SEQ:NTOK].rearrange("p (b t) -> p b t", b=DB), T[:, 1, 0:NS].rearrange("p (b t) -> p b t", b=DB),
                            pars[:, 2, hh * P:hh * P + DT].unsqueeze(1).broadcast_to((P, DB, DT)), ALU.add))
                    if u == 9:
                        for key in ("vt0", "vt1", "vt2"):
                            side.wait_read(key)
                        for b in range(5):
                            r = P if b < NBLK else NS
                            own.mark(dve.bn_stats(stats[0:r, b, :], vn[0:r, b, :]))
                        own.settle()
                        apart(dve)
                        for b in range(5):
                            r = P if b < NBLK else NS
                            ins = dve.bn_aggr(mv[0:r, b, :], stats[0:r, b, :])
                        ins.then_inc(var_ready, 1)
                    if u == 10:
                        dve.wait_ge(std_ready, l + 1)
                        own.mark(dve.reciprocal(rstd[:, 0:4], rstd[:, 0:4]))
                        own.mark(dve.reciprocal(rstd[0:NS, 4:5], rstd[0:NS, 4:5]))
                        own.settle()
                        for b in range(5):
                            r = P if b < NBLK else NS
                            ins = dve.tensor_scalar(vn[0:r, b, :], vn[0:r, b, :], mv[0:r, b, 0:1], rstd[0:r, b:b + 1], ALU.subtract, ALU.mult)
                        ins.then_inc(ln_mid, 1)
                    if n > GB0:
                        gate(n - 1, mix[:, n - 1 - 16, :])
                    if n < VS0:
                        if u >= 2:
                            dve.wait_ge(ext_ready, l * 4 + u - 1)
                        z_out(n, n % 2, zr[:, n % 2, :])
                    elif n < U0:
                        if n == VS0:
                            side.wait_full("spv")
                        z_out(n, n % 2, mix[:, 12 + n - VS0, :])
                    elif n < GB0:
                        if n == U0:
                            side.wait_full("vt2")
                            side.wait_full("vt1")
                        z_out(n, n % 2, mix[:, 12 + n - U0, :])
                    else:
                        if n == GB0:
                            dve.wait_ge(ext_ready, l * 4 + 4)
                        z_out(n, n % 2, zr[:, n % 2, :])
                probs_lo(15)
                dve.wait_ge(sg_out, l * 4 + 4)
                apart(dve)
                with dve.Fori(0, (GA0 - GC0) // 2) as i:
                    for j in range(2):
                        n = GC0 + i * 2 + j
                        split(n, 1)
                        gate(n - 1, tile_at(n - 17))
                        split(n + 1, 0)
                        z_out(n, j, zr[:, j, :])
                attended(15)
                side.wait_read(("pv", 15))
                split(GA0, 1)
                gate(GA0 - 1, mix[:, 15, :])
                split(GA0 + 1, 0)
                z_out(GA0, 0, zr[:, 0, :])
                with dve.Fori(0, 3) as i:
                    for j in range(2):
                        n = GA0 + 1 + i * 2 + j
                        split(n, 1)
                        gate(n - 1, tile_at(i * 2 + j))
                        split(n + 1, 0)
                        z_out(n, 1 - j, zr[:, 1 - j, :])
                n = OUT0 - 1
                split(n, 1)
                gate(n - 1, mix[:, 6, :])
                split(n + 1, 0)
                for i, k in enumerate(OUT_ORDER):
                    if i == HK:
                        z_out(n, 1, zr[:, 1, :])
                        split(OUT0, 1)
                        gate(n, mix[:, 7, :])
                    dve.wait_ge(h_hi_ready, (l * 2 + 1) * KT + i + 1)
                    dve.scalar_tensor_tensor(h_lo[:, i, :], mix[:, k, :], 0.5, h_hi[:, i, :].bitcast(F32), ALU.mult,
                                             ALU.subtract).then_inc(h_ready, 1)

                def y_out(n, j, dst):
                    dve.wait_ge(sq_ready, l * 32 + 16 + n - OUT0 + 1)
                    dve.tensor_scalar(two(dst), zcols(Z[j]), g_post[:, bass.ds(l * KT + n - OUT0, 1)], None, ALU.mult).then_inc(z_free, 1)

                for n in (OUT0, OUT0 + 1):
                    if n > OUT0:
                        split(n, 1)
                    split(n + 1, 0)
                    y_out(n, n % 2, mix[:, n - OUT0, :])
                with dve.Fori(0, (N_OUT - 4) // 2) as i:
                    for j in range(2):
                        n = OUT0 + 2 + i * 2 + j
                        split(n, 1)
                        split(n + 1, 0)
                        y_out(n, j, tile_at(i * 2 + j + 2))
                split(NB - 2, 1)
                split(NB - 1, 0)
                y_out(NB - 2, 0, mix[:, KT - 2, :])
                split(NB - 1, 1)
                with dve.If(l < DEPTH - 1):
                    split_of(l + 1, 0, 0)
                y_out(NB - 1, 1, mix[:, KT - 1, :])
                side.wait_read("ysum")
                dve.reciprocal(ynorm[:, :], ynorm[:, :]).then_inc(ynorm_ready, 1)
                assert own.n == DVE_OWN, own.n
                dve.wait_ge(z_free, l * NB + NB + 2)
                side.wait_full("ynorm")
                dve.tensor_tensor(two(mix[:, 0, :]), two(mix[:, 0, :]), zcols(T), ALU.mult).then_inc(upd_ready, 1)
                dve.wait_ge(upd_ready, l * KT + 1)
                dve.wait_ge(park_in, 64 * (l + 1))
                dve.tensor_tensor(mix[:, 0, :], mix[:, 0, :], x_old[:, 0, :], ALU.add).then_inc(x_ready, 1)
                side.freed("ynorm", dve.tensor_copy(two(rms[:, :]), zcols(T)))
                side.wait_read("ynorm")
                for t in range(1, EARLY):
                    normalise_y(t)
                with dve.If(l < DEPTH - 1):
                    x_parts(l + 1)

            for t in range(EARLY, KT):
                normalise_y(t)
                if t in FIN_DVE:
                    dve.wait_ge(upd_ready, (DEPTH - 1) * KT + t + 1)
                    dve.tensor_tensor(mix[:, t, :], mix[:, t, :], x_old[:, t, :], ALU.add).then_inc(fin_added, 1)

        @block.gpsimd
        def _(pool):
            for i, g in enumerate((norm_pre, norm_post)):
                pool.dma_start(g_raw[:, i, :], g.rearrange("l (t p) -> (l t) p", p=P)).then_inc(g_in, 16)
            pool.memset(ones[:, :], 1.0).then_inc(ready0, 1)
            pool.memset(qbd[:, :, :, :], 0.0).then_inc(ready0, 1)
            pool.memset(w4[:, :, :], 0.0).then_inc(ready0, 1)
            pool.memset(eps[:, :], EPS).then_inc(ready0, 1)
            pool.memset(zeros[:, :], 0.0).then_inc(ready0, 1)
            pool.memset(junk[:, 0:1], 0.0).then_inc(w_split, 2)
            pool.memset(junk[:, 1:2], 0.0).then_inc(z_free, 2)
            for i, start in enumerate((z_ready, w_half_used, s_free, t_free)):
                pool.memset(junk[:, 2 + i:3 + i], 0.0).then_inc(start, 1)
            for q in range(4):
                pool.wait_ge(x_quarter_in[q], 16)
            for src, dst in ((c_band, band), (c_cos, cos), (c_sin, sin), (c_smask, smask), (c_sel, sel), (c_fix, fix)):
                pool.dma_start(dst[tuple([slice(None)] * len(dst.shape))], src).then_inc(const_in, 16)

            def add_square(l, i, phase, j):
                pool.wait_ge(sq_ready, l * 32 + phase * 16 + i + 1)
                if not isinstance(i, int) or i > 1:
                    pool.wait_ge(acc_done, l * ACC + phase * 15 + i - 1)
                pool.tensor_tensor(acc[:, :], acc[:, :], sq[:, j, :], ALU.add).then_inc(acc_done, 1)

            def residual(l, t):
                pool.wait_ge(upd_ready, (l - 1) * KT + t + 1)
                pool.tensor_tensor(mix[:, t, :], mix[:, t, :], x_old[:, t, :], ALU.add).then_inc(x_ready, 1)

            def park(q, dst, src):
                a, b = [v if len(v.shape) == 2 else v[:, :, :].rearrange("p t n -> p (t n)") for v in (dst, src)]
                c = slice(q * 4 * NTOK, (q + 1) * 4 * NTOK)
                pool.dma_start(a[:, c], b[:, c]).then_inc(park_out if dst is x_park else park_in, 16)

            def x_parts(l):
                first = isinstance(l, int)
                for step in range(KT + 2):
                    if 0 < step < KT and not first:
                        residual(l, step)
                    t = step - 2
                    if t > 0 and t % 2 == 0:
                        add_square(l, t, 0, t % 2)
                    if t > 0 and t % 4 == 3:
                        pool.wait_ge(x_ready, l * KT + t + 1)
                        if not first:
                            apart(pool)
                        park(t // 4, x_park, mix)

            x_parts(0)
            with pool.Fori(0, DEPTH) as l:
                own = Own(pool, own_p, POOL_OWN)
                own.layer = l
                side = Sides(pool, l)

                def normalise(u):
                    w = P * min(u % NBLK + 1, 2)
                    pool.wait_ge(den_ready, l * 16 + u + 1)
                    apart(pool)
                    for hh in range(GROUP):
                        ins = pool.tensor_scalar(prob[:, hh, 0:w], prob[:, hh, 0:w], sm[:, u % 2, 5, hh:hh + 1], 1.0, ALU.mult, ALU.mult)
                    ins.then_inc(norm_ready, 1)

                def pool_windows(g):
                    pool.wait_ge(ext_ready, l * 4 + g + 1)
                    src, shift = ext_a, 1
                    for i in range(g + 1):
                        dst = (ext_b, ext_c)[i % 2]
                        own.mark(pool.tensor_tensor(dst[:, HIST:EXT], src[:, HIST:EXT], src[:, HIST - shift:EXT - shift], ALU.add)
                                 if g == i else
                                 pool.tensor_tensor(dst[:, 2 * shift - 1:EXT], src[:, 2 * shift - 1:EXT], src[:, shift - 1:EXT - shift], ALU.add))
                        own.settle()
                        src, shift = dst, 2 * shift
                    own.mark(pool.tensor_tensor(src[:, HIST:HIST + 16], src[:, HIST:HIST + 16], fix[:, g, :], ALU.mult))
                    own.settle()
                    if g == 0:
                        pool.wait_ge(kv_out, 64 * (l + 1))
                    tail = [x[:, HIST + SEQ:EXT].rearrange("p (b n) -> p b n", b=DB)[:, :, HIST:SEXT] for x in (src, ext_a)]
                    apart(pool)
                    own.mark(pool.tensor_scalar(src[:, HIST:EXT], src[:, HIST:EXT], 1.0 / POOLW[g], 0.0, ALU.mult, ALU.add))
                    own.settle()
                    pool.tensor_tensor(mix[:, 8 + g, 0:SEQ], src[:, HIST:HIST + SEQ], ext_a[:, HIST:HIST + SEQ], ALU.subtract)
                    pool.tensor_tensor(mix[:, 8 + g, SEQ:NTOK].rearrange("p (b t) -> p b t", b=DB), tail[0], tail[1],
                                       ALU.subtract).then_inc(pooled_ready, 1)

                def ln_affine(i, op):
                    own.mark(pool.tensor_tensor(vn[:, 0:4, :], vn[:, 0:4, :], pars[:, i, :].unsqueeze(1).broadcast_to((P, 4, SEQ)), op))
                    return pool.tensor_tensor(vn[0:NS, 4, :], vn[0:NS, 4, :], pars[0:NS, i, :], op)

                def gate(n, j, tile):
                    pool.wait_ge(z_free, l * NB + n + 3)
                    pool.tensor_tensor(tile, tile, zr[:, j, :], ALU.mult).then_inc(gate_t, 1)

                def tile_at(t):
                    return mix[:, bass.ds(t, 1), :].rearrange("p a n -> p (a n)")

                pool.dma_start(sgw_raw, sgu_w[l].rearrange("h t s -> t h s")).then_inc(raw_in, 16)
                pool.dma_start(st_raw, state_pool[l].rearrange("b n c -> (b n) c")).then_inc(raw_in, 16)
                pool.wait_ge(park_out, 64 * (l + 1))
                pool.wait_ge(h_ready, l * 2 * KT + KT)
                pool.wait_ge(sq_ready, l * 32 + KT)
                apart(pool)
                pool.dma_start(cache, cache_k[l].rearrange("b n h d -> n b (h d)")).then_inc(kc_in, 16)
                pool.dma_start(pscale[:, :], pool_scale[l].rearrange("(g p) -> p g", p=P)).then_inc(par_in, 16)
                pool.dma_start(sink[:, :], sinks[l].partition_broadcast(P)).then_inc(par_in, 16)
                pool.dma_start(poolw[:, :, :], pool_w[l].rearrange("g c d -> c g d")).then_inc(par_in, 16)
                side.wait_full("kc0")
                side.wait_full("kc1")
                apart(pool)
                pool.dma_start(cache, cache_v[l].rearrange("b n h d -> n b (h d)")).then_inc(vc_in, 16)
                side.wait_read("v")
                apart(pool)
                pool.dma_start(nv_p[l, 0].rearrange("n h d -> n (h d)"), v_tok[:, NBLK - 1, :]).then_inc(kv_out, 16)
                side.wait_read("kvtail")
                apart(pool)
                pool.dma_start(nk_p[l, 0].rearrange("n h d -> n (h d)"), k_tail).then_inc(kv_out, 16)
                for dst, src in ((nk_s, k_new), (nv_s, v_new[:, :])):
                    pool.dma_start(dst[l, :, P - DT:P].rearrange("b t h d -> b t (h d)"), src).then_inc(kv_out, 16)
                side.wait_read("wm")
                apart(pool)
                pool.affine_select(out=wmt[:, :, :], in_=wmt[:, :, :], compare_op=ALU.is_ge, fill=0.0, base=0,
                                   pattern=[[0, 4], [1, P]], channel_multiplier=-1).then_inc(wm_masked, 1)
                pool.wait_ge(wm_masked, l + 1)
                apart(pool)
                for b in range(DB):
                    pool.dma_start(w4[b * DT:(b + 1) * DT, :, b * DT:(b + 1) * DT], wmt[0:DT, :, 0:DT]).then_inc(w4_in, 16)
                for u in range(16):
                    if u in (0, 1, 7, 9):
                        new, old = (nk_s, cache_k) if u < 7 else (nv_s, cache_v)
                        b0 = 0 if u in (0, 7) else DB // 2
                        pool.dma_start(new[l, b0:b0 + DB // 2, 0:P - DT], old[l, b0:b0 + DB // 2, DT:P]).then_inc(copy_out, 16)
                    if u == 8:
                        pool.dma_start(npool_s[l, :, 0:HIST - DT], state_pool[l, :, DT:HIST]).then_inc(copy_out, 16)
                    if 2 <= u <= 5:
                        pool_windows(u - 2)
                    if u == 6:
                        pool.wait_ge(pooled_ready, l * 4 + 4)
                        apart(pool)
                        for i, src in enumerate((ln_g[l], ln_b[l], sgu_b[l].rearrange("h t -> (h t)"))):
                            pool.dma_start(pars[:, i, :], src.partition_broadcast(P)).then_inc(lnp_in, 16)
                    if u == 10:
                        side.wait_read("xbo")
                        apart(pool)
                        pool.dma_start(npool_p[l, 0], xbo[0:HIST, :]).then_inc(xb_out, 16)
                        pool.dma_start(npool_s[l, :, HIST - DT:HIST], xbo[HIST:HIST + NS, :]).then_inc(xb_out, 16)
                    if u == 11:
                        pool.wait_ge(ln_mid, l + 1)
                        pool.wait_ge(lnp_in, 48 * (l + 1))
                        own.mark(ln_affine(0, ALU.mult))
                    normalise(u)
                    if u == 11:
                        own.settle()
                        ln_affine(1, ALU.add).then_inc(vn_ready, 1)
                        pool.wait_ge(vn_ready, l + 1)
                        apart(pool)
                        pool.dma_start(nchunk_s[l].rearrange("b t f -> (b t) f"), vn[0:NS, 4, :]).then_inc(vn_out, 16)
                    if u >= 13:
                        gate(XB0 + u - 1, (u - 1) % 2, mix[:, XB0 + u - 1 - 16, :])
                        hh = u - 13
                        side.wait_read(("sg", hh))
                        pool.tensor_tensor(mix[:, 12 + hh, :], mix[:, 12 + hh, :], tmp[hh % 2], ALU.mult).then_inc(sg_out, 1)
                side.wait_read(("sg", 3))
                pool.tensor_tensor(mix[:, 15, :], mix[:, 15, :], tmp[1], ALU.mult).then_inc(sg_out, 1)
                with pool.Fori(0, (GA0 - GC0) // 2) as i:
                    for j in range(2):
                        gate(GC0 + i * 2 + j - 1, 1 - j, tile_at(i * 2 + j + 11))
                gate(GA0 - 1, 1, mix[:, 15, :])
                side.wait_read(("pv", 15))
                apart(pool)
                with pool.Fori(0, (OUT0 - GA0) // 2) as i:
                    for j in range(2):
                        gate(GA0 + i * 2 + j, j, tile_at(i * 2 + j))
                pool.wait_ge(gate_done, l * 16 + 16)
                pool.wait_ge(vn_out, 16 * (l + 1))
                pool.wait_ge(xb_out, 32 * (l + 1))
                pool.wait_ge(kv_out, 64 * (l + 1))
                apart(pool)
                park(0, arena, x_park)
                add_square(l, 1, 1, 1)
                for q in range(3):
                    with pool.Fori(2 * q, 2 * q + 2) as i:
                        for j in range(2):
                            add_square(l, 2 + i * 2 + j, 1, j)
                    park(q + 1, arena, x_park)
                add_square(l, N_OUT - 2, 1, 0)
                assert own.n == POOL_OWN, own.n
                with pool.If(l < DEPTH - 1):
                    pool.wait_ge(park_in, 64 * (l + 1))
                    x_parts(l + 1)
            pool.wait_ge(park_in, 64 * DEPTH)
            for t in range(1, KT):
                if t not in FIN_DVE:
                    residual(DEPTH, t)
            pool.wait_ge(kv_out, 64 * DEPTH)
            pool.wait_ge(xb_out, 32 * DEPTH)
            pool.wait_ge(vn_out, 16 * DEPTH)
            pool.wait_ge(park_out, 64 * DEPTH)
            pool.wait_ge(copy_out, 80 * DEPTH)


def tables():
    r = np.arange(P)
    inv = (10000.0 ** (-np.arange(0, HD, 2) / HD)).astype(np.float32)
    pos = np.concatenate([np.arange(SEQ), np.tile(PAST + np.arange(DT), DB)]).astype(np.float32)
    ang = (inv[r % 32][:, None] * pos[None, :]).astype(np.float32)
    sign = np.where(r % HD < 32, 1.0, -1.0).astype(np.float32)[:, None]
    prev = np.where(r[None, :] > r[:, None], 0.0, NEG)
    same = np.where(r[None, :] <= r[:, None], 0.0, NEG)
    b, t = r // 32, r % DT
    smask = np.full((P, 2, P + NS), NEG, np.float32)
    for c in range(2):
        smask[:, c, 0:P] = np.where(r[None, :] > t[:, None], 0.0, NEG)
        nb, nt = np.arange(NS) // DT, np.arange(NS) % DT
        smask[:, c, P:] = np.where((nb[None, :] == (c * 4 + b)[:, None]) & (nt[None, :] <= t[:, None]), 0.0, NEG)
    sel = (((r % 32) // DT)[:, None] == np.arange(8)[None, :]).astype(np.float32)
    fix = np.stack([w / np.minimum(w, np.arange(16) + 1.0) for w in POOLW]).astype(np.float32)
    return {
        "c_cos": np.cos(ang), "c_sin": np.sin(ang) * sign, "c_band": np.concatenate([prev, same], 1).astype(np.float32),
        "c_smask": smask, "c_ident": np.eye(P, dtype=np.float32), "c_sel": sel, "c_fix": np.tile(fix[None], (P, 1, 1)),
    }


_INS = ["x_prompt", "x_sample", "cache_k", "cache_v", "state_pool", "w_in", "w_out", "norm_pre", "norm_post", "attn_sinks",
        "pool_w", "pool_scale", "sgu_ln_g", "sgu_ln_b", "sgu_w", "sgu_b"]
_OUTS = [(1, SEQ, D), (DB, DT, D), (DEPTH, 1, P, NKV, HD), (DEPTH, 1, P, NKV, HD), (DEPTH, 1, HIST, SEQ),
         (DEPTH, DB, P, NKV, HD), (DEPTH, DB, P, NKV, HD), (DEPTH, DB, HIST, SEQ), (DEPTH, DB, DT, SEQ)]


def kernel(**inputs):
    import concourse.bacc as _bacc
    from concourse.bass_utils import run_bass_kernel_spmd as _run

    nc = _bacc.Bacc("TRN2", target_bir_lowering=False, num_devices=1)
    arrays, args = {}, []
    for name, a in [(n, inputs[n]) for n in _INS] + list(tables().items()):
        a = np.ascontiguousarray(a)
        arrays[f"in_{name}_dram"] = a
        args.append(nc.dram_tensor(f"in_{name}_dram", a.shape, mybir.dt.from_np(a.dtype), kind="ExternalInput").ap())
    for i, shape in enumerate(_OUTS):
        args.append(nc.dram_tensor(f"out_{i}_dram", shape, F32, kind="ExternalOutput").ap())
    args.append(nc.dram_tensor("x_park", (P, KT * NTOK), F32, kind="Internal").ap())
    program(nc, *args)
    r = _run(nc, [arrays], core_ids=[0])
    return tuple(r.results[0][f"out_{i}_dram"] for i in range(len(_OUTS)))
```
